# Optimizing a Trainium2 kernel written in Bass

```python
import math
import jax
import jax.numpy as jnp
from jax import lax
import numpy as np

D_MODEL = 1024
BATCH = 1
SEQ = 256
DEPTH = 2

CHUNK = 64
D_MIX = 1024

RWKV_HEADS = 6
RWKV_HEAD_DIM = 64
RWKV_WIDTH = 384
DECAY_LORA = 64
ICLR_LORA = 64
GATE_LORA = 128
RWKV_IN = 1408
RWKV_GN_EPS = 64e-5

S5_GROUPS = 16
S5_GROUP_CH = 16
S5_WIDTH = 256
S5_STATE = 64
S5_MIN_STEP = 1e-3
S5_MAX_STEP = 1e-1

ATTN_HEADS = 6
ATTN_HEAD_DIM = 64
ATTN_WIDTH = 384
LEFT_CHUNKS = 8
BAND_CHUNKS = 9
BAND = 576
MAX_REL = 128

N_IN = 2816
D_FF = 2816
N_EXPERTS = 8
TOP_K = 2
N_DENSE_LAYERS = (DEPTH + 1) // 2
N_MOE_LAYERS = DEPTH // 2
RMS_EPS = 1e-6

kernel_name = 'hybrid_chunk_streaming_block'

def rms_norm(x, gain):
    xf = x.astype(jnp.float32)
    y = xf * lax.rsqrt(jnp.mean(xf * xf, axis=-1, keepdims=True) + RMS_EPS)
    return (y * gain.astype(jnp.float32)).astype(x.dtype)

def token_shift(t):
    return jnp.pad(t, ((0, 0), (1, 0), (0, 0)))[:, :-1]

def swiglu(h, w_gate, w_up, w_down):
    return (jax.nn.silu(h @ w_gate) * (h @ w_up)) @ w_down

def rwkv7_mix(p, mu, w0, w_up, a0, a_up, g_up, k_k, k_a, r_k, ln_w, ln_b):
    B, S, _ = p.shape
    H, N = RWKV_HEADS, RWKV_HEAD_DIM
    p = p + (token_shift(p) - p) * mu
    r, k, v, w_lo, a_lo, g_lo = jnp.split(
        p, [RWKV_WIDTH, 2 * RWKV_WIDTH, 3 * RWKV_WIDTH,
            3 * RWKV_WIDTH + DECAY_LORA, 3 * RWKV_WIDTH + DECAY_LORA + ICLR_LORA], axis=-1)
    w = -jax.nn.softplus(-(w0 + jnp.tanh(w_lo) @ w_up)) - 0.5
    decay = jnp.exp(-jnp.exp(w.astype(jnp.float32)))
    a = jax.nn.sigmoid(a0 + a_lo @ a_up)
    g = jax.nn.sigmoid(g_lo) @ g_up
    kk = (k * k_k).reshape(B, S, H, N).astype(jnp.float32)
    kk = kk / jnp.maximum(jnp.sqrt(jnp.sum(kk * kk, axis=-1, keepdims=True)), 1e-12)
    k = k * (1.0 + (a - 1.0) * k_a)
    rh = r.reshape(B, S, H, N)
    kh = k.reshape(B, S, H, N)
    vh = v.reshape(B, S, H, N)

    def seq_first(t):
        return jnp.moveaxis(t.reshape(B, S, H, N).astype(jnp.float32), 1, 0)

    def step(state, inp):
        r_t, w_t, k_t, v_t, kk_t, a_t = inp
        sa = jnp.einsum('bhvk,bhk->bhv', state, -kk_t)
        state = (state * w_t[:, :, None, :] + sa[..., None] * (kk_t * a_t)[:, :, None, :]
                 + v_t[..., None] * k_t[:, :, None, :])
        return state, jnp.einsum('bhvk,bhk->bhv', state, r_t)

    state0 = jnp.zeros((B, H, N, N), jnp.float32)
    xs = (seq_first(rh), seq_first(decay), seq_first(kh), seq_first(vh), jnp.moveaxis(kk, 1, 0), seq_first(a))
    _, o = lax.scan(step, state0, xs)
    o = jnp.moveaxis(o, 0, 1)
    mean = jnp.mean(o, axis=-1, keepdims=True)
    var = jnp.mean(jnp.square(o - mean), axis=-1, keepdims=True)
    o = ((o - mean) * lax.rsqrt(var + RWKV_GN_EPS)).reshape(B, S, RWKV_WIDTH)
    o = o * ln_w.astype(jnp.float32) + ln_b.astype(jnp.float32)
    bonus = jnp.sum(rh * kh * r_k, axis=-1, keepdims=True) * vh
    o = o + bonus.reshape(B, S, RWKV_WIDTH).astype(jnp.float32)
    return (o * g.astype(jnp.float32)).astype(p.dtype)

def s5_mix(u, a_re, a_im, log_step, b_re, b_im, c_re, c_im, d, w_glu, b_glu, gain):
    B, S, _ = u.shape
    ug = u.astype(jnp.float32).reshape(B, S, S5_GROUPS, S5_GROUP_CH)
    lam = lax.complex(jnp.minimum(a_re.astype(jnp.float32), -1e-4), a_im.astype(jnp.float32))
    step = jnp.exp(log_step.astype(jnp.float32))[:, None]
    lam_bar = jnp.exp(lam * step)
    b = lax.complex(b_re.astype(jnp.float32), b_im.astype(jnp.float32))
    b_bar = ((lam_bar - 1.0) / lam)[..., None] * b
    bu = jnp.einsum('gpc,bsgc->bsgp', b_bar, ug.astype(jnp.complex64))
    lam_seq = jnp.broadcast_to(lam_bar, bu.shape)

    def combine(e1, e2):
        a1, x1 = e1
        a2, x2 = e2
        return a2 * a1, a2 * x1 + x2

    _, states = lax.associative_scan(combine, (lam_seq, bu), axis=1)
    c = lax.complex(c_re.astype(jnp.float32), c_im.astype(jnp.float32))
    y = jnp.real(jnp.einsum('gcp,bsgp->bsgc', c, states)) + d.astype(jnp.float32) * ug
    y = jax.nn.gelu(y.reshape(B, S, S5_WIDTH))
    y = y * jax.nn.sigmoid(y @ w_glu.astype(jnp.float32) + b_glu.astype(jnp.float32))
    return rms_norm(y.astype(u.dtype), gain)

def chunk_attention(q, k, v, rel_bias, gain):
    B, S, _ = q.shape
    NC = S // CHUNK
    H, Dh = ATTN_HEADS, ATTN_HEAD_DIM

    def blocks(t):
        return t.reshape(B, NC, CHUNK, H, Dh)

    band_idx = jnp.arange(NC)[:, None] + jnp.arange(BAND_CHUNKS)[None, :]

    def band(t):
        tp = jnp.pad(blocks(t), ((0, 0), (LEFT_CHUNKS, 0), (0, 0), (0, 0), (0, 0)))
        return tp[:, band_idx].reshape(B, NC, BAND, H, Dh)

    qb = blocks(q)
    kb, vb = band(k), band(v)
    s = jnp.einsum('bcqhd,bckhd->bchqk', qb, kb).astype(jnp.float32) * (Dh ** -0.5)
    qpos = LEFT_CHUNKS * CHUNK + np.arange(CHUNK)
    kpos = np.arange(BAND)
    rel_idx = np.clip(qpos[:, None] - kpos[None, :], -MAX_REL, MAX_REL) + MAX_REL
    s = s + rel_bias.astype(jnp.float32)[:, rel_idx]
    key_abs = (jnp.arange(NC)[:, None] - LEFT_CHUNKS) * CHUNK + jnp.arange(BAND)[None, :]
    valid = key_abs >= 0
    s = jnp.where(valid[None, :, None, None, :], s, jnp.finfo(jnp.float32).min)
    prob = jax.nn.softmax(s, axis=-1).astype(v.dtype)
    o = jnp.einsum('bchqk,bckhd->bcqhd', prob, vb).reshape(B, S, ATTN_WIDTH)
    return rms_norm(o, gain)

def moe_swiglu(h, router, w_gate, w_up, w_down):
    B, S, D = h.shape
    t = h.reshape(B * S, D)
    logits = (t @ router).astype(jnp.float32)
    top_val, top_idx = lax.top_k(logits, TOP_K)
    gates = jax.nn.softmax(top_val, axis=-1)
    combine = jnp.sum(jax.nn.one_hot(top_idx, N_EXPERTS, dtype=jnp.float32) * gates[..., None], axis=1)
    out = jnp.zeros_like(t)
    for e in range(N_EXPERTS):
        out = out + combine[:, e:e + 1].astype(t.dtype) * swiglu(t, w_gate[e], w_up[e], w_down[e])
    return out.reshape(B, S, D)

def setup_inputs(seed: int = 0) -> dict:
    key = jax.random.key(seed)
    ks = iter(jax.random.split(key, 48))
    L, Ld, Lm = DEPTH, N_DENSE_LAYERS, N_MOE_LAYERS
    G, Cg, P = S5_GROUPS, S5_GROUP_CH, S5_STATE

    def nrm(shape, scale):
        return scale * jax.random.normal(next(ks), shape, jnp.float32)

    def gain(shape):
        return 1.0 + 0.02 * jax.random.normal(next(ks), shape, jnp.float32)

    decay_base = jnp.linspace(-6.0, -1.0, RWKV_WIDTH, dtype=jnp.float32) + 0.5
    n = jnp.arange(P, dtype=jnp.float32)
    return {
        'x': nrm((BATCH, SEQ, D_MODEL), 1.0),
        'norm_mix_pre': gain((L, D_MODEL)),
        'norm_mix_post': gain((L, D_MODEL)),
        'norm_ffn_pre': gain((L, D_MODEL)),
        'norm_ffn_post': gain((L, D_MODEL)),
        'w_in': nrm((L, D_MODEL, N_IN), D_MODEL ** -0.5),
        'w_out': nrm((L, D_MIX, D_MODEL), D_MIX ** -0.5),
        'rwkv_mu': jax.random.uniform(next(ks), (L, RWKV_IN), jnp.float32),
        'rwkv_w0': decay_base + nrm((L, RWKV_WIDTH), 0.1),
        'rwkv_w_up': nrm((L, DECAY_LORA, RWKV_WIDTH), 0.05),
        'rwkv_a0': nrm((L, RWKV_WIDTH), 0.1),
        'rwkv_a_up': nrm((L, ICLR_LORA, RWKV_WIDTH), 0.5 * ICLR_LORA ** -0.5),
        'rwkv_g_up': nrm((L, GATE_LORA, RWKV_WIDTH), GATE_LORA ** -0.5),
        'rwkv_k_k': 0.85 + nrm((L, RWKV_WIDTH), 0.02),
        'rwkv_k_a': 1.0 + nrm((L, RWKV_WIDTH), 0.02),
        'rwkv_r_k': nrm((L, RWKV_HEADS, RWKV_HEAD_DIM), 0.1),
        'rwkv_ln_w': gain((L, RWKV_WIDTH)),
        'rwkv_ln_b': nrm((L, RWKV_WIDTH), 0.01),
        's5_a_re': -0.5 + nrm((L, G, P), 0.01),
        's5_a_im': jnp.broadcast_to(math.pi * n, (L, G, P)),
        's5_log_step': jax.random.uniform(next(ks), (L, G), jnp.float32,
                                          minval=math.log(S5_MIN_STEP), maxval=math.log(S5_MAX_STEP)),
        's5_b_re': nrm((L, G, P, Cg), (2 * Cg) ** -0.5),
        's5_b_im': nrm((L, G, P, Cg), (2 * Cg) ** -0.5),
        's5_c_re': nrm((L, G, Cg, P), (2 * P) ** -0.5),
        's5_c_im': nrm((L, G, Cg, P), (2 * P) ** -0.5),
        's5_d': nrm((L, G, Cg), 1.0),
        's5_w_glu': nrm((L, S5_WIDTH, S5_WIDTH), S5_WIDTH ** -0.5),
        's5_b_glu': nrm((L, S5_WIDTH), 0.01),
        's5_norm': gain((L, S5_WIDTH)),
        'attn_rel_bias': nrm((L, ATTN_HEADS, 2 * MAX_REL + 1), 0.2),
        'attn_norm': gain((L, ATTN_WIDTH)),
        'ffn_w_gate': nrm((Ld, D_MODEL, D_FF), D_MODEL ** -0.5),
        'ffn_w_up': nrm((Ld, D_MODEL, D_FF), D_MODEL ** -0.5),
        'ffn_w_down': nrm((Ld, D_FF, D_MODEL), D_FF ** -0.5),
        'moe_router': nrm((Lm, D_MODEL, N_EXPERTS), D_MODEL ** -0.5),
        'moe_w_gate': nrm((Lm, N_EXPERTS, D_MODEL, D_FF), D_MODEL ** -0.5),
        'moe_w_up': nrm((Lm, N_EXPERTS, D_MODEL, D_FF), D_MODEL ** -0.5),
        'moe_w_down': nrm((Lm, N_EXPERTS, D_FF, D_MODEL), D_FF ** -0.5),
    }

def reference(x, norm_mix_pre, norm_mix_post, norm_ffn_pre, norm_ffn_post, w_in, w_out,
              rwkv_mu, rwkv_w0, rwkv_w_up, rwkv_a0, rwkv_a_up, rwkv_g_up, rwkv_k_k, rwkv_k_a, rwkv_r_k,
              rwkv_ln_w, rwkv_ln_b,
              s5_a_re, s5_a_im, s5_log_step, s5_b_re, s5_b_im, s5_c_re, s5_c_im, s5_d, s5_w_glu, s5_b_glu,
              s5_norm, attn_rel_bias, attn_norm,
              ffn_w_gate, ffn_w_up, ffn_w_down, moe_router, moe_w_gate, moe_w_up, moe_w_down):
    split_at = [RWKV_IN, RWKV_IN + S5_WIDTH, RWKV_IN + S5_WIDTH + ATTN_WIDTH,
                RWKV_IN + S5_WIDTH + 2 * ATTN_WIDTH]
    for layer in range(DEPTH):
        h = rms_norm(x, norm_mix_pre[layer])
        proj = h @ w_in[layer]
        p_rwkv, u_s5, q, k, v = jnp.split(proj, split_at, axis=-1)
        o_rwkv = rwkv7_mix(p_rwkv, rwkv_mu[layer], rwkv_w0[layer], rwkv_w_up[layer], rwkv_a0[layer],
                           rwkv_a_up[layer], rwkv_g_up[layer], rwkv_k_k[layer], rwkv_k_a[layer],
                           rwkv_r_k[layer], rwkv_ln_w[layer], rwkv_ln_b[layer])
        o_s5 = s5_mix(u_s5, s5_a_re[layer], s5_a_im[layer], s5_log_step[layer], s5_b_re[layer],
                      s5_b_im[layer], s5_c_re[layer], s5_c_im[layer], s5_d[layer], s5_w_glu[layer],
                      s5_b_glu[layer], s5_norm[layer])
        o_attn = chunk_attention(q, k, v, attn_rel_bias[layer], attn_norm[layer])
        mixed = jnp.concatenate([o_rwkv, o_s5, o_attn], axis=-1)
        x = x + rms_norm(mixed @ w_out[layer], norm_mix_post[layer])
        h = rms_norm(x, norm_ffn_pre[layer])
        if layer % 2 == 0:
            i = layer // 2
            f = swiglu(h, ffn_w_gate[i], ffn_w_up[i], ffn_w_down[i])
        else:
            i = layer // 2
            f = moe_swiglu(h, moe_router[i], moe_w_gate[i], moe_w_up[i], moe_w_down[i])
        x = x + rms_norm(f, norm_ffn_post[layer])
    return x


_drawn_inputs = setup_inputs


def setup_inputs(seed=0):
    import zlib

    import numpy as np

    out = dict(_drawn_inputs(seed))
    spreads = {}
    factors = {}
    for name, (base, spread) in spreads.items():
        noise = np.random.default_rng([zlib.crc32(name.encode()), seed]).standard_normal(out[name].shape)
        drawn = base * np.exp(spread * noise) if base else spread * noise
        out[name] = jnp.asarray(drawn.astype(out[name].dtype))
    for name, factor in factors.items():
        out[name] = (out[name] * factor).astype(out[name].dtype)
    return out
```

```python
from contextlib import ExitStack

import numpy as np

import concourse.bass as bass
from concourse import mybir

F32 = mybir.dt.float32
ALU = mybir.AluOpType
ACT = mybir.ActivationFunctionType
AX = mybir.AxisListType

P = 128
D = 1024
S = 256
NT = S // P
KD = D // P
LAYERS = 2
EXPERTS = 8
F = 2816
FC = 256
CHUNKS = F // FC
WIN = 2816
WT = WIN // P
SLOT = KD * 2 * FC + 2 * D
SLOTS = 5
WIN_GROUP = 6
CHUNK_SLOT = [0, 1, 2, 3, 0, 4, 1, 2, 0, 3, 4]
EPS = 1e-6
GN_EPS = 64e-5
NEG_HALF_EXP = -0.6065306597126334
TWO_PI = 6.283185307179586
TWO_PI_HI = 6.28125
TWO_PI_LO = TWO_PI - TWO_PI_HI
ROUND = 12582912.0
GELU_C = 0.7978845608028654

COLS = {}
_at = 0
for _name, _n in [("mix_pre", 8), ("ffn_pre", 8), ("mu", 11), ("w0", 3), ("a0", 3), ("k_k", 3), ("k_a", 3),
                  ("r_k", 3), ("ln_w", 3), ("ln_b", 3), ("s5_d", 2), ("b_glu", 2), ("s5_norm", 2),
                  ("attn_norm", 3), ("a_re", 8), ("a_im", 8), ("log_step", 8)]:
    COLS[_name] = (_at, _n)
    _at += _n
NCOL = _at

LEVELS = 7
CONST = {}
_at = 0
for _name, _n in [("ident", 128), ("ones", 128), ("ones_head", 128), ("masks4", 512), ("level", LEVELS * 128),
                  ("scan", 256)]:
    CONST[_name] = (_at, _n)
    _at += _n
NCONST = _at


def constants():
    i = np.arange(P)
    s, t = i[:, None], i[None, :]
    strict, incl = (s < t), (s <= t)
    level = [((s // (2 * m)) == (t // (2 * m))) & (s % (2 * m) < m) & (t % (2 * m) >= m)
             for m in (1 << np.arange(LEVELS))]
    scan = np.ones((P, S))
    scan[:, ::P] = 0
    parts = [np.eye(P), np.ones((P, P)), (s // 64) == (t // 64), strict, incl, strict, incl, *level, scan]
    return np.concatenate([np.asarray(a, np.float32) for a in parts], axis=1)


ARENA = {}


def _place(start, items):
    at = start
    for name, n in items:
        ARENA[name] = (at, n)
        at += n
    return at


RING_END = SLOTS * SLOT
_end = _place(RING_END, [
    ("x", NT * D), ("hT", KD * S), ("hn", NT * D), ("const", NCONST), ("cols", NCOL), ("b_blk", 512),
    ("c_blk", 512), ("w_glu", 512), ("lora", 384), ("g_up", 384), ("E", 4096), ("act", 1536),
    ("natural", 2304), ("bonus", 768), ("g", 768), ("gain", D), ("small", 320), ("router", 64)])
ARENA_END = _end
MIX0 = 2 * SLOT
_end = _place(MIX0, [("kh", 768), ("bh", 768), ("pT", 11 * 257 + 1), ("pm", 2816), ("a", 768), ("lw", 768),
                     ("c", 768), ("qkT", 1536), ("vA", 768), ("bias", 2304), ("s", 1536),
                     ("PT", 1536), ("aO", 768)])
assert _end <= RING_END, (_end, RING_END)
_place(ARENA["pT"][0], [("kkn", 768), ("e1", 768), ("e2", 768)])
_place(ARENA["bias"][0], [(f"z{i}", 1024) for i in range(5)])
_place(ARENA["pT"][0], [("MAT", 12 * 512), ("T", 1536), ("TT", 1536), ("Pm", 1536), ("Am", 1536)])
assert ARENA["Am"][0] + 1536 <= RING_END
_place(ARENA["hn"][0], [("AR", 1536), ("uT", 512)])
_place(ARENA["act"][0], [("rhs", 384), ("sa", 384), ("st", 384)])
_place(ARENA["Pm"][0], [("OT", 768), ("o1", 768)])
_place(ARENA["Am"][0], [("o2", 768)])

SMALL = {}
_at = 0
for _name, _n in [("ss", 2), ("v", 2), ("sq", 2), ("rstd", 2), ("theta", 16), ("t0", 16), ("t1", 16), ("t2", 16),
                  ("lr", 16), ("r", 16), ("sn", 16), ("cs", 16), ("fr", 8), ("fi", 8), ("u0", 8), ("u1", 8),
                  ("half", 8), ("rmax", 12), ("rsum", 12), ("rinv", 12), ("dec", 3), ("cmid", 6), ("lg", 16),
                  ("m8", 16), ("comb", 16), ("g1", 2), ("g2", 2)]:
    SMALL[_name] = (_at, _n)
    _at += _n
assert _at <= 320, _at


class Steps:

    def __init__(self):
        self.at = {}
        self.per = {}
        self.final = False


class Engine:

    def __init__(self, name, sems, steps):
        self.name, self.sems, self.steps = name, sems, steps
        self.count, self.loop = 0, None

    def step(self, name=None):
        self.count += 1
        if name is not None:
            self.steps.at[name] = (self.name, self.count)
        return self.sems[self.name], 1

    def value(self, engine, value, back=0):
        if self.loop is not None:
            value = value + self.steps.per.get(engine, 1) * (self.loop[1] - back)
        return self.sems[engine], value

    def last(self):
        return self.value(self.name, self.count)

    def at(self, name, back=0):
        if name not in self.steps.at and self.steps.final:
            raise KeyError(name)
        engine, value = self.steps.at.get(name, ("pe", 1 << 12))
        return self.value(engine, value, back)


def build(nc, steps, io):
    ctx = ExitStack()
    with ctx:
        arena = ctx.enter_context(nc.sbuf_tensor("arena", [P, ARENA_END], F32))
        ps = ctx.enter_context(nc.psum_tensor("ps", [P, 8, 512], F32))
        sems = {n: ctx.enter_context(nc.semaphore(f"{n}_done")) for n in ("pe", "act", "dve", "pool")}
        slot_filled = [ctx.enter_context(nc.semaphore(f"slot_filled{i}")) for i in range(SLOTS)]
        x_loaded = ctx.enter_context(nc.semaphore("x_loaded"))
        const_loaded = ctx.enter_context(nc.semaphore("const_loaded"))
        params_loaded = ctx.enter_context(nc.semaphore("params_loaded"))
        bias_loaded = ctx.enter_context(nc.semaphore("bias_loaded"))
        gain_loaded = ctx.enter_context(nc.semaphore("gain_loaded"))
        router_loaded = ctx.enter_context(nc.semaphore("router_loaded"))
        out_stored = ctx.enter_context(nc.semaphore("out_stored"))

        def V(name, *dims):
            at, n = ARENA[name]
            size = int(np.prod(dims)) if dims else n
            a = arena[:, at:at + size]
            if len(dims) > 1:
                names = "abcd"[:len(dims)]
                a = a.rearrange(f"p ({' '.join(names)}) -> p {' '.join(names)}", **dict(zip(names, dims)))
            return a

        def C(name):
            at, n = CONST[name]
            return V("const")[:, at:at + n]

        def col(name, i=None):
            at, n = COLS[name]
            c = V("cols")
            return c[:, at:at + n] if i is None else c[:, at + i:at + i + 1]

        def sm(name, i=None, n=1):
            at, k = SMALL[name]
            s = V("small")
            return s[:, at:at + k] if i is None else s[:, at + i:at + i + n]

        def slot(i):
            return arena[:, i * SLOT:(i + 1) * SLOT]

        x, hT, hn = V("x", NT, D), V("hT", KD, S), V("hn", NT, D)
        ident, ones, ones_head = C("ident"), C("ones"), C("ones_head")
        E = V("E", 2, 8, S)
        pT, pm = V("pT", 11, 257), V("pm", 11, S)
        AR = V("AR", 3, NT, 2, P)
        kh, bh = V("kh", 3, S), V("bh", 3, S)
        natural = V("natural", 3, NT, 384)
        MAT = V("MAT", 12, 4, P)
        T, TT, Pm, Am = (V(n, 2, 6, P) for n in ("T", "TT", "Pm", "Am"))
        act_buf, actT = V("act")[:, 0:1024].rearrange("p (a b) -> p a b", a=4), \
            V("act")[:, 1024:1536].rearrange("p (a b c) -> p a b c", a=2, b=2)
        uT, qkT, vA = V("uT", 2, S), V("qkT", 6, S), V("vA", NT, 384)

        def bc(a, n):
            return a.unsqueeze(2).to_broadcast([P, a.shape[1], n])

        block = ctx.enter_context(nc.Block())

        uses = []
        for L in range(LAYERS):
            uses += [("win", L, g, g % 2) for g in range(4)] + [("wout", L, g, g % 2) for g in range(2)]
            if L == 0:
                uses += [("ffn", 0, j, CHUNK_SLOT[j]) for j in range(CHUNKS)]
        fill_no, fills = {}, [0] * SLOTS
        last_reader = [None] * SLOTS
        prev_reader = {}
        for u in uses:
            prev_reader[u] = last_reader[u[3]]
            last_reader[u[3]] = f"{u[0]} {u[1]} {u[2]} read"
            fills[u[3]] += 1
            fill_no[u[:3]] = fills[u[3]]
        static_fills = list(fills)
        per_fill = [CHUNK_SLOT.count(i) for i in range(SLOTS)]

        def filled(kind, L, part, s):
            return slot_filled[s], 16 * fill_no[(kind, L, part)]

        @block.sync
        def _(sp):
            en = Engine("sp", sems, steps)
            sp.dma_start(V("x", NT, D), io["x"].rearrange("(n p) d -> p n d", p=P)).then_inc(x_loaded, 16)
            sp.dma_start(V("const"), io["const"]).then_inc(const_loaded, 16)

            def params(L):
                for k, name in enumerate(["cols", "b_blk", "c_blk", "w_glu", "lora", "g_up"]):
                    sp.dma_start(V(name), io[name][L]).then_inc(params_loaded, 16)

            params(0)
            def static(u):
                kind, L, g, s = u
                if kind == "win" and g == 0 and L == 1:
                    sp.wait_ge(*en.at("0 ffn pre gained"))
                    sp.wait_ge(*en.at("0 mix used params"))
                    params(1)
                if prev_reader[u]:
                    sp.wait_ge(*en.at(prev_reader[u]))
                if kind == "win":
                    a, b = g * WIN_GROUP * D, min((g + 1) * WIN_GROUP, WT) * D
                    sp.dma_start(slot(s)[:, 0:b - a], io["w_in"][L][:, a:b]).then_inc(slot_filled[s], 16)
                elif kind == "wout":
                    sp.dma_start(slot(s)[:, 0:4096], io["w_out"][L][:, g * 4096:(g + 1) * 4096]
                                 ).then_inc(slot_filled[s], 16)
                else:
                    if s >= 2 and g < 6:
                        sp.wait_ge(*en.at(f"{L} mixing over"))
                    sp.dma_start(slot(s), io["ffn"][g]).then_inc(slot_filled[s], 16)
                if kind == "win" and g == 3:
                    sp.wait_ge(*en.at(f"{L} s5 scratch free"))
                    sp.dma_start(V("bias"), io["bias"][L]).then_inc(bias_loaded, 16)
                if kind == "wout" and g == 1:
                    sp.wait_ge(*en.at(f"{L} gain 0 free")) if L else None
                    sp.dma_start(V("gain"), io["mix_post"][L:L + 1].to_broadcast([P, D])).then_inc(gain_loaded, 16)
                    if L == 1:
                        sp.dma_start(V("router"), io["router"]).then_inc(router_loaded, 16)
                    sp.wait_ge(*en.at(f"{L} mix post gained"))
                    sp.dma_start(V("gain"), io["ffn_post"][L:L + 1].to_broadcast([P, D])).then_inc(gain_loaded, 16)
            for u in uses:
                static(u)
            sp.wait_ge(*en.at("1 mixing over"))
            sp.wait_ge(*en.at("wout 1 1 read"))
            with sp.Fori(0, EXPERTS) as e:
                en.loop = (0, e)
                for j, s in enumerate(CHUNK_SLOT):
                    before = [k for k in range(j) if CHUNK_SLOT[k] == s]
                    if before:
                        sp.wait_ge(*en.at(f"moe chunk {before[-1]} read"))
                    else:
                        last = [k for k in range(CHUNKS) if CHUNK_SLOT[k] == s][-1]
                        sp.wait_ge(*en.at(f"moe chunk {last} read", back=1))
                    sp.dma_start(slot(s), io["moe"][e * CHUNKS + j]).then_inc(slot_filled[s], 16)
                en.loop = None
            sp.wait_ge(*en.at("final"))
            sp.dma_start(io["out"].rearrange("(n p) d -> p n d", p=P), x).then_inc(out_stored, 16)
            sp.wait_ge(out_stored, 16)

        @block.tensor
        def _(t):
            pe = Engine("pe", sems, steps)

            def mm(out, lhsT, rhs, start=True, stop=True, **kw):
                return nc.tensor.matmul(out, lhsT, rhs, start=start, stop=stop, **kw)

            reader = {}

            def take(banks, by):
                for b in banks:
                    for r in reader.get(b, ()):
                        t.wait_ge(*pe.at(r))
                    reader[b] = (by,) if isinstance(by, str) else tuple(by)

            def hidden(L, which):
                for c in range(KD):
                    take([c], f"{L} {which} hT {c}")
                    for n in range(NT):
                        t.wait_ge(*pe.at(f"{L} {which} hn {n}"))
                        last = nc.tensor.transpose(ps[:, c, n * P:(n + 1) * P], hn[:, n, c * P:(c + 1) * P], ident)
                    last.then_inc(*pe.step(f"{L} {which} hT psum {c}"))

            def ffn(L, tag, back):
                loop = pe.loop is not None

                def gate_up(i):
                    j, n = i // NT, i % NT
                    s = CHUNK_SLOT[j]
                    if n == 0:
                        if loop:
                            k = CHUNK_SLOT[:j + 1].count(s)
                            t.wait_ge(slot_filled[s], 16 * static_fills[s] + 16 * k + pe.loop[1] * (16 * per_fill[s]))
                        else:
                            t.wait_ge(*filled("ffn", L, j, s))
                    if i >= 2:
                        t.wait_ge(*pe.at(f"{tag} act {i - 2}"))
                    elif loop:
                        t.wait_ge(*pe.at(f"{tag} act {20 + i}", back=1))
                    w = slot(s)[:, 0:KD * 512].rearrange("p (c m) -> p c m", c=KD)
                    for c in range(KD):
                        last = mm(ps[:, i % 2, :], hT[:, c, n * P:(n + 1) * P], w[:, c, :],
                                  start=(c == 0), stop=(c == KD - 1))
                    last.then_inc(*pe.step(f"{tag} gate_up {i}"))

                def turn(i):
                    t.wait_ge(*pe.at(f"{tag} act {i}"))
                    if i >= 2:
                        t.wait_ge(*pe.at(f"{tag} actT {i - 2}"))
                    elif loop:
                        t.wait_ge(*pe.at(f"{tag} actT {20 + i}", back=1))
                    for k in range(2):
                        last = nc.tensor.transpose(ps[:, 2 + i % 2, k * P:(k + 1) * P],
                                                   act_buf[:, i % 2, k * P:(k + 1) * P], ident)
                    last.then_inc(*pe.step(f"{tag} turned {i}"))

                def down(i):
                    j, n = i // NT, i % NT
                    t.wait_ge(*pe.at(f"{tag} actT {i}"))
                    if j == 0 and loop:
                        t.wait_ge(*pe.at(f"{tag} y{n} taken", back=1))
                    w = slot(CHUNK_SLOT[j])[:, KD * 512:].rearrange("p (k m) -> p k m", k=2)
                    for k in range(2):
                        for h in range(2):
                            last = mm(ps[:, 4 + 2 * n + h, :], actT[:, i % 2, k, :], w[:, k, h * 512:(h + 1) * 512],
                                      start=(j == 0 and k == 0), stop=(j == CHUNKS - 1 and k == 1))
                    last.then_inc(*pe.step(f"{tag} down {i}"))
                    if n == NT - 1:
                        steps.at[f"moe chunk {j} read" if loop else f"ffn {L} {j} read"] = ("pe", pe.count)

                for i in range(NT * CHUNKS + 2):
                    if i < NT * CHUNKS:
                        gate_up(i)
                    if 1 <= i <= NT * CHUNKS:
                        turn(i - 1)
                    if i >= 2:
                        down(i - 2)

            t.wait_ge(const_loaded, 16)
            for L in range(LAYERS):
                hidden(L, "mix")
                t.wait_ge(params_loaded, 96 * (L + 1))
                for f in range(19):
                    g, s = f // WIN_GROUP, (f // WIN_GROUP) % 2
                    if f % WIN_GROUP == 0:
                        t.wait_ge(*filled("win", L, g, s))
                    if f == 0:
                        for c in range(KD):
                            t.wait_ge(*pe.at(f"{L} mix hT {c}"))
                    take([f % 8], f"{L} proj {f}")
                    w = slot(s)[:, (f % WIN_GROUP) * D:(f % WIN_GROUP + 1) * D].rearrange("p (c m) -> p c m", c=KD)
                    for c in range(KD):
                        last = mm(ps[:, f % 8, 0:S], w[:, c, :], hT[:, c, :], start=(c == 0), stop=(c == KD - 1))
                    last.then_inc(*pe.step(f"{L} proj psum {f}"))
                    if f % WIN_GROUP == WIN_GROUP - 1:
                        steps.at[f"win {L} {g} read"] = ("pe", pe.count)
                w = slot(1)[:, D:4 * D].rearrange("p (f c m) -> p f c m", f=3, c=KD)
                for n in range(NT):
                    b = 3 + n
                    take([b], f"{L} vA {n}")
                    for c in range(KD):
                        last = mm(ps[:, b, 0:384].rearrange("p (a b) -> p a b", a=3), hT[:, c, n * P:(n + 1) * P],
                                  w[:, :, c, :], start=(c == 0), stop=(c == KD - 1))
                    last.then_inc(*pe.step(f"{L} vA psum {n}"))
                steps.at[f"win {L} 3 read"] = ("pe", pe.count)
                lora, g_up = V("lora"), V("g_up")
                t.wait_ge(*pe.at(f"{L} w_lo tanh"))
                t.wait_ge(*pe.at(f"{L} shifted 9"))
                for q in range(3):
                    take([q], f"{L} decay {q}")
                    mm(ps[:, q, 0:S], lora[0:64, q * P:(q + 1) * P], pm[0:64, 9, :]).then_inc(*pe.step(f"{L} decay psum {q}"))
                for q in range(3):
                    take([3 + q], f"{L} rate {q}")
                    mm(ps[:, 3 + q, 0:S], lora[64:128, q * P:(q + 1) * P], pm[64:128, 9, :]).then_inc(*pe.step(f"{L} rate psum {q}"))
                t.wait_ge(*pe.at(f"{L} g_lo sigmoid"))
                take([6, 7], f"{L} g")
                for q in range(3):
                    last = mm(ps[:, 6 + q // 2, (q % 2) * S:(q % 2 + 1) * S], g_up[:, q * P:(q + 1) * P], pm[:, 10, :],
                              start=True, stop=True)
                last.then_inc(*pe.step(f"{L} g psum"))
                t.wait_ge(*pe.at(f"{L} kk squared"))
                take([0, 1], f"{L} kk sum out")
                sq = V("e2")
                mm(ps[:, 0, :], ones_head, sq[:, 0:512])
                mm(ps[:, 1, 0:256], ones_head, sq[:, 512:768]).then_inc(*pe.step(f"{L} kk sum"))
                t.wait_ge(*pe.at(f"{L} rk"))
                take([2, 3], f"{L} bonus")
                sq = V("e1")
                mm(ps[:, 2, :], ones_head, sq[:, 0:512])
                mm(ps[:, 3, 0:256], ones_head, sq[:, 512:768]).then_inc(*pe.step(f"{L} rk sum"))
                b_blk = V("b_blk", 2, 2, P)
                c_blk = V("c_blk", 2, 8, 32)
                for H in range(2):
                    t.wait_ge(*pe.at(f"{L} proj {11 + H}"))
                    take([4, 5, 6, 7], f"{L} bu {H} read")
                    for i in range(4):
                        r = slice(32 * i, 32 * i + 32)
                        for ri in range(2):
                            last = mm(ps[:, 4 + i, ri * S:(ri + 1) * S], b_blk[r, H, ri, :], uT[r, H, :],
                                      start=True, stop=True, tile_position=(32 * i, 0))
                    last.then_inc(*pe.step(f"{L} bu {H}"))
                    t.wait_ge(*pe.at(f"{L} s5 x {H}"))
                    t.wait_ge(*pe.at(f"{L} c scaled"))
                    take([H], f"{L} y0 {H}")
                    xr, xi = V("z0", 4, S), V("z2", 4, S)
                    for i in range(4):
                        for ri, xx in enumerate((xr, xi)):
                            last = mm(ps[32 * i:32 * i + 32, H, 0:S], c_blk[:, ri, 4 * H + i, :], xx[:, i, :],
                                      start=(ri == 0), stop=(ri == 1))
                    last.then_inc(*pe.step(f"{L} y psum {H}"))
                y = V("z0", 2, S)
                t.wait_ge(*pe.at(f"{L} gelu"))
                take([2], f"{L} glu")
                w_glu = V("w_glu", 2, S)
                for m in range(2):
                    for c in range(2):
                        last = mm(ps[:, 2, m * S:(m + 1) * S], w_glu[:, c, m * P:(m + 1) * P], y[:, c, :],
                                  start=(c == 0), stop=(c == 1))
                last.then_inc(*pe.step(f"{L} glu psum"))
                t.wait_ge(*pe.at(f"{L} s5 squared"))
                take([3], f"{L} s5 var")
                sq = V("z1", 2, S)
                for c in range(2):
                    last = mm(ps[:, 3, 0:S], ones, sq[:, c, :], start=(c == 0), stop=(c == 1))
                last.then_inc(*pe.step(f"{L} s5 sum"))
                for n in range(NT):
                    keys = (n + 1) * P
                    if n == 0:
                        for f in range(13, 19):
                            t.wait_ge(*pe.at(f"{L} proj {f}"))
                    take(range(6), f"{L} scores {n} out")
                    for h in range(6):
                        r, q = slice(64 * (h // 3), 64 * (h // 3) + 64), h % 3
                        last = mm(ps[:, h, 0:keys], qkT[r, q, n * P:(n + 1) * P], qkT[r, 3 + q, 0:keys])
                    last.then_inc(*pe.step(f"{L} scores {n}"))
                    t.wait_ge(*pe.at(f"{L} probs {n}"))
                    PT = V("PT", 3, 4, P)
                    sprob = V("s", 6, keys)
                    k = 0
                    banks = [6, 7, 0] if n else [6, 7]
                    for m in banks:
                        take([m], f"{L} PT {n} {m}")
                        blocks = [(h, jb) for h in range(6) for jb in range(n + 1)][k:k + 4]
                        for i, (h, jb) in enumerate(blocks):
                            last = nc.tensor.transpose(ps[:, m, i * P:(i + 1) * P], sprob[:, h, jb * P:(jb + 1) * P],
                                                       ident)
                        k += 4
                        last.then_inc(*pe.step(f"{L} PT psum {n} {m}"))
                    take([1], f"{L} o {n}")
                    for n2 in range(n + 1):
                        t.wait_ge(*pe.at(f"{L} vA {n2}"))
                    for m in banks:
                        t.wait_ge(*pe.at(f"{L} PT {n} {m}"))
                    for h in range(6):
                        head = 2 * (h % 3) + h // 3
                        for jb in range(n + 1):
                            i = h * (n + 1) + jb
                            last = mm(ps[:, 1, head * 64:head * 64 + 64], PT[:, i // 4, i % 4, :],
                                      vA[:, jb, head * 64:head * 64 + 64], start=(jb == 0), stop=(jb == n))
                    last.then_inc(*pe.step(f"{L} o psum {n}"))
                    t.wait_ge(*pe.at(f"{L} o normed {n}"))
                    take([2], f"{L} oT {n}")
                    aO = V("aO", 2, 384)
                    for q in range(3):
                        last = nc.tensor.transpose(ps[:, 2, q * P:(q + 1) * P], aO[:, n, q * P:(q + 1) * P], ident)
                    last.then_inc(*pe.step(f"{L} oT psum {n}"))
                for k, (src, step) in enumerate([(bh, "bh"), (kh, "kh"), (pm[:, 6:9, :], "shifted 8")]):
                    t.wait_ge(*pe.at(f"{L} {step}"))
                    for n in range(NT):
                        b = (4 + 2 * k + n) % 8
                        take([b], f"{L} natural {k} {n}")
                        for q in range(3):
                            last = nc.tensor.transpose(ps[:, b, q * P:(q + 1) * P], src[:, q, n * P:(n + 1) * P], ident)
                        last.then_inc(*pe.step(f"{L} natural psum {k} {n}"))
                t.wait_ge(*pe.at(f"{L} AR"))
                for n in range(NT):
                    for h in range(6):
                        q, r = h // 2, slice(64 * (h % 2), 64 * (h % 2) + 64)
                        i = n * 6 + h
                        b = i % 4
                        take([b], f"{L} mat {i}")
                        ar = AR[r, q, n, :, :]
                        mm(ps[:, b, 0:256].rearrange("p (a b) -> p a b", a=2), bh[r, q, n * P:(n + 1) * P], ar)
                        mm(ps[:, b, 256:512].rearrange("p (a b) -> p a b", a=2),
                                   kh[r, q, n * P:(n + 1) * P], ar).then_inc(*pe.step(f"{L} mat psum {i}"))
                def six(out_bank, lhs, rhs, step):
                    for h in range(6):
                        last = mm(ps[:, out_bank + h // 4, (h % 4) * P:(h % 4 + 1) * P], lhs(h), rhs(h),
                                  start=True, stop=True)
                    last.then_inc(*pe.step(step))

                for lv in range(LEVELS):
                    for n in range(NT):
                        t.wait_ge(*pe.at(f"{L} Am {lv} {n}"))
                        if lv:
                            t.wait_ge(*pe.at(f"{L} T {lv - 1} {n}"))
                            if lv > 1:
                                t.wait_ge(*pe.at(f"{L} TT {lv - 1} {n}"))
                        take([4 * n, 4 * n + 1], f"{L} Pm {lv} {n}")
                        six(4 * n, lambda h: Am[:, n, h, :], lambda h: T[:, n, h, :] if lv else ident,
                            f"{L} Pm psum {lv} {n}")
                    if lv == 0:
                        continue
                    for n in range(NT):
                        t.wait_ge(*pe.at(f"{L} Pm {lv} {n}"))
                        if lv < LEVELS - 1:
                            take([4 * n + 2, 4 * n + 3], f"{L} T {lv} {n}")
                            six(4 * n + 2, lambda h: TT[:, n, h, :], lambda h: Pm[:, n, h, :], f"{L} T psum {lv} {n}")
                        take([4 * n, 4 * n + 1], f"{L} TT {lv} {n}")
                        six(4 * n, lambda h: Pm[:, n, h, :], lambda h: TT[:, n, h, :], f"{L} TT psum {lv} {n}")
                rhs, sa, st = V("rhs"), V("sa"), V("st", 3, P)
                for n in range(NT):
                    take([2], f"{L} rhs {n}")
                    for q in range(3):
                        if n:
                            t.wait_ge(*pe.at(f"{L} state"))
                            mm(ps[:, 2, q * P:(q + 1) * P], AR[:, q, n, 0, :], st[:, q, :], start=True, stop=False,
                               skip_group_check=True)
                        for h in (2 * q, 2 * q + 1):
                            last = mm(ps[:, 2, h * 64:h * 64 + 64], MAT[:, n * 6 + h, 2, :],
                                      natural[:, 2, n, h * 64:h * 64 + 64], start=(n == 0), stop=True,
                                      skip_group_check=True)
                    last.then_inc(*pe.step(f"{L} rhs psum {n}"))
                    t.wait_ge(*pe.at(f"{L} rhs {n}"))
                    t.wait_ge(*pe.at(f"{L} TT {LEVELS - 1} {n}"))
                    take([3], f"{L} sa {n}")
                    for h in range(6):
                        last = mm(ps[:, 3, h * 64:h * 64 + 64], TT[:, n, h, :], rhs[:, h * 64:h * 64 + 64])
                    last.then_inc(*pe.step(f"{L} sa psum {n}"))
                    t.wait_ge(*pe.at(f"{L} sa {n}"))
                    take([6], f"{L} OT {n}")
                    for q in range(3):
                        if n:
                            mm(ps[:, 6, q * P:(q + 1) * P], st[:, q, :], AR[:, q, n, 1, :], start=True, stop=False,
                               skip_group_check=True)
                        for h in (2 * q, 2 * q + 1):
                            o = ps[64 * (h % 2):64 * (h % 2) + 64, 6, q * P:(q + 1) * P]
                            mm(o, sa[:, h * 64:h * 64 + 64], MAT[:, n * 6 + h, 1, :], start=(n == 0), stop=False,
                               skip_group_check=True)
                            last = mm(o, natural[:, 2, n, h * 64:h * 64 + 64], MAT[:, n * 6 + h, 3, :],
                                      start=False, stop=True, skip_group_check=True)
                    last.then_inc(*pe.step(f"{L} OT psum {n}"))
                    if n == 0:
                        take([7], f"{L} state")
                        for q in range(3):
                            w = slice(q * P, (q + 1) * P)
                            mm(ps[:, 7, w], natural[:, 0, n, w], sa[:, w], start=True, stop=False)
                            last = mm(ps[:, 7, w], natural[:, 1, n, w], natural[:, 2, n, w], start=False, stop=True)
                        last.then_inc(*pe.step(f"{L} state psum"))
                OT, o1, o2 = V("OT"), V("o1"), V("o2")
                t.wait_ge(*pe.at(f"{L} OT 1"))
                take([0, 1], f"{L} centred")
                mm(ps[:, 0, :], ones_head, OT[:, 0:512])
                mm(ps[:, 1, 0:256], ones_head, OT[:, 512:768]).then_inc(*pe.step(f"{L} mean psum"))
                t.wait_ge(*pe.at(f"{L} o squared"))
                take([4, 5], f"{L} gn var")
                mm(ps[:, 4, :], ones_head, o2[:, 0:512])
                mm(ps[:, 5, 0:256], ones_head, o2[:, 512:768]).then_inc(*pe.step(f"{L} var psum"))
                t.wait_ge(*pe.at(f"{L} mixed rwkv"))
                t.wait_ge(*pe.at(f"{L} mixed s5"))
                for n in range(NT):
                    t.wait_ge(*pe.at(f"{L} oT {n}"))
                    take([2 * n, 2 * n + 1], (f"{L} post square {n}", f"{L} post read {n}"))
                    for g in range(2):
                        t.wait_ge(*filled("wout", L, g, g))
                        w = slot(g)[:, 0:4096].rearrange("p (c m) -> p c m", c=4)
                        for h in range(2):
                            for c in range(4):
                                last = mm(ps[:, 2 * n + h, :], hT[:, 4 * g + c, n * P:(n + 1) * P],
                                          w[:, c, h * 512:(h + 1) * 512], start=(g == 0 and c == 0),
                                          stop=(g == 1 and c == 3), skip_group_check=True)
                    last.then_inc(*pe.step(f"{L} out psum {n}"))
                for g in range(2):
                    steps.at[f"wout {L} {g} read"] = ("pe", pe.count)
                hidden(L, "ffn")
                for c in range(KD):
                    t.wait_ge(*pe.at(f"{L} ffn hT {c}"))
                if L == 0:
                    ffn(0, "ffn", False)
                    reader = {4: ("ffn y0 taken",), 5: ("ffn y0 taken",), 6: ("ffn y1 taken",), 7: ("ffn y1 taken",),
                              2: ("ffn actT 20",), 3: ("ffn actT 21",), 0: ("ffn act 20",), 1: ("ffn act 21",)}
                else:
                    t.wait_ge(router_loaded, 16)
                    router = V("router", KD, 8)
                    take([0], "logits")
                    for n in range(NT):
                        for c in range(KD):
                            last = mm(ps[:, 0, n * 8:n * 8 + 8], hT[:, c, n * P:(n + 1) * P], router[:, c, :],
                                      start=(c == 0), stop=(c == KD - 1))
                    last.then_inc(*pe.step("logits psum"))
                    t.wait_ge(*pe.at("logits"))
                    with t.Fori(0, EXPERTS) as e:
                        pe.loop = (pe.count, e)
                        ffn(1, "moe", True)
                        steps.per["pe"] = pe.count - pe.loop[0]
                        start = pe.loop[0]
                        pe.loop = None
                    pe.count = start + EXPERTS * steps.per["pe"]

        @block.scalar
        def _(a):
            act = Engine("act", sems, steps)
            fn = nc.scalar.activation

            def rms(L, which):
                if L == 0 and which == "mix":
                    a.wait_ge(x_loaded, 16)
                for n in range(NT):
                    if not (L == 0 and which == "mix"):
                        a.wait_ge(*act.at(f"{L} x ready {which} {n}"))
                    a.wait_ge(*act.last())
                    fn(V("act")[:, 0:D], x[:, n, :], ACT.Square, accum_out=sm("ss", n)).then_inc(*act.step(f"{L} {which} ss {n}"))
                a.wait_ge(*act.at(f"{L} {which} ss mean"))
                a.wait_ge(*act.last())
                fn(sm("sq"), sm("v"), ACT.Sqrt).then_inc(*act.step(f"{L} {which} root"))
                for c in range(KD):
                    a.wait_ge(*act.at(f"{L} {which} hT psum {c}"))
                    a.wait_ge(*act.last())
                    fn(hT[:, c, :], ps[:, c, 0:S], ACT.Copy,
                                scale=col("mix_pre" if which == "mix" else "ffn_pre", c)).then_inc(*act.step(f"{L} {which} hT {c}"))
                if which == "ffn":
                    steps.at[f"{L} ffn pre gained"] = ("act", act.count)

            def ffn(tag):
                loop = act.loop is not None
                for i in range(NT * CHUNKS + 1):
                    if i < NT * CHUNKS:
                        a.wait_ge(*act.at(f"{tag} gate_up {i}"))
                        if i >= 2:
                            a.wait_ge(*act.at(f"{tag} act {i - 2}"))
                        elif loop:
                            a.wait_ge(*act.at(f"{tag} act {20 + i}", back=1))
                        a.wait_ge(*act.last())
                        fn(act_buf[:, 2 + i % 2, :], ps[:, i % 2, 0:FC], ACT.Silu).then_inc(*act.step(f"{tag} silu {i}"))
                    if i >= 1:
                        k = i - 1
                        a.wait_ge(*act.at(f"{tag} turned {k}"))
                        if k >= 2:
                            a.wait_ge(*act.at(f"{tag} down {k - 2}"))
                        elif loop:
                            a.wait_ge(*act.at(f"{tag} down {20 + k}", back=1))
                        a.wait_ge(*act.last())
                        fn(actT[:, k % 2, :, :], ps[:, 2 + k % 2, 0:2 * P].rearrange("p (a b) -> p a b", a=2),
                                    ACT.Copy).then_inc(*act.step(f"{tag} actT {k}"))

            for L in range(LAYERS):
                a.wait_ge(params_loaded, 96 * (L + 1))
                rms(L, "mix")
                a.wait_ge(*act.last())
                fn(sm("lr", 0, 8), col("log_step"), ACT.Exp).then_inc(*act.step(f"{L} step"))
                a.wait_ge(*act.at(f"{L} half angle"))
                a.wait_ge(*act.last())
                fn(sm("sn", 0, 8), sm("t1", 0, 8), ACT.Sin).then_inc(*act.step())
                a.wait_ge(*act.at(f"{L} half co-angle"))
                a.wait_ge(*act.last())
                fn(sm("cs", 0, 8), sm("t2", 0, 8), ACT.Sin).then_inc(*act.step(f"{L} sines"))
                a.wait_ge(*act.at(f"{L} log r"))
                a.wait_ge(*act.last())
                fn(sm("r", 0, 8), sm("r", 0, 8), ACT.Exp).then_inc(*act.step(f"{L} r"))
                for f in range(0, 19, 2):
                    a.wait_ge(*act.at(f"{L} proj psum {f}"))
                    dst = pT[:, f, 1:257] if f < 11 else uT[:, f - 11, :] if f < 13 else qkT[:, f - 13, :]
                    a.wait_ge(*act.last())
                    fn(dst, ps[:, f % 8, 0:S], ACT.Copy).then_inc(*act.step(f"{L} proj {f}"))
                a.wait_ge(*act.at(f"{L} vA psum 0"))
                a.wait_ge(*act.last())
                fn(vA[:, 0, :], ps[:, 3, 0:384], ACT.Copy).then_inc(*act.step(f"{L} vA 0"))
                a.wait_ge(*act.at(f"{L} shifted 9"))
                a.wait_ge(*act.last())
                fn(pm[0:64, 9, :], pm[0:64, 9, :], ACT.Tanh).then_inc(*act.step(f"{L} w_lo tanh"))
                a.wait_ge(*act.at(f"{L} shifted 10"))
                a.wait_ge(*act.last())
                fn(pm[:, 10, :], pm[:, 10, :], ACT.Tanh, scale=0.5).then_inc(*act.step(f"{L} g_lo tanh"))
                a.wait_ge(*act.at(f"{L} halved"))
                for q in range(3):
                    a.wait_ge(*act.at(f"{L} decay psum {q}"))
                    a.wait_ge(*act.last())
                    fn(V("lw", 3, S)[:, q, :], ps[:, q, 0:S], ACT.Tanh, scale=0.5, bias=sm("half", q)).then_inc(*act.step(f"{L} decay {q}"))
                for q in range(3):
                    a.wait_ge(*act.at(f"{L} rate psum {q}"))
                    a.wait_ge(*act.last())
                    fn(V("a", 3, S)[:, q, :], ps[:, 3 + q, 0:S], ACT.Tanh, scale=0.5, bias=sm("half", 3 + q)).then_inc(*act.step(f"{L} rate {q}"))
                a.wait_ge(*act.at(f"{L} g psum"))
                a.wait_ge(*act.last())
                fn(V("g"), ps[:, 6:8, :].rearrange("p a b -> p (a b)")[:, 0:768], ACT.Copy).then_inc(*act.step(f"{L} g"))
                a.wait_ge(*act.at(f"{L} kk"))
                a.wait_ge(*act.last())
                fn(V("e2"), V("kkn"), ACT.Square).then_inc(*act.step(f"{L} kk squared"))
                a.wait_ge(*act.at(f"{L} kk sum out"))
                a.wait_ge(*act.last())
                fn(V("e2"), V("e2"), ACT.Sqrt).then_inc(*act.step(f"{L} kk root"))
                a.wait_ge(*act.at(f"{L} c centred"))
                a.wait_ge(*act.last())
                fn(V("e1"), V("c"), ACT.Exp).then_inc(*act.step(f"{L} grown"))
                a.wait_ge(*act.at(f"{L} r~"))
                a.wait_ge(*act.last())
                fn(V("e1"), V("lw"), ACT.Exp).then_inc(*act.step(f"{L} grown before"))
                a.wait_ge(*act.at(f"{L} b k"))
                a.wait_ge(*act.last())
                fn(V("e2"), V("c"), ACT.Exp, scale=-1.0).then_inc(*act.step(f"{L} shrunk"))
                a.wait_ge(*act.at(f"{L} dec sum"))
                a.wait_ge(*act.last())
                fn(sm("dec"), sm("dec"), ACT.Exp).then_inc(*act.step(f"{L} dec"))
                a.wait_ge(*act.at(f"{L} gelu in"))
                a.wait_ge(*act.last())
                fn(V("z1")[:, 0:512], V("z1")[:, 0:512], ACT.Tanh, scale=GELU_C).then_inc(*act.step(f"{L} gelu tanh"))
                a.wait_ge(*act.at(f"{L} glu psum"))
                for m in range(2):
                    a.wait_ge(*act.last())
                    fn(V("z2", 2, S)[:, m, :], ps[:, 2, m * S:(m + 1) * S], ACT.Tanh, scale=0.5,
                                bias=sm("half", 6 + m)).then_inc(*act.step(f"{L} glu" if m else None))
                a.wait_ge(*act.at(f"{L} s5 y"))
                a.wait_ge(*act.last())
                fn(V("z1")[:, 0:512], V("z0")[:, 0:512], ACT.Square).then_inc(*act.step(f"{L} s5 squared"))
                a.wait_ge(*act.at(f"{L} s5 var"))
                a.wait_ge(*act.last())
                fn(V("z3")[:, 0:S], V("z3")[:, 0:S], ACT.Sqrt).then_inc(*act.step(f"{L} s5 root"))
                for n in range(NT):
                    keys = (n + 1) * P
                    sprob = V("s", 6, keys)
                    a.wait_ge(*act.at(f"{L} max {n}"))
                    for h in range(6):
                        a.wait_ge(*act.last())
                        fn(sprob[:, h, :], sprob[:, h, :], ACT.Exp, bias=sm("rmax", h),
                                    accum_out=sm("rsum", h)).then_inc(*act.step(f"{L} probs {n}" if h == 5 else None))
                    PT = V("PT", 3, 4, P)
                    for k, m in enumerate([6, 7, 0] if n else [6, 7]):
                        a.wait_ge(*act.at(f"{L} PT psum {n} {m}"))
                        w = 4 if n or k == 0 else 2
                        a.wait_ge(*act.last())
                        fn(PT[:, k, 0:w, :], ps[:, m, 0:w * P].rearrange("p (a b) -> p a b", a=w), ACT.Copy).then_inc(*act.step(f"{L} PT {n} {m}"))
                    a.wait_ge(*act.at(f"{L} o {n}"))
                    aO = V("aO", 2, 384)
                    a.wait_ge(*act.last())
                    fn(V("act")[:, 0:384], aO[:, n, :], ACT.Square, accum_out=sm("ss", n)).then_inc(*act.step(f"{L} o ss {n}"))
                    a.wait_ge(*act.at(f"{L} o ss mean {n}"))
                    a.wait_ge(*act.last())
                    fn(sm("sq", n), sm("v", n), ACT.Sqrt).then_inc(*act.step(f"{L} o root {n}"))
                    a.wait_ge(*act.at(f"{L} oT psum {n}"))
                    for q in range(3):
                        a.wait_ge(*act.last())
                        fn(hT[:, 5 + q, n * P:(n + 1) * P], ps[:, 2, q * P:(q + 1) * P], ACT.Copy,
                                    scale=col("attn_norm", q)).then_inc(*act.step(f"{L} oT {n}" if q == 2 else None))
                a.wait_ge(*act.at(f"{L} E"))
                for k in range(3):
                    for n in range(NT):
                        a.wait_ge(*act.at(f"{L} natural psum {k} {n}"))
                        a.wait_ge(*act.last())
                        fn(natural[:, k, n, :], ps[:, (4 + 2 * k + n) % 8, 0:384], ACT.Copy).then_inc(*act.step(f"{L} natural {k} {n}"))
                for lv in range(LEVELS):
                    for n in range(NT):
                        a.wait_ge(*act.at(f"{L} Pm psum {lv} {n}"))
                        if lv >= 1:
                            a.wait_ge(*act.at(f"{L} TT psum {lv - 1} {n}")) if lv > 1 else None
                        a.wait_ge(*act.last())
                        fn(V("Pm", 2, 768)[:, n, :],
                                    ps[:, 4 * n:4 * n + 2, :].rearrange("p a b -> p (a b)")[:, 0:768], ACT.Copy).then_inc(*act.step(f"{L} Pm {lv} {n}"))
                for n in range(NT):
                    a.wait_ge(*act.at(f"{L} rhs psum {n}"))
                    a.wait_ge(*act.last())
                    fn(V("rhs"), ps[:, 2, 0:384], ACT.Copy).then_inc(*act.step(f"{L} rhs {n}"))
                    a.wait_ge(*act.at(f"{L} sa psum {n}"))
                    a.wait_ge(*act.last())
                    fn(V("sa"), ps[:, 3, 0:384], ACT.Copy).then_inc(*act.step(f"{L} sa {n}"))
                    a.wait_ge(*act.at(f"{L} OT psum {n}"))
                    a.wait_ge(*act.last())
                    fn(V("OT", 3, NT, P)[:, :, n, :], ps[:, 6, 0:384].rearrange("p (a b) -> p a b", a=3),
                                ACT.Copy).then_inc(*act.step(f"{L} OT {n}"))
                a.wait_ge(*act.at(f"{L} centred"))
                a.wait_ge(*act.last())
                fn(V("o2"), V("o1"), ACT.Square).then_inc(*act.step(f"{L} o squared"))
                a.wait_ge(*act.at(f"{L} gn var"))
                a.wait_ge(*act.last())
                fn(V("o2"), V("o2"), ACT.Sqrt).then_inc(*act.step(f"{L} gn root"))
                for n in range(NT):
                    a.wait_ge(*act.at(f"{L} out psum {n}"))
                    a.wait_ge(*act.last())
                    fn(V("natural")[:, 0:D], ps[:, 2 * n:2 * n + 2, :].rearrange("p a b -> p (a b)"),
                                ACT.Square, accum_out=sm("ss", n)).then_inc(*act.step(f"{L} post square {n}"))
                a.wait_ge(*act.at(f"{L} post ss mean"))
                a.wait_ge(*act.last())
                fn(sm("sq"), sm("v"), ACT.Sqrt).then_inc(*act.step(f"{L} post root"))
                rms(L, "ffn")
                if L == 0:
                    ffn("ffn")
                else:
                    a.wait_ge(*act.at("gate in"))
                    a.wait_ge(*act.last())
                    fn(sm("g1"), sm("g1"), ACT.Exp).then_inc(*act.step("gate exp"))
                    a.wait_ge(*act.at("lg shifted"))
                    a.wait_ge(*act.last())
                    fn(sm("lg"), sm("lg"), ACT.Exp).then_inc(*act.step("lg exp"))
                    with a.Fori(0, EXPERTS) as e:
                        act.loop = (act.count, e)
                        ffn("moe")
                        steps.per["act"] = act.count - act.loop[0]
                        start = act.loop[0]
                        act.loop = None
                    act.count = start + EXPERTS * steps.per["act"]
                a.wait_ge(*act.at(f"{L} f ready"))
                for n in range(NT):
                    a.wait_ge(*act.last())
                    fn(V("natural")[:, 0:D], hn[:, n, :], ACT.Square, accum_out=sm("ss", n)).then_inc(*act.step(f"{L} fpost square {n}"))
                a.wait_ge(*act.at(f"{L} fpost ss mean"))
                a.wait_ge(*act.last())
                fn(sm("sq"), sm("v"), ACT.Sqrt).then_inc(*act.step(f"{L} fpost root"))

        @block.vector
        def _(v):
            dve = Engine("dve", sems, steps)
            ve = nc.vector

            def tt(out, a0, a1, op, step=None):
                v.wait_ge(*dve.last())
                ve.tensor_tensor(out, a0, a1, op).then_inc(*dve.step(step))

            def ts(out, a0, s1, s2, op0, op1=None, step=None):
                v.wait_ge(*dve.last())
                (ve.tensor_scalar(out, a0, s1, s2, op0, op1) if op1 is not None
                         else ve.tensor_scalar(out, a0, s1, None, op0)).then_inc(*dve.step(step))

            def stt(out, a0, s, a1, op0, op1, step=None):
                v.wait_ge(*dve.last())
                ve.scalar_tensor_tensor(out=out, in0=a0, scalar=s, in1=a1, op0=op0, op1=op1).then_inc(*dve.step(step))

            def rstd(L, what, ssname, rootname, width, n=None):
                for s in ssname:
                    v.wait_ge(*dve.at(s))
                s = (lambda k: sm(k)) if n is None else (lambda k: sm(k, n))
                ts(s("v"), s("ss"), 1.0 / width, EPS, ALU.mult, ALU.add, what)
                v.wait_ge(*dve.at(rootname))
                v.wait_ge(*dve.last())
                ve.reciprocal(s("rstd"), s("sq")).then_inc(*dve.step())

            def normed(L, which):
                rstd(L, f"{L} {which} ss mean", [f"{L} {which} ss {n}" for n in range(NT)], f"{L} {which} root", D)
                for n in range(NT):
                    ts(hn[:, n, :], x[:, n, :], sm("rstd", n), None, ALU.mult, None, f"{L} {which} hn {n}")

            def table(L):
                th, st, r = sm("theta", 0, 8), sm("lr", 0, 8), sm("r", 0, 8)
                sn, cs, t0, t1, t2 = (sm(k, 0, 8) for k in ("sn", "cs", "t0", "t1", "t2"))
                v.wait_ge(*dve.at(f"{L} step"))
                tt(th, col("a_im"), st, ALU.mult)
                ts(t0, th, 1.0 / TWO_PI, ROUND, ALU.mult, ALU.add)
                ts(t0, t0, ROUND, None, ALU.subtract)
                stt(th, t0, -TWO_PI_HI, th, ALU.mult, ALU.add)
                stt(th, t0, -TWO_PI_LO, th, ALU.mult, ALU.add)
                ts(t1, th, 0.5, None, ALU.mult, None, f"{L} half angle")
                ts(t2, t1, -1.0, None, ALU.mult)
                tt(t2, t1, t2, ALU.max)
                ts(t2, t2, -1.0, TWO_PI / 4, ALU.mult, ALU.add, f"{L} half co-angle")
                ts(t0, col("a_re"), -1e-4, None, ALU.min)
                tt(r, t0, st, ALU.mult, f"{L} log r")
                v.wait_ge(*dve.at(f"{L} sines"))
                tt(t1, sn, sn, ALU.mult)
                stt(sn, sn, 2.0, cs, ALU.mult, ALU.mult)
                ts(cs, t1, -2.0, 1.0, ALU.mult, ALU.add)
                v.wait_ge(*dve.at(f"{L} r"))
                are, aim, fr, fi, u0, u1 = t0, col("a_im"), sm("fr"), sm("fi"), sm("u0"), sm("u1")
                tt(u0, r, cs, ALU.mult)
                ts(u0, u0, 1.0, None, ALU.subtract)
                tt(u1, r, sn, ALU.mult)
                tt(fr, u0, are, ALU.mult)
                tt(t1, u1, aim, ALU.mult)
                tt(fr, fr, t1, ALU.add)
                tt(fi, u1, are, ALU.mult)
                tt(t1, u0, aim, ALU.mult)
                tt(fi, fi, t1, ALU.subtract)
                tt(t1, are, are, ALU.mult)
                tt(t2, aim, aim, ALU.mult)
                tt(t1, t1, t2, ALU.add)
                v.wait_ge(*dve.last())
                ve.reciprocal(t1, t1).then_inc(*dve.step())
                tt(fr, fr, t1, ALU.mult)
                tt(fi, fi, t1, ALU.mult)
                cb = V("c_blk", 2, 8, 32)
                s0, s1, s2 = (V("natural")[:, k * 256:(k + 1) * 256].rearrange("p (a b) -> p a b", a=8)
                              for k in range(3))
                tt(s0, cb[:, 0], bc(fi, 32), ALU.mult)
                tt(s1, cb[:, 1], bc(fi, 32), ALU.mult)
                tt(s2, cb[:, 0], bc(fr, 32), ALU.mult)
                tt(cb[:, 0], s2, s1, ALU.subtract)
                tt(s1, cb[:, 1], bc(fr, 32), ALU.mult)
                stt(cb[:, 1], s1, -1.0, s0, ALU.mult, ALU.subtract, f"{L} c scaled")

            def ffn(tag, e):
                loop = dve.loop is not None
                for i in range(NT * CHUNKS):
                    v.wait_ge(*dve.at(f"{tag} silu {i}"))
                    if i >= 2:
                        v.wait_ge(*dve.at(f"{tag} turned {i - 2}"))
                    elif loop:
                        v.wait_ge(*dve.at(f"{tag} turned {20 + i}", back=1))
                    tt(act_buf[:, i % 2, :], act_buf[:, 2 + i % 2, :], ps[:, i % 2, FC:2 * FC], ALU.mult,
                       f"{tag} act {i}")
                for n in range(NT):
                    v.wait_ge(*dve.at(f"{tag} down {20 + n}"))
                    y = ps[:, 4 + 2 * n:6 + 2 * n, :].rearrange("p a b -> p (a b)")
                    if loop:
                        c = sm("comb")[:, bass.ds(e + 8 * n, 1)]
                        stt(hn[:, n, :], y, c, hn[:, n, :], ALU.mult, ALU.add, f"{tag} y{n} taken")
                    else:
                        v.wait_ge(*dve.last())
                        ve.tensor_copy(hn[:, n, :], y).then_inc(*dve.step(f"{tag} y{n} taken"))

            for L in range(LAYERS):
                normed(L, "mix")
                v.wait_ge(params_loaded, 96 * (L + 1))
                table(L)
                v.wait_ge(*dve.last())
                ve.memset(pT[:, :, 0:1], 0.0).then_inc(*dve.step())
                for f in range(1, 19, 2):
                    v.wait_ge(*dve.at(f"{L} proj psum {f}"))
                    dst = pT[:, f, 1:257] if f < 11 else uT[:, f - 11, :] if f < 13 else qkT[:, f - 13, :]
                    v.wait_ge(*dve.last())
                    ve.tensor_copy(dst, ps[:, f % 8, 0:S]).then_inc(*dve.step(f"{L} proj {f}"))
                v.wait_ge(*dve.at(f"{L} vA psum 1"))
                v.wait_ge(*dve.last())
                ve.tensor_copy(vA[:, 1, :], ps[:, 4, 0:384]).then_inc(*dve.step(f"{L} vA 1"))
                for f in (9, 10, 3, 4, 5, 0, 1, 2, 6, 7, 8):
                    v.wait_ge(*dve.at(f"{L} proj {f}"))
                    tt(pm[:, f, :], pT[:, f, 0:256], pT[:, f, 1:257], ALU.subtract)
                    stt(pm[:, f, :], pm[:, f, :], col("mu", f), pT[:, f, 1:257], ALU.mult, ALU.add,
                        f"{L} shifted {f}")
                ts(sm("half", 0, 3), col("w0"), 0.5, None, ALU.mult)
                ts(sm("half", 3, 3), col("a0"), 0.5, None, ALU.mult)
                ts(sm("half", 6, 2), col("b_glu"), 0.5, None, ALU.mult, None, f"{L} halved")
                v.wait_ge(*dve.at(f"{L} g_lo tanh"))
                ts(pm[:, 10, :], pm[:, 10, :], 0.5, 0.5, ALU.mult, ALU.add, f"{L} g_lo sigmoid")
                kkn, e1, e2, a_, lw, c = (V(k, 3, S) for k in ("kkn", "e1", "e2", "a", "lw", "c"))
                flat = {k: V(k) for k in ("kkn", "e1", "e2", "a", "lw", "c", "kh", "bh")}
                r_, k_, v_ = pm[:, 0:3, :], pm[:, 3:6, :], pm[:, 6:9, :]
                for q in range(3):
                    ts(kkn[:, q, :], k_[:, q, :], col("k_k", q), None, ALU.mult, None, f"{L} kk")
                v.wait_ge(*dve.at(f"{L} kk sum"))
                ts(flat["e2"], ps[:, 0:2, :].rearrange("p a b -> p (a b)")[:, 0:768], 1e-24, None, ALU.max, None,
                   f"{L} kk sum out")
                v.wait_ge(*dve.at(f"{L} kk root"))
                v.wait_ge(*dve.last())
                ve.reciprocal(flat["e2"], flat["e2"]).then_inc(*dve.step())
                tt(flat["kkn"], flat["kkn"], flat["e2"], ALU.mult)
                v.wait_ge(*dve.at(f"{L} rate 2"))
                ts(flat["a"], flat["a"], 0.5, 0.5, ALU.mult, ALU.add)
                v.wait_ge(*dve.at(f"{L} decay 2"))
                ts(flat["lw"], flat["lw"], 0.5 * NEG_HALF_EXP, 0.5 * NEG_HALF_EXP, ALU.mult, ALU.add)
                for q in range(3):
                    v.wait_ge(*dve.last())
                    ve.tensor_tensor_scan(c[:, q, :], C("scan"), lw[:, q, :], 0.0, ALU.mult, ALU.add).then_inc(*dve.step())
                c4 = V("c", 3, NT, P)
                mid = c4[:, :, :, 63:64]
                v.wait_ge(*dve.last())
                ve.tensor_copy(sm("cmid").rearrange("p (a b c) -> p a b c", a=3, b=2), mid).then_inc(*dve.step())
                cm = sm("cmid").rearrange("p (a b) -> p a b", a=3)
                tt(sm("dec"), c4[:, :, 0, 127], cm[:, :, 0], ALU.subtract)
                tt(sm("dec"), sm("dec"), cm[:, :, 1], ALU.add, f"{L} dec sum")
                tt(V("c", 6, P), V("c", 6, P), bc(sm("cmid"), P), ALU.subtract, f"{L} c centred")
                tt(flat["lw"], flat["c"], flat["lw"], ALU.subtract)
                for q in range(3):
                    ts(bh[:, q, :], a_[:, q, :], 1.0, col("k_a", q), ALU.subtract, ALU.mult)
                stt(k_, bh, 1.0, k_, ALU.add, ALU.mult)
                v.wait_ge(*dve.at(f"{L} grown"))
                for q in range(3):
                    tt(AR[:, q, :, 1, :], r_[:, q, :].rearrange("p (n s) -> p n s", n=NT),
                       e1[:, q, :].rearrange("p (n s) -> p n s", n=NT), ALU.mult, f"{L} r~")
                v.wait_ge(*dve.at(f"{L} grown before"))
                for q in range(3):
                    stt(AR[:, q, :, 0, :], kkn[:, q, :].rearrange("p (n s) -> p n s", n=NT), -1.0,
                        e1[:, q, :].rearrange("p (n s) -> p n s", n=NT), ALU.mult, ALU.mult, f"{L} AR")
                for q in range(3):
                    stt(e1[:, q, :], r_[:, q, :], col("r_k", q), k_[:, q, :], ALU.mult, ALU.mult, f"{L} rk")
                tt(flat["bh"], flat["kkn"], flat["a"], ALU.mult, f"{L} b k")
                v.wait_ge(*dve.at(f"{L} shrunk"))
                tt(flat["bh"], flat["bh"], flat["e2"], ALU.mult, f"{L} bh")
                tt(kh, k_, e2, ALU.mult, f"{L} kh")
                v.wait_ge(*dve.at(f"{L} rk sum"))
                tt(V("bonus"), ps[:, 2:4, :].rearrange("p a b -> p (a b)")[:, 0:768],
                   pm[:, 6:9, :].rearrange("p a b -> p (a b)"), ALU.mult, f"{L} bonus")
                v.wait_ge(*dve.at(f"{L} E"))
                for H in range(2):
                    Er, Ei = E[:, 0, 4 * H:4 * H + 4, :], E[:, 1, 4 * H:4 * H + 4, :]
                    z = [V(f"z{i}", 4, S) for i in range(5)]
                    v.wait_ge(*dve.at(f"{L} bu {H}"))
                    if H:
                        v.wait_ge(*dve.at(f"{L} y psum 0"))
                    br, bi = ps[:, 4:8, 0:S], ps[:, 4:8, S:2 * S]
                    tt(z[0], br, Er, ALU.mult)
                    tt(z[1], bi, Ei, ALU.mult)
                    tt(z[2], bi, Er, ALU.mult)
                    tt(z[3], br, Ei, ALU.mult, f"{L} bu {H} read")
                    tt(z[0], z[0], z[1], ALU.add)
                    tt(z[2], z[2], z[3], ALU.subtract)
                    for i in range(4):
                        rr = sm("r", 4 * H + i).to_broadcast([P, S])
                        v.wait_ge(*dve.last())
                        ve.tensor_tensor_scan(z[1][:, i, :], rr, z[0][:, i, :], 0.0, ALU.mult, ALU.add).then_inc(*dve.step())
                        v.wait_ge(*dve.last())
                        ve.tensor_tensor_scan(z[3][:, i, :], rr, z[2][:, i, :], 0.0, ALU.mult, ALU.add).then_inc(*dve.step())
                    tt(z[0], z[1], Er, ALU.mult)
                    tt(z[2], z[3], Ei, ALU.mult)
                    tt(z[0], z[0], z[2], ALU.subtract)
                    tt(z[2], z[3], Er, ALU.mult)
                    tt(z[4], z[1], Ei, ALU.mult)
                    tt(z[2], z[2], z[4], ALU.add, f"{L} s5 x {H}")
                    v.wait_ge(*dve.at(f"{L} y psum {H}"))
                    stt(uT[:, H, :], uT[:, H, :], col("s5_d", H), ps[:, H, 0:S], ALU.mult, ALU.add, f"{L} y0 {H}")
                y, w1, w2 = V("z0")[:, 0:512], V("z1")[:, 0:512], V("z2")[:, 0:512]
                u = V("uT")
                tt(w1, u, u, ALU.mult)
                ts(w1, w1, 0.044715, 1.0, ALU.mult, ALU.add)
                tt(w1, w1, u, ALU.mult, f"{L} gelu in")
                v.wait_ge(*dve.at(f"{L} gelu tanh"))
                stt(y, w1, 1.0, u, ALU.add, ALU.mult)
                ts(y, y, 0.5, None, ALU.mult, None, f"{L} gelu")
                v.wait_ge(*dve.at(f"{L} glu"))
                ts(w2, w2, 0.5, 0.5, ALU.mult, ALU.add)
                tt(y, y, w2, ALU.mult, f"{L} s5 y")
                v.wait_ge(*dve.at(f"{L} s5 sum"))
                ts(V("z3")[:, 0:S], ps[:, 3, 0:S], 1.0 / S, EPS, ALU.mult, ALU.add, f"{L} s5 var")
                v.wait_ge(*dve.at(f"{L} s5 root"))
                v.wait_ge(*dve.last())
                ve.reciprocal(V("z3")[:, 0:S], V("z3")[:, 0:S]).then_inc(*dve.step())
                for m in range(2):
                    stt(hT[:, 3 + m, :], V("z0", 2, S)[:, m, :], col("s5_norm", m), V("z3")[:, 0:S], ALU.mult,
                        ALU.mult, f"{L} mixed s5")
                steps.at[f"{L} s5 scratch free"] = ("dve", dve.count)
                bias = V("bias", 6, 384)
                v.wait_ge(bias_loaded, 16 * (L + 1))
                for n in range(NT):
                    keys = (n + 1) * P
                    sprob = V("s", 6, keys)
                    v.wait_ge(*dve.at(f"{L} scores {n}"))
                    if n:
                        v.wait_ge(*dve.at(f"{L} PT psum 0 7"))
                    stt(sprob, ps[:, 0:6, 0:keys], 0.125, bias[:, :, (1 - n) * P:(1 - n) * P + keys],
                        ALU.mult, ALU.add, f"{L} scores {n} out")
                    v.wait_ge(*dve.last())
                    ve.memset(sprob[0:64, :, keys - 64:keys], -3.0e38).then_inc(*dve.step())
                    if n:
                        v.wait_ge(*dve.at(f"{L} probs 0"))
                    v.wait_ge(*dve.last())
                    ve.tensor_reduce(sm("rmax", 0, 6), sprob, AX.X, ALU.max).then_inc(*dve.step())
                    ts(sm("rmax", 0, 6), sm("rmax", 0, 6), -1.0, None, ALU.mult, None, f"{L} max {n}")
                    v.wait_ge(*dve.at(f"{L} probs {n}"))
                    v.wait_ge(*dve.last())
                    ve.reciprocal(sm("rinv", 0, 6), sm("rsum", 0, 6)).then_inc(*dve.step())
                    v.wait_ge(*dve.at(f"{L} o psum {n}"))
                    aO = V("aO", 2, 3, 2, 64)
                    for par in range(2):
                        tt(aO[:, n, :, par, :], ps[:, 1, 0:384].rearrange("p (a b c) -> p a b c", a=3, b=2)[:, :, par, :],
                           bc(sm("rinv", 3 * par, 3), 64), ALU.mult, f"{L} o {n}")
                    rstd(L, f"{L} o ss mean {n}", [f"{L} o ss {n}"], f"{L} o root {n}", 384, n)
                    ts(V("aO", 2, 384)[:, n, :], V("aO", 2, 384)[:, n, :], sm("rstd", n), None, ALU.mult, None,
                       f"{L} o normed {n}")
                for b in range(3):
                    for n in range(NT):
                        v.wait_ge(*dve.at(f"{L} natural psum {b} {n}"))
                for i in range(12):
                    v.wait_ge(*dve.at(f"{L} mat psum {i}"))
                    tt(MAT[:, i].rearrange("p a b -> p (a b)"), ps[:, i % 4, :], C("masks4"), ALU.mult, f"{L} mat {i}")
                for n in range(NT):
                    a_t = MAT[:, n * 6:n * 6 + 6, 0, :]
                    tt(Am[:, n], a_t, C("level")[:, 0:P].unsqueeze(1).to_broadcast([P, 6, P]), ALU.mult,
                       f"{L} Am 0 {n}")
                    tt(TT[:, n], Am[:, n], ident.unsqueeze(1).to_broadcast([P, 6, P]), ALU.add)
                for n in range(NT):
                    v.wait_ge(*dve.at(f"{L} Pm 0 {n}"))
                    tt(T[:, n], Pm[:, n], ident.unsqueeze(1).to_broadcast([P, 6, P]), ALU.add, f"{L} T 0 {n}")
                for lv in range(1, LEVELS):
                    for n in range(NT):
                        if lv < LEVELS - 1:
                            v.wait_ge(*dve.at(f"{L} T psum {lv} {n}"))
                            v.wait_ge(*dve.at(f"{L} Pm psum {lv} {n}"))
                            tt(V("T", 2, 768)[:, n], V("T", 2, 768)[:, n],
                               ps[:, 4 * n + 2:4 * n + 4, :].rearrange("p a b -> p (a b)")[:, 0:768], ALU.add,
                               f"{L} T {lv} {n}")
                        v.wait_ge(*dve.at(f"{L} TT psum {lv} {n}"))
                        tt(V("TT", 2, 768)[:, n], V("TT", 2, 768)[:, n],
                           ps[:, 4 * n:4 * n + 2, :].rearrange("p a b -> p (a b)")[:, 0:768], ALU.add,
                           f"{L} TT {lv} {n}")
                v.wait_ge(*dve.at(f"{L} state psum"))
                for q in range(3):
                    stt(V("st", 3, P)[:, q, :], ps[:, 7, q * P:(q + 1) * P], sm("dec", q), ones_head, ALU.mult,
                        ALU.mult, f"{L} state")
                OT, o1, o2 = V("OT"), V("o1"), V("o2")
                v.wait_ge(*dve.at(f"{L} mean psum"))
                v.wait_ge(*dve.at(f"{L} OT 1"))
                stt(o1, ps[:, 0:2, :].rearrange("p a b -> p (a b)")[:, 0:768], -1.0 / 64, OT, ALU.mult, ALU.add,
                    f"{L} centred")
                v.wait_ge(*dve.at(f"{L} var psum"))
                ts(o2, ps[:, 4:6, :].rearrange("p a b -> p (a b)")[:, 0:768], 1.0 / 64, GN_EPS, ALU.mult, ALU.add,
                   f"{L} gn var")
                v.wait_ge(*dve.at(f"{L} gn root"))
                v.wait_ge(*dve.last())
                ve.reciprocal(o2, o2).then_inc(*dve.step())
                tt(o1, o1, o2, ALU.mult)
                for q in range(3):
                    oq = V("o1", 3, S)[:, q, :]
                    ts(oq, oq, col("ln_w", q), col("ln_b", q), ALU.mult, ALU.add)
                tt(o1, o1, V("bonus"), ALU.add)
                v.wait_ge(*dve.at(f"{L} g"))
                tt(hT[:, 0:3, :].rearrange("p a b -> p (a b)"), o1, V("g"), ALU.mult, f"{L} mixed rwkv")
                steps.at[f"{L} mixing over"] = ("dve", dve.count)
                steps.at[f"{L} mix used params"] = ("dve", dve.count)
                rstd(L, f"{L} post ss mean", [f"{L} post square {n}" for n in range(NT)], f"{L} post root", D)
                v.wait_ge(gain_loaded, 16 + 32 * L)
                tmp = V("natural")[:, 0:D]
                for n in range(NT):
                    stt(tmp, ps[:, 2 * n:2 * n + 2, :].rearrange("p a b -> p (a b)"), sm("rstd", n), V("gain"),
                        ALU.mult, ALU.mult, f"{L} post read {n}")
                    if n == NT - 1:
                        steps.at[f"{L} mix post gained"] = ("dve", dve.count)
                    tt(x[:, n, :], x[:, n, :], tmp, ALU.add, f"{L} x ready ffn {n}")
                steps.at["final"] = ("dve", dve.count)
                normed(L, "ffn")
                if L == 0:
                    ffn("ffn", None)
                    steps.at["0 f ready"] = ("dve", dve.count)
                else:
                    v.wait_ge(*dve.at("logits psum"))
                    lg = sm("lg")
                    v.wait_ge(*dve.last())
                    ve.tensor_copy(lg, ps[:, 0, 0:16]).then_inc(*dve.step("logits"))
                    for n in range(NT):
                        v.wait_ge(*dve.last())
                        ve.max(sm("m8", 8 * n, 8), sm("lg", 8 * n, 8)).then_inc(*dve.step())
                    m8 = sm("m8").rearrange("p (n e) -> p n e", n=NT)
                    tt(sm("g1"), m8[:, :, 1], m8[:, :, 0], ALU.subtract, "gate in")
                    v.wait_ge(*dve.at("gate exp"))
                    ts(sm("g1"), sm("g1"), 1.0, None, ALU.add)
                    v.wait_ge(*dve.last())
                    ve.reciprocal(sm("g1"), sm("g1")).then_inc(*dve.step())
                    comb, lg3 = sm("comb").rearrange("p (n e) -> p n e", n=NT), lg.rearrange("p (n e) -> p n e", n=NT)
                    tt(comb, lg3, m8[:, :, 1:2].to_broadcast([P, NT, 8]), ALU.is_ge)
                    tt(lg3, lg3, m8[:, :, 0:1].to_broadcast([P, NT, 8]), ALU.subtract, "lg shifted")
                    v.wait_ge(*dve.at("lg exp"))
                    tt(comb, comb, lg3, ALU.mult)
                    tt(comb, comb, bc(sm("g1"), 8), ALU.mult)
                    v.wait_ge(*dve.at("1 ffn hT 7"))
                    v.wait_ge(*dve.last())
                    ve.memset(V("hn"), 0.0).then_inc(*dve.step())
                    with v.Fori(0, EXPERTS) as e:
                        dve.loop = (dve.count, e)
                        ffn("moe", e)
                        steps.per["dve"] = dve.count - dve.loop[0]
                        start = dve.loop[0]
                        dve.loop = None
                    dve.count = start + EXPERTS * steps.per["dve"]
                    steps.at["1 f ready"] = ("dve", dve.count)
                rstd(L, f"{L} fpost ss mean", [f"{L} fpost square {n}" for n in range(NT)], f"{L} fpost root", D)
                v.wait_ge(gain_loaded, 32 + 32 * L)
                tmp = V("natural")[:, 0:D]
                for n in range(NT):
                    stt(tmp, hn[:, n, :], sm("rstd", n), V("gain"), ALU.mult, ALU.mult)
                    tt(x[:, n, :], x[:, n, :], tmp, ALU.add, f"{L + 1} x ready mix {n}")
                steps.at[f"{L + 1} gain 0 free"] = ("dve", dve.count)
                steps.at["final"] = ("dve", dve.count)

        @block.gpsimd
        def _(g):
            pool = Engine("pool", sems, steps)

            def tt(out, a0, a1, op, step=None):
                g.wait_ge(*pool.last())
                nc.gpsimd.tensor_tensor(out, a0, a1, op).then_inc(*pool.step(step))

            for L in range(LAYERS):
                g.wait_ge(*pool.at(f"{L} c scaled"))
                g.wait_ge(*pool.last())
                nc.gpsimd.memset(E[:, 0, :, 0:1], 1.0).then_inc(*pool.step())
                g.wait_ge(*pool.last())
                nc.gpsimd.memset(E[:, 1, :, 0:1], 0.0).then_inc(*pool.step())
                g.wait_ge(*pool.last())
                nc.gpsimd.tensor_copy(E[:, 0, :, 1], sm("cs", 0, 8)).then_inc(*pool.step())
                g.wait_ge(*pool.last())
                nc.gpsimd.tensor_copy(E[:, 1, :, 1], sm("sn", 0, 8)).then_inc(*pool.step(f"{L} E"))
                m = 2
                w0, w1 = V("natural")[:, 0:1016].rearrange("p (a b) -> p a b", a=8), \
                    V("natural")[:, 1024:2040].rearrange("p (a b) -> p a b", a=8)
                while m < S:
                    for first in (True, False):
                        a0, b0 = (slice(m - 1, m), 1) if first else (slice(1, m), m)
                        out = slice(m, m + 1) if first else slice(m + 1, 2 * m)
                        n = out.stop - out.start
                        br, bi = (E[:, q, :, b0:b0 + 1].to_broadcast([P, 8, n]) for q in range(2))
                        ar, ai = E[:, 0, :, a0], E[:, 1, :, a0]
                        o0, o1 = w0[:, :, 0:n], w1[:, :, 0:n]
                        tt(o0, ar, br, ALU.mult)
                        tt(o1, ai, bi, ALU.mult)
                        tt(E[:, 0, :, out], o0, o1, ALU.subtract)
                        tt(o0, ar, bi, ALU.mult)
                        tt(o1, ai, br, ALU.mult)
                        tt(E[:, 1, :, out], o0, o1, ALU.add, f"{L} E")
                    m *= 2
                for lv in range(1, LEVELS):
                    for n in range(NT):
                        g.wait_ge(*pool.at(f"{L} Pm psum {lv - 1} {n}"))
                        if lv == 1:
                            g.wait_ge(*pool.at(f"{L} T 0 {n}"))
                        level = C("level")[:, lv * P:(lv + 1) * P].unsqueeze(1).to_broadcast([P, 6, P])
                        tt(Am[:, n], MAT[:, n * 6:n * 6 + 6, 0, :], level, ALU.mult, f"{L} Am {lv} {n}")


def kernel(**inputs):
    import concourse.bacc as _bacc
    from concourse.bass_utils import run_bass_kernel_spmd as _run

    L = LAYERS
    i = {k: np.asarray(v) for k, v in inputs.items()}

    def tiles(a, n):
        return a.reshape(L, n, P).transpose(0, 2, 1)

    def groups(a):
        return a.reshape(L, 8, P).transpose(0, 2, 1)

    cols = np.concatenate([
        tiles(i["norm_mix_pre"], 8), tiles(i["norm_ffn_pre"], 8), tiles(i["rwkv_mu"], 11), tiles(i["rwkv_w0"], 3),
        tiles(i["rwkv_a0"], 3), tiles(i["rwkv_k_k"], 3), tiles(i["rwkv_k_a"], 3), tiles(i["rwkv_r_k"], 3),
        tiles(i["rwkv_ln_w"], 3), tiles(i["rwkv_ln_b"], 3), tiles(i["s5_d"], 2), tiles(i["s5_b_glu"], 2),
        tiles(i["s5_norm"], 2), tiles(i["attn_norm"], 3), groups(i["s5_a_re"]), groups(i["s5_a_im"]),
        groups(np.repeat(i["s5_log_step"][:, :, None], 64, axis=2))], axis=2)
    b_blk = np.zeros((L, 2, 4, 2, 16, 2, 2, 64), np.float32)
    c_blk = np.zeros((L, 2, 64, 2, 8, 2, 16), np.float32)
    for ri, (b, c) in enumerate([("s5_b_re", "s5_c_re"), ("s5_b_im", "s5_c_im")]):
        bb = i[b].reshape(L, 2, 4, 2, 64, 16)
        cc = i[c].reshape(L, 8, 2, 16, 64)
        for g in range(2):
            b_blk[:, :, :, g, :, ri, g, :] = bb[:, :, :, g].transpose(0, 1, 2, 4, 3)
            c_blk[:, g, :, ri, :, g, :] = cc[:, :, g].transpose(0, 3, 1, 2)
    b_blk = b_blk.transpose(0, 2, 3, 4, 1, 5, 6, 7).reshape(L, P, 512)
    c_blk = c_blk.reshape(L, P, 512)
    rel = np.clip(np.arange(P)[:, None] + P - np.arange(384)[None, :], -128, 128) + 128
    bias = i["attn_rel_bias"][:, :, rel][:, [0, 2, 4, 1, 3, 5]].transpose(0, 2, 1, 3).reshape(L, P, 2304)

    def ffn(gate, up, down):
        n = gate.shape[0]
        gu = np.stack([gate.reshape(n, KD, P, CHUNKS, FC), up.reshape(n, KD, P, CHUNKS, FC)], axis=4)
        gu = gu.transpose(0, 3, 2, 1, 4, 5).reshape(n, CHUNKS, P, KD * 512)
        dn = down.reshape(n, CHUNKS, 2, P, D).transpose(0, 1, 3, 2, 4).reshape(n, CHUNKS, P, 2 * D)
        return np.concatenate([gu, dn], axis=3).reshape(n * CHUNKS, P, SLOT)

    arrays = {
        "x": i["x"].reshape(S, D),
        "const": constants(),
        "cols": cols,
        "b_blk": b_blk,
        "c_blk": c_blk,
        "w_glu": i["s5_w_glu"].reshape(L, 2, P, S).transpose(0, 2, 1, 3).reshape(L, P, 512),
        "lora": np.concatenate([i["rwkv_w_up"], i["rwkv_a_up"]], axis=1),
        "g_up": i["rwkv_g_up"],
        "w_in": i["w_in"].reshape(L, KD, P, WT, P).transpose(0, 2, 3, 1, 4).reshape(L, P, WT * D),
        "w_out": i["w_out"].reshape(L, KD, P, D).transpose(0, 2, 1, 3).reshape(L, P, KD * D),
        "bias": bias,
        "mix_post": i["norm_mix_post"],
        "ffn_post": i["norm_ffn_post"],
        "router": i["moe_router"][0].reshape(KD, P, EXPERTS).transpose(1, 0, 2).reshape(P, KD * EXPERTS),
        "ffn": ffn(i["ffn_w_gate"], i["ffn_w_up"], i["ffn_w_down"]),
        "moe": ffn(i["moe_w_gate"][0], i["moe_w_up"][0], i["moe_w_down"][0]),
    }
    arrays = {k: np.ascontiguousarray(v) for k, v in arrays.items()}

    steps = Steps()
    for _ in range(2):
        nc = _bacc.Bacc("TRN2", target_bir_lowering=False, num_devices=1)
        io = {k: nc.dram_tensor(f"in_{k}", a.shape, mybir.dt.from_np(a.dtype), kind="ExternalInput").ap()
              for k, a in arrays.items()}
        io["out"] = nc.dram_tensor("out_0", (S, D), F32, kind="ExternalOutput").ap()
        build(nc, steps, io)
        steps.final = True
    r = _run(nc, [{f"in_{k}": a for k, a in arrays.items()}], core_ids=[0])
    return r.results[0]["out_0"].reshape(1, S, D)
```

```python
from contextlib import ExitStack

import numpy as np

import concourse.bass as bass
from concourse import mybir

F32 = mybir.dt.float32
ALU = mybir.AluOpType
ACT = mybir.ActivationFunctionType
AX = mybir.AxisListType

P = 128
D = 1024
S = 256
NT = S // P
KD = D // P
LAYERS = 2
EXPERTS = 8
MORE = 3
COLUMNS = EXPERTS + MORE + 1
F = 2816
FC = 256
CHUNKS = F // FC
WIN = 2816
WT = WIN // P
SLOT = KD * 2 * FC + 2 * D
SLOTS = 5
WIN_GROUP = 6
CHUNK_SLOT = [0, 1, 2, 3, 0, 4, 1, 2, 0, 3, 4]
EPS = 1e-6
GN_EPS = 64e-5
NEG_HALF_EXP = -0.6065306597126334
TWO_PI = 6.283185307179586
TWO_PI_HI = 6.28125
TWO_PI_LO = TWO_PI - TWO_PI_HI
ROUND = 12582912.0
GELU_C = 0.7978845608028654

COLS = {}
_at = 0
for _name, _n in [("mix_pre", 8), ("ffn_pre", 8), ("mu", 11), ("w0", 3), ("a0", 3), ("k_k", 3), ("k_a", 3),
                  ("r_k", 3), ("ln_w", 3), ("ln_b", 3), ("s5_d", 2), ("b_glu", 2), ("s5_norm", 2),
                  ("attn_norm", 3), ("a_re", 8), ("a_im", 8), ("log_step", 8)]:
    COLS[_name] = (_at, _n)
    _at += _n
NCOL = _at

LEVELS = 7
CONST = {}
_at = 0
for _name, _n in [("ident", 128), ("ones", 128), ("ones_head", 128), ("masks4", 512), ("level", LEVELS * 128),
                  ("scan", 256), ("iota", 128)]:
    CONST[_name] = (_at, _n)
    _at += _n
NCONST = _at


def constants():
    i = np.arange(P)
    s, t = i[:, None], i[None, :]
    strict, incl = (s < t), (s <= t)
    level = [((s // (2 * m)) == (t // (2 * m))) & (s % (2 * m) < m) & (t % (2 * m) >= m)
             for m in (1 << np.arange(LEVELS))]
    scan = np.ones((P, S))
    scan[:, ::P] = 0
    parts = [np.eye(P), np.ones((P, P)), (s // 64) == (t // 64), strict, incl, strict, incl, *level, scan,
             np.broadcast_to(i, (P, P))]
    return np.concatenate([np.asarray(a, np.float32) for a in parts], axis=1)


ARENA = {}


def _place(start, items):
    at = start
    for name, n in items:
        ARENA[name] = (at, n)
        at += n
    return at


RING_END = SLOTS * SLOT
_end = _place(RING_END, [
    ("x", NT * D), ("hT", KD * S), ("hn", NT * D), ("const", NCONST), ("cols", NCOL), ("b_blk", 512),
    ("c_blk", 512), ("w_glu", 512), ("lora", 384), ("g_up", 384), ("E", 4096), ("act", 1536),
    ("natural", 2304), ("bonus", 768), ("g", 768), ("gain", D), ("small", 320), ("router", 64)])
ARENA_END = _end
MIX0 = 2 * SLOT
_end = _place(MIX0, [("kh", 768), ("bh", 768), ("pT", 11 * 257 + 1), ("pm", 2816), ("a", 768), ("lw", 768),
                     ("c", 768), ("qkT", 1536), ("vA", 768), ("bias", 2304), ("s", 1536),
                     ("PT", 1536), ("aO", 768)])
assert _end <= RING_END, (_end, RING_END)
_place(ARENA["pT"][0], [("kkn", 768), ("e1", 768), ("e2", 768)])
_place(ARENA["bias"][0], [(f"z{i}", 1024) for i in range(5)])
_place(ARENA["pT"][0], [("MAT", 12 * 512), ("T", 1536), ("TT", 1536), ("Pm", 1536), ("Am", 1536)])
assert ARENA["Am"][0] + 1536 <= RING_END
_place(ARENA["hn"][0], [("AR", 1536), ("uT", 512)])
_place(ARENA["act"][0], [("rhs", 384), ("sa", 384), ("st", 384)])
_place(ARENA["hT"][0], [("hTe", 1024), ("disp", 256), ("gated", 256), ("gatedT", 256)])
_place(ARENA["E"][0], [("ffn_sum", 2048), ("y", 1024), ("sel", 16), ("rank", 24), ("eq", 16), ("cum", 16), ("over", 8),
                       ("order", 8), ("onehot", 8), ("prod", 16), ("pick", 2), ("slot_of", NT * COLUMNS),
                       ("gate_of", NT * COLUMNS)])
_place(ARENA["Pm"][0], [("OT", 768), ("o1", 768)])
_place(ARENA["Am"][0], [("o2", 768)])

SMALL = {}
_at = 0
for _name, _n in [("ss", 2), ("v", 2), ("sq", 2), ("rstd", 2), ("theta", 16), ("t0", 16), ("t1", 16), ("t2", 16),
                  ("lr", 16), ("r", 16), ("sn", 16), ("cs", 16), ("fr", 8), ("fi", 8), ("u0", 8), ("u1", 8),
                  ("half", 8), ("rmax", 12), ("rsum", 12), ("rinv", 12), ("dec", 3), ("cmid", 6), ("lg", 16),
                  ("m8", 16), ("comb", 16), ("g1", 2), ("passes", 16), ("total", 1)]:
    SMALL[_name] = (_at, _n)
    _at += _n
assert _at <= 320, _at


class Steps:

    def __init__(self):
        self.at = {}
        self.per = {}
        self.final = False


class Engine:

    def __init__(self, name, sems, steps):
        self.name, self.sems, self.steps = name, sems, steps
        self.count, self.part, self.i, self.start = 0, "before", None, 0

    def step(self, name=None):
        self.count += 1
        if name is not None:
            self.steps.at[name] = (self.name, self.count, self.part)
        return self.sems[self.name], 1

    def enter(self, i):
        self.part, self.i, self.start = "loop", i, self.count

    def leave(self, total):
        self.steps.per[self.name] = self.count - self.start
        self.part, self.i, self.count = "after", total, self.start

    def value(self, engine, value, part, back=0):
        if part != "before":
            value = value + self.steps.per.get(engine, 1) * (self.i - back)
        return self.sems[engine], value

    def last(self):
        part = self.part
        if part != "before" and self.count == self.start:
            part = "loop"
        return self.value(self.name, self.count, part)

    def at(self, name, back=0):
        if name not in self.steps.at and self.steps.final:
            raise KeyError(name)
        engine, value, part = self.steps.at.get(name, ("pe", 1 << 12, "before"))
        return self.value(engine, value, part, back)


def build(nc, steps, io):
    ctx = ExitStack()
    with ctx:
        arena = ctx.enter_context(nc.sbuf_tensor("arena", [P, ARENA_END], F32))
        ps = ctx.enter_context(nc.psum_tensor("ps", [P, 8, 512], F32))
        sems = {n: ctx.enter_context(nc.semaphore(f"{n}_done")) for n in ("pe", "act", "dve", "pool")}
        slot_filled = [ctx.enter_context(nc.semaphore(f"slot_filled{i}")) for i in range(SLOTS)]
        x_loaded = ctx.enter_context(nc.semaphore("x_loaded"))
        const_loaded = ctx.enter_context(nc.semaphore("const_loaded"))
        params_loaded = ctx.enter_context(nc.semaphore("params_loaded"))
        bias_loaded = ctx.enter_context(nc.semaphore("bias_loaded"))
        gain_loaded = ctx.enter_context(nc.semaphore("gain_loaded"))
        router_loaded = ctx.enter_context(nc.semaphore("router_loaded"))
        out_stored = ctx.enter_context(nc.semaphore("out_stored"))

        def V(name, *dims):
            at, n = ARENA[name]
            size = int(np.prod(dims)) if dims else n
            a = arena[:, at:at + size]
            if len(dims) > 1:
                names = "abcd"[:len(dims)]
                a = a.rearrange(f"p ({' '.join(names)}) -> p {' '.join(names)}", **dict(zip(names, dims)))
            return a

        def C(name):
            at, n = CONST[name]
            return V("const")[:, at:at + n]

        def col(name, i=None):
            at, n = COLS[name]
            c = V("cols")
            return c[:, at:at + n] if i is None else c[:, at + i:at + i + 1]

        def sm(name, i=None, n=1):
            at, k = SMALL[name]
            s = V("small")
            return s[:, at:at + k] if i is None else s[:, at + i:at + i + n]

        def slot(i):
            return arena[:, i * SLOT:(i + 1) * SLOT]

        x, hT, hn = V("x", NT, D), V("hT", KD, S), V("hn", NT, D)
        ident, ones, ones_head = C("ident"), C("ones"), C("ones_head")
        E = V("E", 2, 8, S)
        pT, pm = V("pT", 11, 257), V("pm", 11, S)
        AR = V("AR", 3, NT, 2, P)
        kh, bh = V("kh", 3, S), V("bh", 3, S)
        natural = V("natural", 3, NT, 384)
        MAT = V("MAT", 12, 4, P)
        T, TT, Pm, Am = (V(n, 2, 6, P) for n in ("T", "TT", "Pm", "Am"))
        act_buf, actT = V("act")[:, 0:1024].rearrange("p (a b) -> p a b", a=4), \
            V("act")[:, 1024:1536].rearrange("p (a b c) -> p a b c", a=2, b=2)
        uT, qkT, vA = V("uT", 2, S), V("qkT", 6, S), V("vA", NT, 384)

        def bc(a, n):
            return a.unsqueeze(2).to_broadcast([P, a.shape[1], n])

        ffn_sum, hTe, y_sb = V("ffn_sum", NT, D), V("hTe", KD, P), V("y")
        disp, gated, gatedT = V("disp", NT, P), V("gated", NT, P), V("gatedT", NT, P)
        slot_of, gate_of = V("slot_of", NT, COLUMNS), V("gate_of", NT, COLUMNS)
        passes_at = ARENA["small"][0] + SMALL["passes"][0]
        passes = arena[0:1, passes_at:passes_at + 17].bitcast(mybir.dt.int32)

        block = ctx.enter_context(nc.Block())

        uses = []
        for L in range(LAYERS):
            uses += [("win", L, g, g % 2) for g in range(4)] + [("wout", L, g, g % 2) for g in range(2)]
            if L == 0:
                uses += [("ffn", 0, j, CHUNK_SLOT[j]) for j in range(CHUNKS)]
        fill_no, fills = {}, [0] * SLOTS
        last_reader = [None] * SLOTS
        prev_reader = {}
        for u in uses:
            prev_reader[u] = last_reader[u[3]]
            last_reader[u[3]] = f"{u[0]} {u[1]} {u[2]} read"
            fills[u[3]] += 1
            fill_no[u[:3]] = fills[u[3]]
        static_fills = list(fills)
        per_fill = [CHUNK_SLOT.count(i) for i in range(SLOTS)]

        def filled(kind, L, part, s):
            return slot_filled[s], 16 * fill_no[(kind, L, part)]

        @block.sync
        def _(sp):
            en = Engine("sp", sems, steps)
            sp.dma_start(V("x", NT, D), io["x"].rearrange("(n p) d -> p n d", p=P)).then_inc(x_loaded, 16)
            sp.dma_start(V("const"), io["const"]).then_inc(const_loaded, 16)

            def params(L):
                for k, name in enumerate(["cols", "b_blk", "c_blk", "w_glu", "lora", "g_up"]):
                    sp.dma_start(V(name), io[name][L]).then_inc(params_loaded, 16)

            params(0)
            def static(u):
                kind, L, g, s = u
                if kind == "win" and g == 0 and L == 1:
                    sp.wait_ge(*en.at("0 ffn pre gained"))
                    sp.wait_ge(*en.at("0 mix used params"))
                    params(1)
                if prev_reader[u]:
                    sp.wait_ge(*en.at(prev_reader[u]))
                if kind == "win":
                    a, b = g * WIN_GROUP * D, min((g + 1) * WIN_GROUP, WT) * D
                    sp.dma_start(slot(s)[:, 0:b - a], io["w_in"][L][:, a:b]).then_inc(slot_filled[s], 16)
                elif kind == "wout":
                    sp.dma_start(slot(s)[:, 0:4096], io["w_out"][L][:, g * 4096:(g + 1) * 4096]
                                 ).then_inc(slot_filled[s], 16)
                else:
                    if s >= 2 and g < 6:
                        sp.wait_ge(*en.at(f"{L} mixing over"))
                    sp.dma_start(slot(s), io["ffn"][g]).then_inc(slot_filled[s], 16)
                if kind == "win" and g == 3:
                    sp.wait_ge(*en.at(f"{L} s5 scratch free"))
                    sp.dma_start(V("bias"), io["bias"][L]).then_inc(bias_loaded, 16)
                if kind == "wout" and g == 1:
                    sp.wait_ge(*en.at(f"{L} gain 0 free")) if L else None
                    sp.dma_start(V("gain"), io["mix_post"][L:L + 1].to_broadcast([P, D])).then_inc(gain_loaded, 16)
                    if L == 1:
                        sp.dma_start(V("router"), io["router"]).then_inc(router_loaded, 16)
                    sp.wait_ge(*en.at(f"{L} mix post gained"))
                    sp.dma_start(V("gain"), io["ffn_post"][L:L + 1].to_broadcast([P, D])).then_inc(gain_loaded, 16)
            for u in uses:
                static(u)
            sp.wait_ge(*en.at("1 mixing over"))
            sp.wait_ge(*en.at("wout 1 1 read"))
            sp.wait_ge(*en.at("passes"))
            total = sp.value_load(passes[:, 16:17], min_val=EXPERTS, max_val=EXPERTS + MORE)
            with sp.Fori(0, total) as i:
                en.enter(i)
                expert = sp.value_load(passes[:, bass.ds(i, 1)], min_val=0, max_val=EXPERTS - 1)
                for j, s in enumerate(CHUNK_SLOT):
                    before = [k for k in range(j) if CHUNK_SLOT[k] == s]
                    if before:
                        sp.wait_ge(*en.at(f"moe down {before[-1]}"))
                    else:
                        last = [k for k in range(CHUNKS) if CHUNK_SLOT[k] == s][-1]
                        sp.wait_ge(*en.at(f"moe down {last}", back=1))
                    sp.dma_start(slot(s), io["moe"][expert * CHUNKS + j]).then_inc(slot_filled[s], 16)
            en.leave(total)
            sp.wait_ge(*en.at("final"))
            sp.dma_start(io["out"].rearrange("(n p) d -> p n d", p=P), x).then_inc(out_stored, 16)
            sp.wait_ge(out_stored, 16)

        @block.tensor
        def _(t):
            pe = Engine("pe", sems, steps)

            def mm(out, lhsT, rhs, start=True, stop=True, **kw):
                return nc.tensor.matmul(out, lhsT, rhs, start=start, stop=stop, **kw)

            reader = {}

            def take(banks, by):
                for b in banks:
                    for r in reader.get(b, ()):
                        t.wait_ge(*pe.at(r))
                    reader[b] = (by,) if isinstance(by, str) else tuple(by)

            def hidden(L, which):
                for c in range(KD):
                    take([c], f"{L} {which} hT {c}")
                    for n in range(NT):
                        t.wait_ge(*pe.at(f"{L} {which} hn {n}"))
                        last = nc.tensor.transpose(ps[:, c, n * P:(n + 1) * P], hn[:, n, c * P:(c + 1) * P], ident)
                    last.then_inc(*pe.step(f"{L} {which} hT psum {c}"))

            def ffn():

                def gate_up(i):
                    j, n = i // NT, i % NT
                    s = CHUNK_SLOT[j]
                    if n == 0:
                        t.wait_ge(*filled("ffn", 0, j, s))
                    if i >= 2:
                        t.wait_ge(*pe.at(f"ffn act {i - 2}"))
                    w = slot(s)[:, 0:KD * 512].rearrange("p (c m) -> p c m", c=KD)
                    for c in range(KD):
                        last = mm(ps[:, i % 2, :], hT[:, c, n * P:(n + 1) * P], w[:, c, :],
                                  start=(c == 0), stop=(c == KD - 1))
                    last.then_inc(*pe.step(f"ffn gate_up {i}"))

                def turn(i):
                    t.wait_ge(*pe.at(f"ffn act {i}"))
                    if i >= 2:
                        t.wait_ge(*pe.at(f"ffn actT {i - 2}"))
                    for k in range(2):
                        last = nc.tensor.transpose(ps[:, 2 + i % 2, k * P:(k + 1) * P],
                                                   act_buf[:, i % 2, k * P:(k + 1) * P], ident)
                    last.then_inc(*pe.step(f"ffn turned {i}"))

                def down(i):
                    j, n = i // NT, i % NT
                    t.wait_ge(*pe.at(f"ffn actT {i}"))
                    w = slot(CHUNK_SLOT[j])[:, KD * 512:].rearrange("p (k m) -> p k m", k=2)
                    for k in range(2):
                        for h in range(2):
                            last = mm(ps[:, 4 + 2 * n + h, :], actT[:, i % 2, k, :], w[:, k, h * 512:(h + 1) * 512],
                                      start=(j == 0 and k == 0), stop=(j == CHUNKS - 1 and k == 1))
                    last.then_inc(*pe.step(f"ffn down {i}"))
                    if n == NT - 1:
                        steps.at[f"ffn 0 {j} read"] = ("pe", pe.count, pe.part)

                for i in range(NT * CHUNKS + 2):
                    if i < NT * CHUNKS:
                        gate_up(i)
                    if 1 <= i <= NT * CHUNKS:
                        turn(i - 1)
                    if i >= 2:
                        down(i - 2)

            def gather(tag):
                for b in range(2):
                    for c in range(4 * b, 4 * b + 4):
                        for n in range(NT):
                            last = mm(ps[:, 6 + b, (c % 4) * P:(c % 4 + 1) * P], hn[:, n, c * P:(c + 1) * P],
                                      disp[:, n, :], start=(n == 0), stop=(n == NT - 1))
                    last.then_inc(*pe.step(f"{tag} gathered {b}"))

            def experts():
                t.wait_ge(*pe.at("disp built"))
                gather("first")
                t.wait_ge(*pe.at("first hTe 1"))
                total = t.value_load(passes[:, 16:17], min_val=EXPERTS, max_val=EXPERTS + MORE)
                with t.Fori(0, total) as i:
                    pe.enter(i)

                    def gate_up(j):
                        s = CHUNK_SLOT[j]
                        k = CHUNK_SLOT[:j + 1].count(s)
                        t.wait_ge(slot_filled[s], 16 * (static_fills[s] + k) + i * (16 * per_fill[s]))
                        t.wait_ge(*(pe.at(f"moe act {j - 2}") if j >= 2 else pe.at(f"moe act {9 + j}", back=1)))
                        w = slot(s)[:, 0:KD * 512].rearrange("p (c m) -> p c m", c=KD)
                        for c in range(KD):
                            last = mm(ps[:, j % 2, :], hTe[:, c, :], w[:, c, :], start=(c == 0), stop=(c == KD - 1))
                        last.then_inc(*pe.step(f"moe gate_up {j}"))

                    def turn(j):
                        t.wait_ge(*pe.at(f"moe act {j}"))
                        t.wait_ge(*(pe.at(f"moe actT {j - 2}") if j >= 2 else pe.at(f"moe actT {9 + j}", back=1)))
                        for k in range(2):
                            last = nc.tensor.transpose(ps[:, 2 + j % 2, k * P:(k + 1) * P],
                                                       act_buf[:, j % 2, k * P:(k + 1) * P], ident)
                        last.then_inc(*pe.step(f"moe turned {j}"))

                    def down(j):
                        t.wait_ge(*pe.at(f"moe actT {j}"))
                        if j == 0:
                            t.wait_ge(*pe.at("moe y taken", back=1))
                        w = slot(CHUNK_SLOT[j])[:, KD * 512:].rearrange("p (k m) -> p k m", k=2)
                        for k in range(2):
                            for h in range(2):
                                last = mm(ps[:, 4 + h, :], actT[:, j % 2, k, :], w[:, k, h * 512:(h + 1) * 512],
                                          start=(j == 0 and k == 0), stop=(j == CHUNKS - 1 and k == 1))
                        last.then_inc(*pe.step(f"moe down {j}"))

                    t.wait_ge(*pe.at("moe hTe 1", back=1))
                    for j in range(CHUNKS + 2):
                        if j < CHUNKS:
                            gate_up(j)
                        if j == 0:
                            t.wait_ge(*pe.at("moe f 3", back=1))
                            for n in range(NT):
                                last = nc.tensor.transpose(ps[:, 6, n * P:(n + 1) * P], gated[:, n, :], ident)
                            last.then_inc(*pe.step("moe gated turned"))
                        if j == CHUNKS:
                            t.wait_ge(*pe.at("moe disp built"))
                            t.wait_ge(*pe.at("moe gatedT"))
                            gather("moe")
                        if 1 <= j <= CHUNKS:
                            turn(j - 1)
                        if j >= 2:
                            down(j - 2)
                    t.wait_ge(*pe.at("moe y taken"))
                    for q in range(4):
                        n, h = q // 2, q % 2
                        t.wait_ge(*pe.at(f"moe hTe {q}" if q < 2 else f"moe f {q - 2}"))
                        mm(ps[:, 6 + h, :], gatedT[:, n, :], y_sb[:, h * 512:(h + 1) * 512]
                           ).then_inc(*pe.step(f"moe scattered {q}"))
                pe.leave(total)

            t.wait_ge(const_loaded, 16)
            for L in range(LAYERS):
                hidden(L, "mix")
                t.wait_ge(params_loaded, 96 * (L + 1))
                for f in range(19):
                    g, s = f // WIN_GROUP, (f // WIN_GROUP) % 2
                    if f % WIN_GROUP == 0:
                        t.wait_ge(*filled("win", L, g, s))
                    if f == 0:
                        for c in range(KD):
                            t.wait_ge(*pe.at(f"{L} mix hT {c}"))
                    take([f % 8], f"{L} proj {f}")
                    w = slot(s)[:, (f % WIN_GROUP) * D:(f % WIN_GROUP + 1) * D].rearrange("p (c m) -> p c m", c=KD)
                    for c in range(KD):
                        last = mm(ps[:, f % 8, 0:S], w[:, c, :], hT[:, c, :], start=(c == 0), stop=(c == KD - 1))
                    last.then_inc(*pe.step(f"{L} proj psum {f}"))
                    if f % WIN_GROUP == WIN_GROUP - 1:
                        steps.at[f"win {L} {g} read"] = ("pe", pe.count, pe.part)
                w = slot(1)[:, D:4 * D].rearrange("p (f c m) -> p f c m", f=3, c=KD)
                for n in range(NT):
                    b = 3 + n
                    take([b], f"{L} vA {n}")
                    for c in range(KD):
                        last = mm(ps[:, b, 0:384].rearrange("p (a b) -> p a b", a=3), hT[:, c, n * P:(n + 1) * P],
                                  w[:, :, c, :], start=(c == 0), stop=(c == KD - 1))
                    last.then_inc(*pe.step(f"{L} vA psum {n}"))
                steps.at[f"win {L} 3 read"] = ("pe", pe.count, pe.part)
                lora, g_up = V("lora"), V("g_up")
                t.wait_ge(*pe.at(f"{L} w_lo tanh"))
                t.wait_ge(*pe.at(f"{L} shifted 9"))
                for q in range(3):
                    take([q], f"{L} decay {q}")
                    mm(ps[:, q, 0:S], lora[0:64, q * P:(q + 1) * P], pm[0:64, 9, :]).then_inc(*pe.step(f"{L} decay psum {q}"))
                for q in range(3):
                    take([3 + q], f"{L} rate {q}")
                    mm(ps[:, 3 + q, 0:S], lora[64:128, q * P:(q + 1) * P], pm[64:128, 9, :]).then_inc(*pe.step(f"{L} rate psum {q}"))
                t.wait_ge(*pe.at(f"{L} g_lo sigmoid"))
                take([6, 7], f"{L} g")
                for q in range(3):
                    last = mm(ps[:, 6 + q // 2, (q % 2) * S:(q % 2 + 1) * S], g_up[:, q * P:(q + 1) * P], pm[:, 10, :],
                              start=True, stop=True)
                last.then_inc(*pe.step(f"{L} g psum"))
                t.wait_ge(*pe.at(f"{L} kk squared"))
                take([0, 1], f"{L} kk sum out")
                sq = V("e2")
                mm(ps[:, 0, :], ones_head, sq[:, 0:512])
                mm(ps[:, 1, 0:256], ones_head, sq[:, 512:768]).then_inc(*pe.step(f"{L} kk sum"))
                t.wait_ge(*pe.at(f"{L} rk"))
                take([2, 3], f"{L} bonus")
                sq = V("e1")
                mm(ps[:, 2, :], ones_head, sq[:, 0:512])
                mm(ps[:, 3, 0:256], ones_head, sq[:, 512:768]).then_inc(*pe.step(f"{L} rk sum"))
                b_blk = V("b_blk", 2, 2, P)
                c_blk = V("c_blk", 2, 8, 32)
                for H in range(2):
                    t.wait_ge(*pe.at(f"{L} proj {11 + H}"))
                    take([4, 5, 6, 7], f"{L} bu {H} read")
                    for i in range(4):
                        r = slice(32 * i, 32 * i + 32)
                        for ri in range(2):
                            last = mm(ps[:, 4 + i, ri * S:(ri + 1) * S], b_blk[r, H, ri, :], uT[r, H, :],
                                      start=True, stop=True, tile_position=(32 * i, 0))
                    last.then_inc(*pe.step(f"{L} bu {H}"))
                    t.wait_ge(*pe.at(f"{L} s5 x {H}"))
                    t.wait_ge(*pe.at(f"{L} c scaled"))
                    take([H], f"{L} y0 {H}")
                    xr, xi = V("z0", 4, S), V("z2", 4, S)
                    for i in range(4):
                        for ri, xx in enumerate((xr, xi)):
                            last = mm(ps[32 * i:32 * i + 32, H, 0:S], c_blk[:, ri, 4 * H + i, :], xx[:, i, :],
                                      start=(ri == 0), stop=(ri == 1))
                    last.then_inc(*pe.step(f"{L} y psum {H}"))
                y = V("z0", 2, S)
                t.wait_ge(*pe.at(f"{L} gelu"))
                take([2], f"{L} glu")
                w_glu = V("w_glu", 2, S)
                for m in range(2):
                    for c in range(2):
                        last = mm(ps[:, 2, m * S:(m + 1) * S], w_glu[:, c, m * P:(m + 1) * P], y[:, c, :],
                                  start=(c == 0), stop=(c == 1))
                last.then_inc(*pe.step(f"{L} glu psum"))
                t.wait_ge(*pe.at(f"{L} s5 squared"))
                take([3], f"{L} s5 var")
                sq = V("z1", 2, S)
                for c in range(2):
                    last = mm(ps[:, 3, 0:S], ones, sq[:, c, :], start=(c == 0), stop=(c == 1))
                last.then_inc(*pe.step(f"{L} s5 sum"))
                for n in range(NT):
                    keys = (n + 1) * P
                    if n == 0:
                        for f in range(13, 19):
                            t.wait_ge(*pe.at(f"{L} proj {f}"))
                    take(range(6), f"{L} scores {n} out")
                    for h in range(6):
                        r, q = slice(64 * (h // 3), 64 * (h // 3) + 64), h % 3
                        last = mm(ps[:, h, 0:keys], qkT[r, q, n * P:(n + 1) * P], qkT[r, 3 + q, 0:keys])
                    last.then_inc(*pe.step(f"{L} scores {n}"))
                    t.wait_ge(*pe.at(f"{L} probs {n}"))
                    PT = V("PT", 3, 4, P)
                    sprob = V("s", 6, keys)
                    k = 0
                    banks = [6, 7, 0] if n else [6, 7]
                    for m in banks:
                        take([m], f"{L} PT {n} {m}")
                        blocks = [(h, jb) for h in range(6) for jb in range(n + 1)][k:k + 4]
                        for i, (h, jb) in enumerate(blocks):
                            last = nc.tensor.transpose(ps[:, m, i * P:(i + 1) * P], sprob[:, h, jb * P:(jb + 1) * P],
                                                       ident)
                        k += 4
                        last.then_inc(*pe.step(f"{L} PT psum {n} {m}"))
                    take([1], f"{L} o {n}")
                    for n2 in range(n + 1):
                        t.wait_ge(*pe.at(f"{L} vA {n2}"))
                    for m in banks:
                        t.wait_ge(*pe.at(f"{L} PT {n} {m}"))
                    for h in range(6):
                        head = 2 * (h % 3) + h // 3
                        for jb in range(n + 1):
                            i = h * (n + 1) + jb
                            last = mm(ps[:, 1, head * 64:head * 64 + 64], PT[:, i // 4, i % 4, :],
                                      vA[:, jb, head * 64:head * 64 + 64], start=(jb == 0), stop=(jb == n))
                    last.then_inc(*pe.step(f"{L} o psum {n}"))
                    t.wait_ge(*pe.at(f"{L} o normed {n}"))
                    take([2], f"{L} oT {n}")
                    aO = V("aO", 2, 384)
                    for q in range(3):
                        last = nc.tensor.transpose(ps[:, 2, q * P:(q + 1) * P], aO[:, n, q * P:(q + 1) * P], ident)
                    last.then_inc(*pe.step(f"{L} oT psum {n}"))
                for k, (src, step) in enumerate([(bh, "bh"), (kh, "kh"), (pm[:, 6:9, :], "shifted 8")]):
                    t.wait_ge(*pe.at(f"{L} {step}"))
                    for n in range(NT):
                        b = (4 + 2 * k + n) % 8
                        take([b], f"{L} natural {k} {n}")
                        for q in range(3):
                            last = nc.tensor.transpose(ps[:, b, q * P:(q + 1) * P], src[:, q, n * P:(n + 1) * P], ident)
                        last.then_inc(*pe.step(f"{L} natural psum {k} {n}"))
                t.wait_ge(*pe.at(f"{L} AR"))
                for n in range(NT):
                    for h in range(6):
                        q, r = h // 2, slice(64 * (h % 2), 64 * (h % 2) + 64)
                        i = n * 6 + h
                        b = i % 4
                        take([b], f"{L} mat {i}")
                        ar = AR[r, q, n, :, :]
                        mm(ps[:, b, 0:256].rearrange("p (a b) -> p a b", a=2), bh[r, q, n * P:(n + 1) * P], ar)
                        mm(ps[:, b, 256:512].rearrange("p (a b) -> p a b", a=2),
                                   kh[r, q, n * P:(n + 1) * P], ar).then_inc(*pe.step(f"{L} mat psum {i}"))
                def six(out_bank, lhs, rhs, step):
                    for h in range(6):
                        last = mm(ps[:, out_bank + h // 4, (h % 4) * P:(h % 4 + 1) * P], lhs(h), rhs(h),
                                  start=True, stop=True)
                    last.then_inc(*pe.step(step))

                for lv in range(LEVELS):
                    for n in range(NT):
                        t.wait_ge(*pe.at(f"{L} Am {lv} {n}"))
                        if lv:
                            t.wait_ge(*pe.at(f"{L} T {lv - 1} {n}"))
                            if lv > 1:
                                t.wait_ge(*pe.at(f"{L} TT {lv - 1} {n}"))
                        take([4 * n, 4 * n + 1], f"{L} Pm {lv} {n}")
                        six(4 * n, lambda h: Am[:, n, h, :], lambda h: T[:, n, h, :] if lv else ident,
                            f"{L} Pm psum {lv} {n}")
                    if lv == 0:
                        continue
                    for n in range(NT):
                        t.wait_ge(*pe.at(f"{L} Pm {lv} {n}"))
                        if lv < LEVELS - 1:
                            take([4 * n + 2, 4 * n + 3], f"{L} T {lv} {n}")
                            six(4 * n + 2, lambda h: TT[:, n, h, :], lambda h: Pm[:, n, h, :], f"{L} T psum {lv} {n}")
                        take([4 * n, 4 * n + 1], f"{L} TT {lv} {n}")
                        six(4 * n, lambda h: Pm[:, n, h, :], lambda h: TT[:, n, h, :], f"{L} TT psum {lv} {n}")
                rhs, sa, st = V("rhs"), V("sa"), V("st", 3, P)
                for n in range(NT):
                    take([2], f"{L} rhs {n}")
                    for q in range(3):
                        if n:
                            t.wait_ge(*pe.at(f"{L} state"))
                            mm(ps[:, 2, q * P:(q + 1) * P], AR[:, q, n, 0, :], st[:, q, :], start=True, stop=False,
                               skip_group_check=True)
                        for h in (2 * q, 2 * q + 1):
                            last = mm(ps[:, 2, h * 64:h * 64 + 64], MAT[:, n * 6 + h, 2, :],
                                      natural[:, 2, n, h * 64:h * 64 + 64], start=(n == 0), stop=True,
                                      skip_group_check=True)
                    last.then_inc(*pe.step(f"{L} rhs psum {n}"))
                    t.wait_ge(*pe.at(f"{L} rhs {n}"))
                    t.wait_ge(*pe.at(f"{L} TT {LEVELS - 1} {n}"))
                    take([3], f"{L} sa {n}")
                    for h in range(6):
                        last = mm(ps[:, 3, h * 64:h * 64 + 64], TT[:, n, h, :], rhs[:, h * 64:h * 64 + 64])
                    last.then_inc(*pe.step(f"{L} sa psum {n}"))
                    t.wait_ge(*pe.at(f"{L} sa {n}"))
                    take([6], f"{L} OT {n}")
                    for q in range(3):
                        if n:
                            mm(ps[:, 6, q * P:(q + 1) * P], st[:, q, :], AR[:, q, n, 1, :], start=True, stop=False,
                               skip_group_check=True)
                        for h in (2 * q, 2 * q + 1):
                            o = ps[64 * (h % 2):64 * (h % 2) + 64, 6, q * P:(q + 1) * P]
                            mm(o, sa[:, h * 64:h * 64 + 64], MAT[:, n * 6 + h, 1, :], start=(n == 0), stop=False,
                               skip_group_check=True)
                            last = mm(o, natural[:, 2, n, h * 64:h * 64 + 64], MAT[:, n * 6 + h, 3, :],
                                      start=False, stop=True, skip_group_check=True)
                    last.then_inc(*pe.step(f"{L} OT psum {n}"))
                    if n == 0:
                        take([7], f"{L} state")
                        for q in range(3):
                            w = slice(q * P, (q + 1) * P)
                            mm(ps[:, 7, w], natural[:, 0, n, w], sa[:, w], start=True, stop=False)
                            last = mm(ps[:, 7, w], natural[:, 1, n, w], natural[:, 2, n, w], start=False, stop=True)
                        last.then_inc(*pe.step(f"{L} state psum"))
                OT, o1, o2 = V("OT"), V("o1"), V("o2")
                t.wait_ge(*pe.at(f"{L} OT 1"))
                take([0, 1], f"{L} centred")
                mm(ps[:, 0, :], ones_head, OT[:, 0:512])
                mm(ps[:, 1, 0:256], ones_head, OT[:, 512:768]).then_inc(*pe.step(f"{L} mean psum"))
                t.wait_ge(*pe.at(f"{L} o squared"))
                take([4, 5], f"{L} gn var")
                mm(ps[:, 4, :], ones_head, o2[:, 0:512])
                mm(ps[:, 5, 0:256], ones_head, o2[:, 512:768]).then_inc(*pe.step(f"{L} var psum"))
                t.wait_ge(*pe.at(f"{L} mixed rwkv"))
                t.wait_ge(*pe.at(f"{L} mixed s5"))
                for n in range(NT):
                    t.wait_ge(*pe.at(f"{L} oT {n}"))
                    take([2 * n, 2 * n + 1], (f"{L} post square {n}", f"{L} post read {n}"))
                    for g in range(2):
                        t.wait_ge(*filled("wout", L, g, g))
                        w = slot(g)[:, 0:4096].rearrange("p (c m) -> p c m", c=4)
                        for h in range(2):
                            for c in range(4):
                                last = mm(ps[:, 2 * n + h, :], hT[:, 4 * g + c, n * P:(n + 1) * P],
                                          w[:, c, h * 512:(h + 1) * 512], start=(g == 0 and c == 0),
                                          stop=(g == 1 and c == 3), skip_group_check=True)
                    last.then_inc(*pe.step(f"{L} out psum {n}"))
                for g in range(2):
                    steps.at[f"wout {L} {g} read"] = ("pe", pe.count, pe.part)
                hidden(L, "ffn")
                for c in range(KD):
                    t.wait_ge(*pe.at(f"{L} ffn hT {c}"))
                if L == 0:
                    ffn()
                    reader = {4: ("ffn y0 taken",), 5: ("ffn y0 taken",), 6: ("ffn y1 taken",), 7: ("ffn y1 taken",),
                              2: ("ffn actT 20",), 3: ("ffn actT 21",), 0: ("ffn act 20",), 1: ("ffn act 21",)}
                else:
                    t.wait_ge(router_loaded, 16)
                    router = V("router", KD, 8)
                    take([0], "logits")
                    for n in range(NT):
                        for c in range(KD):
                            last = mm(ps[:, 0, n * 8:n * 8 + 8], hT[:, c, n * P:(n + 1) * P], router[:, c, :],
                                      start=(c == 0), stop=(c == KD - 1))
                    last.then_inc(*pe.step("logits psum"))
                    sel = V("sel", NT, EXPERTS)
                    before = C("masks4")[:, 0:P]
                    take([1], "ranks")
                    t.wait_ge(*pe.at("sel"))
                    mm(ps[:, 1, 0:8], before, sel[:, 0, :])
                    mm(ps[:, 1, 8:16], before, sel[:, 1, :], stop=False)
                    mm(ps[:, 1, 8:16], ones, sel[:, 0, :], start=False)
                    mm(ps[:, 1, 16:24], ones, sel[:, 0, :], stop=False)
                    mm(ps[:, 1, 16:24], ones, sel[:, 1, :], start=False).then_inc(*pe.step("ranks psum"))
                    experts()

        @block.scalar
        def _(a):
            act = Engine("act", sems, steps)
            fn = nc.scalar.activation

            def rms(L, which):
                if L == 0 and which == "mix":
                    a.wait_ge(x_loaded, 16)
                for n in range(NT):
                    if not (L == 0 and which == "mix"):
                        a.wait_ge(*act.at(f"{L} x ready {which} {n}"))
                    a.wait_ge(*act.last())
                    fn(V("act")[:, 0:D], x[:, n, :], ACT.Square, accum_out=sm("ss", n)).then_inc(*act.step(f"{L} {which} ss {n}"))
                a.wait_ge(*act.at(f"{L} {which} ss mean"))
                a.wait_ge(*act.last())
                fn(sm("sq"), sm("v"), ACT.Sqrt).then_inc(*act.step(f"{L} {which} root"))
                for c in range(KD):
                    a.wait_ge(*act.at(f"{L} {which} hT psum {c}"))
                    a.wait_ge(*act.last())
                    fn(hT[:, c, :], ps[:, c, 0:S], ACT.Copy,
                                scale=col("mix_pre" if which == "mix" else "ffn_pre", c)).then_inc(*act.step(f"{L} {which} hT {c}"))
                if which == "ffn":
                    steps.at[f"{L} ffn pre gained"] = ("act", act.count, act.part)

            def ffn(tag, parts, body=None):
                loop = act.part == "loop"
                for i in range(parts + 1):
                    if i < parts:
                        a.wait_ge(*act.at(f"{tag} gate_up {i}"))
                        if i >= 2:
                            a.wait_ge(*act.at(f"{tag} act {i - 2}"))
                        elif loop:
                            a.wait_ge(*act.at(f"{tag} act {parts - 2 + i}", back=1))
                        a.wait_ge(*act.last())
                        fn(act_buf[:, 2 + i % 2, :], ps[:, i % 2, 0:FC], ACT.Silu).then_inc(*act.step(f"{tag} silu {i}"))
                    if i == 0 and loop:
                        a.wait_ge(*act.at("moe gated turned"))
                        a.wait_ge(*act.at("moe scattered 3", back=1))
                        a.wait_ge(*act.last())
                        fn(gatedT, ps[:, 6, 0:2 * P].rearrange("p (a b) -> p a b", a=2), ACT.Copy
                           ).then_inc(*act.step("moe gatedT"))
                    if i >= 1:
                        k = i - 1
                        a.wait_ge(*act.at(f"{tag} turned {k}"))
                        if k >= 2:
                            a.wait_ge(*act.at(f"{tag} down {k - 2}"))
                        elif loop:
                            a.wait_ge(*act.at(f"{tag} down {parts - 2 + k}", back=1))
                        a.wait_ge(*act.last())
                        fn(actT[:, k % 2, :, :], ps[:, 2 + k % 2, 0:2 * P].rearrange("p (a b) -> p a b", a=2),
                           ACT.Copy).then_inc(*act.step(f"{tag} actT {k}"))

            for L in range(LAYERS):
                a.wait_ge(params_loaded, 96 * (L + 1))
                rms(L, "mix")
                a.wait_ge(*act.last())
                fn(sm("lr", 0, 8), col("log_step"), ACT.Exp).then_inc(*act.step(f"{L} step"))
                a.wait_ge(*act.at(f"{L} half angle"))
                a.wait_ge(*act.last())
                fn(sm("sn", 0, 8), sm("t1", 0, 8), ACT.Sin).then_inc(*act.step())
                a.wait_ge(*act.at(f"{L} half co-angle"))
                a.wait_ge(*act.last())
                fn(sm("cs", 0, 8), sm("t2", 0, 8), ACT.Sin).then_inc(*act.step(f"{L} sines"))
                a.wait_ge(*act.at(f"{L} log r"))
                a.wait_ge(*act.last())
                fn(sm("r", 0, 8), sm("r", 0, 8), ACT.Exp).then_inc(*act.step(f"{L} r"))
                for f in range(0, 19, 2):
                    a.wait_ge(*act.at(f"{L} proj psum {f}"))
                    dst = pT[:, f, 1:257] if f < 11 else uT[:, f - 11, :] if f < 13 else qkT[:, f - 13, :]
                    a.wait_ge(*act.last())
                    fn(dst, ps[:, f % 8, 0:S], ACT.Copy).then_inc(*act.step(f"{L} proj {f}"))
                a.wait_ge(*act.at(f"{L} vA psum 0"))
                a.wait_ge(*act.last())
                fn(vA[:, 0, :], ps[:, 3, 0:384], ACT.Copy).then_inc(*act.step(f"{L} vA 0"))
                a.wait_ge(*act.at(f"{L} shifted 9"))
                a.wait_ge(*act.last())
                fn(pm[0:64, 9, :], pm[0:64, 9, :], ACT.Tanh).then_inc(*act.step(f"{L} w_lo tanh"))
                a.wait_ge(*act.at(f"{L} shifted 10"))
                a.wait_ge(*act.last())
                fn(pm[:, 10, :], pm[:, 10, :], ACT.Tanh, scale=0.5).then_inc(*act.step(f"{L} g_lo tanh"))
                a.wait_ge(*act.at(f"{L} halved"))
                for q in range(3):
                    a.wait_ge(*act.at(f"{L} decay psum {q}"))
                    a.wait_ge(*act.last())
                    fn(V("lw", 3, S)[:, q, :], ps[:, q, 0:S], ACT.Tanh, scale=0.5, bias=sm("half", q)).then_inc(*act.step(f"{L} decay {q}"))
                for q in range(3):
                    a.wait_ge(*act.at(f"{L} rate psum {q}"))
                    a.wait_ge(*act.last())
                    fn(V("a", 3, S)[:, q, :], ps[:, 3 + q, 0:S], ACT.Tanh, scale=0.5, bias=sm("half", 3 + q)).then_inc(*act.step(f"{L} rate {q}"))
                a.wait_ge(*act.at(f"{L} g psum"))
                a.wait_ge(*act.last())
                fn(V("g"), ps[:, 6:8, :].rearrange("p a b -> p (a b)")[:, 0:768], ACT.Copy).then_inc(*act.step(f"{L} g"))
                a.wait_ge(*act.at(f"{L} kk"))
                a.wait_ge(*act.last())
                fn(V("e2"), V("kkn"), ACT.Square).then_inc(*act.step(f"{L} kk squared"))
                a.wait_ge(*act.at(f"{L} kk sum out"))
                a.wait_ge(*act.last())
                fn(V("e2"), V("e2"), ACT.Sqrt).then_inc(*act.step(f"{L} kk root"))
                a.wait_ge(*act.at(f"{L} c centred"))
                a.wait_ge(*act.last())
                fn(V("e1"), V("c"), ACT.Exp).then_inc(*act.step(f"{L} grown"))
                a.wait_ge(*act.at(f"{L} r~"))
                a.wait_ge(*act.last())
                fn(V("e1"), V("lw"), ACT.Exp).then_inc(*act.step(f"{L} grown before"))
                a.wait_ge(*act.at(f"{L} b k"))
                a.wait_ge(*act.last())
                fn(V("e2"), V("c"), ACT.Exp, scale=-1.0).then_inc(*act.step(f"{L} shrunk"))
                a.wait_ge(*act.at(f"{L} dec sum"))
                a.wait_ge(*act.last())
                fn(sm("dec"), sm("dec"), ACT.Exp).then_inc(*act.step(f"{L} dec"))
                a.wait_ge(*act.at(f"{L} gelu in"))
                a.wait_ge(*act.last())
                fn(V("z1")[:, 0:512], V("z1")[:, 0:512], ACT.Tanh, scale=GELU_C).then_inc(*act.step(f"{L} gelu tanh"))
                a.wait_ge(*act.at(f"{L} glu psum"))
                for m in range(2):
                    a.wait_ge(*act.last())
                    fn(V("z2", 2, S)[:, m, :], ps[:, 2, m * S:(m + 1) * S], ACT.Tanh, scale=0.5,
                                bias=sm("half", 6 + m)).then_inc(*act.step(f"{L} glu" if m else None))
                a.wait_ge(*act.at(f"{L} s5 y"))
                a.wait_ge(*act.last())
                fn(V("z1")[:, 0:512], V("z0")[:, 0:512], ACT.Square).then_inc(*act.step(f"{L} s5 squared"))
                a.wait_ge(*act.at(f"{L} s5 var"))
                a.wait_ge(*act.last())
                fn(V("z3")[:, 0:S], V("z3")[:, 0:S], ACT.Sqrt).then_inc(*act.step(f"{L} s5 root"))
                for n in range(NT):
                    keys = (n + 1) * P
                    sprob = V("s", 6, keys)
                    a.wait_ge(*act.at(f"{L} max {n}"))
                    for h in range(6):
                        a.wait_ge(*act.last())
                        fn(sprob[:, h, :], sprob[:, h, :], ACT.Exp, bias=sm("rmax", h),
                                    accum_out=sm("rsum", h)).then_inc(*act.step(f"{L} probs {n}" if h == 5 else None))
                    PT = V("PT", 3, 4, P)
                    for k, m in enumerate([6, 7, 0] if n else [6, 7]):
                        a.wait_ge(*act.at(f"{L} PT psum {n} {m}"))
                        w = 4 if n or k == 0 else 2
                        a.wait_ge(*act.last())
                        fn(PT[:, k, 0:w, :], ps[:, m, 0:w * P].rearrange("p (a b) -> p a b", a=w), ACT.Copy).then_inc(*act.step(f"{L} PT {n} {m}"))
                    a.wait_ge(*act.at(f"{L} o {n}"))
                    aO = V("aO", 2, 384)
                    a.wait_ge(*act.last())
                    fn(V("act")[:, 0:384], aO[:, n, :], ACT.Square, accum_out=sm("ss", n)).then_inc(*act.step(f"{L} o ss {n}"))
                    a.wait_ge(*act.at(f"{L} o ss mean {n}"))
                    a.wait_ge(*act.last())
                    fn(sm("sq", n), sm("v", n), ACT.Sqrt).then_inc(*act.step(f"{L} o root {n}"))
                    a.wait_ge(*act.at(f"{L} oT psum {n}"))
                    for q in range(3):
                        a.wait_ge(*act.last())
                        fn(hT[:, 5 + q, n * P:(n + 1) * P], ps[:, 2, q * P:(q + 1) * P], ACT.Copy,
                                    scale=col("attn_norm", q)).then_inc(*act.step(f"{L} oT {n}" if q == 2 else None))
                a.wait_ge(*act.at(f"{L} E"))
                for k in range(3):
                    for n in range(NT):
                        a.wait_ge(*act.at(f"{L} natural psum {k} {n}"))
                        a.wait_ge(*act.last())
                        fn(natural[:, k, n, :], ps[:, (4 + 2 * k + n) % 8, 0:384], ACT.Copy).then_inc(*act.step(f"{L} natural {k} {n}"))
                for lv in range(LEVELS):
                    for n in range(NT):
                        a.wait_ge(*act.at(f"{L} Pm psum {lv} {n}"))
                        if lv >= 1:
                            a.wait_ge(*act.at(f"{L} TT psum {lv - 1} {n}")) if lv > 1 else None
                        a.wait_ge(*act.last())
                        fn(V("Pm", 2, 768)[:, n, :],
                                    ps[:, 4 * n:4 * n + 2, :].rearrange("p a b -> p (a b)")[:, 0:768], ACT.Copy).then_inc(*act.step(f"{L} Pm {lv} {n}"))
                for n in range(NT):
                    a.wait_ge(*act.at(f"{L} rhs psum {n}"))
                    a.wait_ge(*act.last())
                    fn(V("rhs"), ps[:, 2, 0:384], ACT.Copy).then_inc(*act.step(f"{L} rhs {n}"))
                    a.wait_ge(*act.at(f"{L} sa psum {n}"))
                    a.wait_ge(*act.last())
                    fn(V("sa"), ps[:, 3, 0:384], ACT.Copy).then_inc(*act.step(f"{L} sa {n}"))
                    a.wait_ge(*act.at(f"{L} OT psum {n}"))
                    a.wait_ge(*act.last())
                    fn(V("OT", 3, NT, P)[:, :, n, :], ps[:, 6, 0:384].rearrange("p (a b) -> p a b", a=3),
                                ACT.Copy).then_inc(*act.step(f"{L} OT {n}"))
                a.wait_ge(*act.at(f"{L} centred"))
                a.wait_ge(*act.last())
                fn(V("o2"), V("o1"), ACT.Square).then_inc(*act.step(f"{L} o squared"))
                a.wait_ge(*act.at(f"{L} gn var"))
                a.wait_ge(*act.last())
                fn(V("o2"), V("o2"), ACT.Sqrt).then_inc(*act.step(f"{L} gn root"))
                for n in range(NT):
                    a.wait_ge(*act.at(f"{L} out psum {n}"))
                    a.wait_ge(*act.last())
                    fn(V("natural")[:, 0:D], ps[:, 2 * n:2 * n + 2, :].rearrange("p a b -> p (a b)"),
                                ACT.Square, accum_out=sm("ss", n)).then_inc(*act.step(f"{L} post square {n}"))
                a.wait_ge(*act.at(f"{L} post ss mean"))
                a.wait_ge(*act.last())
                fn(sm("sq"), sm("v"), ACT.Sqrt).then_inc(*act.step(f"{L} post root"))
                rms(L, "ffn")
                if L == 0:
                    ffn("ffn", NT * CHUNKS)
                else:
                    a.wait_ge(*act.at("gate in"))
                    a.wait_ge(*act.last())
                    fn(sm("g1"), sm("g1"), ACT.Exp).then_inc(*act.step("gate exp"))
                    a.wait_ge(*act.at("lg shifted"))
                    a.wait_ge(*act.last())
                    fn(sm("lg"), sm("lg"), ACT.Exp).then_inc(*act.step("lg exp"))
                    a.wait_ge(*act.at("passes"))
                    total = a.value_load(passes[:, 16:17], min_val=EXPERTS, max_val=EXPERTS + MORE)
                    with a.Fori(0, total) as i:
                        act.enter(i)
                        ffn("moe", CHUNKS)
                        a.wait_ge(*act.at("moe down 10"))
                        a.wait_ge(*act.at("moe scattered 3", back=1))
                        a.wait_ge(*act.last())
                        fn(y_sb, ps[:, 4:6, :].rearrange("p a b -> p (a b)"), ACT.Copy
                           ).then_inc(*act.step("moe y taken"))
                    act.leave(total)
                a.wait_ge(*act.at(f"{L} f ready"))
                for n in range(NT):
                    a.wait_ge(*act.last())
                    fn(V("natural")[:, 0:D], (hn, ffn_sum)[L][:, n, :], ACT.Square, accum_out=sm("ss", n)).then_inc(*act.step(f"{L} fpost square {n}"))
                a.wait_ge(*act.at(f"{L} fpost ss mean"))
                a.wait_ge(*act.last())
                fn(sm("sq"), sm("v"), ACT.Sqrt).then_inc(*act.step(f"{L} fpost root"))

        @block.vector
        def _(v):
            dve = Engine("dve", sems, steps)
            ve = nc.vector

            def tt(out, a0, a1, op, step=None):
                v.wait_ge(*dve.last())
                ve.tensor_tensor(out, a0, a1, op).then_inc(*dve.step(step))

            def ts(out, a0, s1, s2, op0, op1=None, step=None):
                v.wait_ge(*dve.last())
                (ve.tensor_scalar(out, a0, s1, s2, op0, op1) if op1 is not None
                         else ve.tensor_scalar(out, a0, s1, None, op0)).then_inc(*dve.step(step))

            def stt(out, a0, s, a1, op0, op1, step=None):
                v.wait_ge(*dve.last())
                ve.scalar_tensor_tensor(out=out, in0=a0, scalar=s, in1=a1, op0=op0, op1=op1).then_inc(*dve.step(step))

            def rstd(L, what, ssname, rootname, width, n=None):
                for s in ssname:
                    v.wait_ge(*dve.at(s))
                s = (lambda k: sm(k)) if n is None else (lambda k: sm(k, n))
                ts(s("v"), s("ss"), 1.0 / width, EPS, ALU.mult, ALU.add, what)
                v.wait_ge(*dve.at(rootname))
                v.wait_ge(*dve.last())
                ve.reciprocal(s("rstd"), s("sq")).then_inc(*dve.step())

            def normed(L, which):
                rstd(L, f"{L} {which} ss mean", [f"{L} {which} ss {n}" for n in range(NT)], f"{L} {which} root", D)
                for n in range(NT):
                    ts(hn[:, n, :], x[:, n, :], sm("rstd", n), None, ALU.mult, None, f"{L} {which} hn {n}")

            def table(L):
                th, st, r = sm("theta", 0, 8), sm("lr", 0, 8), sm("r", 0, 8)
                sn, cs, t0, t1, t2 = (sm(k, 0, 8) for k in ("sn", "cs", "t0", "t1", "t2"))
                v.wait_ge(*dve.at(f"{L} step"))
                tt(th, col("a_im"), st, ALU.mult)
                ts(t0, th, 1.0 / TWO_PI, ROUND, ALU.mult, ALU.add)
                ts(t0, t0, ROUND, None, ALU.subtract)
                stt(th, t0, -TWO_PI_HI, th, ALU.mult, ALU.add)
                stt(th, t0, -TWO_PI_LO, th, ALU.mult, ALU.add)
                ts(t1, th, 0.5, None, ALU.mult, None, f"{L} half angle")
                ts(t2, t1, -1.0, None, ALU.mult)
                tt(t2, t1, t2, ALU.max)
                ts(t2, t2, -1.0, TWO_PI / 4, ALU.mult, ALU.add, f"{L} half co-angle")
                ts(t0, col("a_re"), -1e-4, None, ALU.min)
                tt(r, t0, st, ALU.mult, f"{L} log r")
                v.wait_ge(*dve.at(f"{L} sines"))
                tt(t1, sn, sn, ALU.mult)
                stt(sn, sn, 2.0, cs, ALU.mult, ALU.mult)
                ts(cs, t1, -2.0, 1.0, ALU.mult, ALU.add)
                v.wait_ge(*dve.at(f"{L} r"))
                are, aim, fr, fi, u0, u1 = t0, col("a_im"), sm("fr"), sm("fi"), sm("u0"), sm("u1")
                tt(u0, r, cs, ALU.mult)
                ts(u0, u0, 1.0, None, ALU.subtract)
                tt(u1, r, sn, ALU.mult)
                tt(fr, u0, are, ALU.mult)
                tt(t1, u1, aim, ALU.mult)
                tt(fr, fr, t1, ALU.add)
                tt(fi, u1, are, ALU.mult)
                tt(t1, u0, aim, ALU.mult)
                tt(fi, fi, t1, ALU.subtract)
                tt(t1, are, are, ALU.mult)
                tt(t2, aim, aim, ALU.mult)
                tt(t1, t1, t2, ALU.add)
                v.wait_ge(*dve.last())
                ve.reciprocal(t1, t1).then_inc(*dve.step())
                tt(fr, fr, t1, ALU.mult)
                tt(fi, fi, t1, ALU.mult)
                cb = V("c_blk", 2, 8, 32)
                s0, s1, s2 = (V("natural")[:, k * 256:(k + 1) * 256].rearrange("p (a b) -> p a b", a=8)
                              for k in range(3))
                tt(s0, cb[:, 0], bc(fi, 32), ALU.mult)
                tt(s1, cb[:, 1], bc(fi, 32), ALU.mult)
                tt(s2, cb[:, 0], bc(fr, 32), ALU.mult)
                tt(cb[:, 0], s2, s1, ALU.subtract)
                tt(s1, cb[:, 1], bc(fr, 32), ALU.mult)
                stt(cb[:, 1], s1, -1.0, s0, ALU.mult, ALU.subtract, f"{L} c scaled")

            def ffn(tag, parts, after=lambda i: None):
                loop = dve.part == "loop"
                for i in range(parts):
                    v.wait_ge(*dve.at(f"{tag} silu {i}"))
                    if i >= 2:
                        v.wait_ge(*dve.at(f"{tag} turned {i - 2}"))
                    elif loop:
                        v.wait_ge(*dve.at(f"{tag} turned {parts - 2 + i}", back=1))
                    tt(act_buf[:, i % 2, :], act_buf[:, 2 + i % 2, :], ps[:, i % 2, FC:2 * FC], ALU.mult,
                       f"{tag} act {i}")
                    after(i)

            def dispatch(i, name):
                for n in range(NT):
                    at = slot_of[:, n, bass.ds(i, 1)] if dve.part == "loop" else slot_of[:, n, i:i + 1]
                    gate = gate_of[:, n, bass.ds(i, 1)] if dve.part == "loop" else gate_of[:, n, i:i + 1]
                    ts(disp[:, n, :], C("iota"), at, None, ALU.is_equal, None)
                    ts(gated[:, n, :], C("iota"), at, gate, ALU.is_equal, ALU.mult, name)

            def gathered(tag):
                for b in range(2):
                    v.wait_ge(*dve.at(f"{tag} gathered {b}"))
                    tt(hTe[:, 4 * b:4 * b + 4, :], ps[:, 6 + b, :].rearrange("p (c t) -> p c t", c=4),
                       bc(col("ffn_pre")[:, 4 * b:4 * b + 4], P), ALU.mult, f"{tag} hTe {b}")

            def route():
                v.wait_ge(*dve.at("logits psum"))
                lg, lg3 = sm("lg"), sm("lg").rearrange("p (n e) -> p n e", n=NT)
                v.wait_ge(*dve.last())
                ve.tensor_copy(lg, ps[:, 0, 0:16]).then_inc(*dve.step("logits"))
                for n in range(NT):
                    v.wait_ge(*dve.last())
                    ve.max(sm("m8", 8 * n, 8), sm("lg", 8 * n, 8)).then_inc(*dve.step())
                m8 = sm("m8").rearrange("p (n e) -> p n e", n=NT)
                second = m8[:, :, 1:2].to_broadcast([P, NT, EXPERTS])
                sel, eq, cum, prod = (V(k, NT, EXPERTS) for k in ("sel", "eq", "cum", "prod"))
                pick = V("pick")
                tt(sel, lg3, second, ALU.is_gt)
                tt(eq, lg3, second, ALU.is_equal)
                v.wait_ge(*dve.last())
                ve.tensor_reduce(pick, sel, AX.X, ALU.add).then_inc(*dve.step())
                for n in range(NT):
                    v.wait_ge(*dve.last())
                    ve.tensor_tensor_scan(cum[:, n, :], ones[:, 0:8], eq[:, n, :], 0.0, ALU.mult, ALU.add
                                          ).then_inc(*dve.step())
                tt(cum, cum, bc(pick, EXPERTS), ALU.add)
                stt(eq, cum, 2.0, eq, ALU.is_le, ALU.mult)
                tt(sel, sel, eq, ALU.add, "sel")
                tt(sm("g1"), m8[:, :, 1], m8[:, :, 0], ALU.subtract, "gate in")
                tt(lg3, lg3, m8[:, :, 0:1].to_broadcast([P, NT, EXPERTS]), ALU.subtract, "lg shifted")
                v.wait_ge(*dve.at("gate exp"))
                ts(sm("g1"), sm("g1"), 1.0, None, ALU.add)
                v.wait_ge(*dve.last())
                ve.reciprocal(sm("g1"), sm("g1")).then_inc(*dve.step())
                v.wait_ge(*dve.at("lg exp"))
                tt(lg3, lg3, bc(sm("g1"), EXPERTS), ALU.mult)
                tt(lg3, lg3, sel, ALU.mult)
                v.wait_ge(*dve.at("ranks psum"))
                v.wait_ge(*dve.last())
                ve.tensor_copy(V("rank"), ps[:, 1, 0:24]).then_inc(*dve.step("ranks"))
                rank, count = V("rank")[:, 0:16].rearrange("p (n e) -> p n e", n=NT), V("rank")[:, 16:24]
                v.wait_ge(*dve.last())
                ve.memset(V("slot_of"), -1.0).then_inc(*dve.step())
                v.wait_ge(*dve.last())
                ve.memset(V("gate_of"), 0.0).then_inc(*dve.step())
                stt(rank, rank, 1.0, sel, ALU.add, ALU.mult)
                ts(slot_of[:, :, 0:EXPERTS], rank, 1.0, None, ALU.subtract)
                v.wait_ge(*dve.last())
                ve.tensor_copy(gate_of[:, :, 0:EXPERTS], lg3).then_inc(*dve.step())
                over, order, onehot = V("over"), V("order"), V("onehot")
                iota8 = C("iota")[:, 0:EXPERTS]
                ids, total = sm("m8"), sm("total")
                ts(over, count, float(P), None, ALU.is_gt)
                v.wait_ge(*dve.last())
                ve.tensor_tensor_scan(order, ones[:, 0:8], over, 0.0, ALU.mult, ALU.add).then_inc(*dve.step())
                ts(total, order[:, 7:8], float(EXPERTS), None, ALU.add)
                v.wait_ge(*dve.last())
                ve.memset(ids, 0.0).then_inc(*dve.step())
                v.wait_ge(*dve.last())
                ve.tensor_copy(ids[:, 0:EXPERTS], iota8).then_inc(*dve.step())
                for m in range(MORE):
                    stt(onehot, order, float(m + 1), over, ALU.is_equal, ALU.mult)
                    tt(V("prod")[:, 0:8], onehot, iota8, ALU.mult)
                    v.wait_ge(*dve.last())
                    ve.tensor_reduce(ids[:, EXPERTS + m:EXPERTS + m + 1], V("prod")[:, 0:8], AX.X, ALU.add
                                     ).then_inc(*dve.step())
                    hot = onehot.unsqueeze(1).to_broadcast([P, NT, EXPERTS])
                    stt(prod, rank, float(P), hot, ALU.subtract, ALU.mult)
                    v.wait_ge(*dve.last())
                    ve.tensor_reduce(pick, prod, AX.X, ALU.add).then_inc(*dve.step())
                    ts(slot_of[:, :, EXPERTS + m], pick, 1.0, None, ALU.subtract)
                    tt(prod, gate_of[:, :, 0:EXPERTS], hot, ALU.mult)
                    v.wait_ge(*dve.last())
                    ve.tensor_reduce(gate_of[:, :, EXPERTS + m], prod, AX.X, ALU.add).then_inc(*dve.step())
                v.wait_ge(*dve.last())
                ve.tensor_copy(passes[:, 0:16], ids[0:1, :]).then_inc(*dve.step())
                v.wait_ge(*dve.last())
                ve.tensor_copy(passes[:, 16:17], total[0:1, :]).then_inc(*dve.step("passes"))

            def experts():
                v.wait_ge(*dve.last())
                ve.memset(V("ffn_sum"), 0.0).then_inc(*dve.step())
                dispatch(0, "disp built")
                gathered("first")
                total = v.value_load(passes[:, 16:17], min_val=EXPERTS, max_val=EXPERTS + MORE)
                with v.Fori(0, total) as i:
                    dve.enter(i)

                    def after(j):
                        if j == 1:
                            v.wait_ge(*dve.at("moe gated turned"))
                            dispatch(i + 1, "moe disp built")

                    ffn("moe", CHUNKS, after)
                    gathered("moe")
                    for q in range(4):
                        n, h = q // 2, q % 2
                        v.wait_ge(*dve.at(f"moe scattered {q}"))
                        fq = ffn_sum[:, n, h * 512:(h + 1) * 512]
                        tt(fq, fq, ps[:, 6 + h, :], ALU.add, f"moe f {q}")
                dve.leave(total)

            for L in range(LAYERS):
                normed(L, "mix")
                v.wait_ge(params_loaded, 96 * (L + 1))
                table(L)
                v.wait_ge(*dve.last())
                ve.memset(pT[:, :, 0:1], 0.0).then_inc(*dve.step())
                for f in range(1, 19, 2):
                    v.wait_ge(*dve.at(f"{L} proj psum {f}"))
                    dst = pT[:, f, 1:257] if f < 11 else uT[:, f - 11, :] if f < 13 else qkT[:, f - 13, :]
                    v.wait_ge(*dve.last())
                    ve.tensor_copy(dst, ps[:, f % 8, 0:S]).then_inc(*dve.step(f"{L} proj {f}"))
                v.wait_ge(*dve.at(f"{L} vA psum 1"))
                v.wait_ge(*dve.last())
                ve.tensor_copy(vA[:, 1, :], ps[:, 4, 0:384]).then_inc(*dve.step(f"{L} vA 1"))
                for f in (9, 10, 3, 4, 5, 0, 1, 2, 6, 7, 8):
                    v.wait_ge(*dve.at(f"{L} proj {f}"))
                    tt(pm[:, f, :], pT[:, f, 0:256], pT[:, f, 1:257], ALU.subtract)
                    stt(pm[:, f, :], pm[:, f, :], col("mu", f), pT[:, f, 1:257], ALU.mult, ALU.add,
                        f"{L} shifted {f}")
                ts(sm("half", 0, 3), col("w0"), 0.5, None, ALU.mult)
                ts(sm("half", 3, 3), col("a0"), 0.5, None, ALU.mult)
                ts(sm("half", 6, 2), col("b_glu"), 0.5, None, ALU.mult, None, f"{L} halved")
                v.wait_ge(*dve.at(f"{L} g_lo tanh"))
                ts(pm[:, 10, :], pm[:, 10, :], 0.5, 0.5, ALU.mult, ALU.add, f"{L} g_lo sigmoid")
                kkn, e1, e2, a_, lw, c = (V(k, 3, S) for k in ("kkn", "e1", "e2", "a", "lw", "c"))
                flat = {k: V(k) for k in ("kkn", "e1", "e2", "a", "lw", "c", "kh", "bh")}
                r_, k_, v_ = pm[:, 0:3, :], pm[:, 3:6, :], pm[:, 6:9, :]
                for q in range(3):
                    ts(kkn[:, q, :], k_[:, q, :], col("k_k", q), None, ALU.mult, None, f"{L} kk")
                v.wait_ge(*dve.at(f"{L} kk sum"))
                ts(flat["e2"], ps[:, 0:2, :].rearrange("p a b -> p (a b)")[:, 0:768], 1e-24, None, ALU.max, None,
                   f"{L} kk sum out")
                v.wait_ge(*dve.at(f"{L} kk root"))
                v.wait_ge(*dve.last())
                ve.reciprocal(flat["e2"], flat["e2"]).then_inc(*dve.step())
                tt(flat["kkn"], flat["kkn"], flat["e2"], ALU.mult)
                v.wait_ge(*dve.at(f"{L} rate 2"))
                ts(flat["a"], flat["a"], 0.5, 0.5, ALU.mult, ALU.add)
                v.wait_ge(*dve.at(f"{L} decay 2"))
                ts(flat["lw"], flat["lw"], 0.5 * NEG_HALF_EXP, 0.5 * NEG_HALF_EXP, ALU.mult, ALU.add)
                for q in range(3):
                    v.wait_ge(*dve.last())
                    ve.tensor_tensor_scan(c[:, q, :], C("scan"), lw[:, q, :], 0.0, ALU.mult, ALU.add).then_inc(*dve.step())
                c4 = V("c", 3, NT, P)
                mid = c4[:, :, :, 63:64]
                v.wait_ge(*dve.last())
                ve.tensor_copy(sm("cmid").rearrange("p (a b c) -> p a b c", a=3, b=2), mid).then_inc(*dve.step())
                cm = sm("cmid").rearrange("p (a b) -> p a b", a=3)
                tt(sm("dec"), c4[:, :, 0, 127], cm[:, :, 0], ALU.subtract)
                tt(sm("dec"), sm("dec"), cm[:, :, 1], ALU.add, f"{L} dec sum")
                tt(V("c", 6, P), V("c", 6, P), bc(sm("cmid"), P), ALU.subtract, f"{L} c centred")
                tt(flat["lw"], flat["c"], flat["lw"], ALU.subtract)
                for q in range(3):
                    ts(bh[:, q, :], a_[:, q, :], 1.0, col("k_a", q), ALU.subtract, ALU.mult)
                stt(k_, bh, 1.0, k_, ALU.add, ALU.mult)
                v.wait_ge(*dve.at(f"{L} grown"))
                for q in range(3):
                    tt(AR[:, q, :, 1, :], r_[:, q, :].rearrange("p (n s) -> p n s", n=NT),
                       e1[:, q, :].rearrange("p (n s) -> p n s", n=NT), ALU.mult, f"{L} r~")
                v.wait_ge(*dve.at(f"{L} grown before"))
                for q in range(3):
                    stt(AR[:, q, :, 0, :], kkn[:, q, :].rearrange("p (n s) -> p n s", n=NT), -1.0,
                        e1[:, q, :].rearrange("p (n s) -> p n s", n=NT), ALU.mult, ALU.mult, f"{L} AR")
                for q in range(3):
                    stt(e1[:, q, :], r_[:, q, :], col("r_k", q), k_[:, q, :], ALU.mult, ALU.mult, f"{L} rk")
                tt(flat["bh"], flat["kkn"], flat["a"], ALU.mult, f"{L} b k")
                v.wait_ge(*dve.at(f"{L} shrunk"))
                tt(flat["bh"], flat["bh"], flat["e2"], ALU.mult, f"{L} bh")
                tt(kh, k_, e2, ALU.mult, f"{L} kh")
                v.wait_ge(*dve.at(f"{L} rk sum"))
                tt(V("bonus"), ps[:, 2:4, :].rearrange("p a b -> p (a b)")[:, 0:768],
                   pm[:, 6:9, :].rearrange("p a b -> p (a b)"), ALU.mult, f"{L} bonus")
                v.wait_ge(*dve.at(f"{L} E"))
                for H in range(2):
                    Er, Ei = E[:, 0, 4 * H:4 * H + 4, :], E[:, 1, 4 * H:4 * H + 4, :]
                    z = [V(f"z{i}", 4, S) for i in range(5)]
                    v.wait_ge(*dve.at(f"{L} bu {H}"))
                    if H:
                        v.wait_ge(*dve.at(f"{L} y psum 0"))
                    br, bi = ps[:, 4:8, 0:S], ps[:, 4:8, S:2 * S]
                    tt(z[0], br, Er, ALU.mult)
                    tt(z[1], bi, Ei, ALU.mult)
                    tt(z[2], bi, Er, ALU.mult)
                    tt(z[3], br, Ei, ALU.mult, f"{L} bu {H} read")
                    tt(z[0], z[0], z[1], ALU.add)
                    tt(z[2], z[2], z[3], ALU.subtract)
                    for i in range(4):
                        rr = sm("r", 4 * H + i).to_broadcast([P, S])
                        v.wait_ge(*dve.last())
                        ve.tensor_tensor_scan(z[1][:, i, :], rr, z[0][:, i, :], 0.0, ALU.mult, ALU.add).then_inc(*dve.step())
                        v.wait_ge(*dve.last())
                        ve.tensor_tensor_scan(z[3][:, i, :], rr, z[2][:, i, :], 0.0, ALU.mult, ALU.add).then_inc(*dve.step())
                    tt(z[0], z[1], Er, ALU.mult)
                    tt(z[2], z[3], Ei, ALU.mult)
                    tt(z[0], z[0], z[2], ALU.subtract)
                    tt(z[2], z[3], Er, ALU.mult)
                    tt(z[4], z[1], Ei, ALU.mult)
                    tt(z[2], z[2], z[4], ALU.add, f"{L} s5 x {H}")
                    v.wait_ge(*dve.at(f"{L} y psum {H}"))
                    stt(uT[:, H, :], uT[:, H, :], col("s5_d", H), ps[:, H, 0:S], ALU.mult, ALU.add, f"{L} y0 {H}")
                y, w1, w2 = V("z0")[:, 0:512], V("z1")[:, 0:512], V("z2")[:, 0:512]
                u = V("uT")
                tt(w1, u, u, ALU.mult)
                ts(w1, w1, 0.044715, 1.0, ALU.mult, ALU.add)
                tt(w1, w1, u, ALU.mult, f"{L} gelu in")
                v.wait_ge(*dve.at(f"{L} gelu tanh"))
                stt(y, w1, 1.0, u, ALU.add, ALU.mult)
                ts(y, y, 0.5, None, ALU.mult, None, f"{L} gelu")
                v.wait_ge(*dve.at(f"{L} glu"))
                ts(w2, w2, 0.5, 0.5, ALU.mult, ALU.add)
                tt(y, y, w2, ALU.mult, f"{L} s5 y")
                v.wait_ge(*dve.at(f"{L} s5 sum"))
                ts(V("z3")[:, 0:S], ps[:, 3, 0:S], 1.0 / S, EPS, ALU.mult, ALU.add, f"{L} s5 var")
                v.wait_ge(*dve.at(f"{L} s5 root"))
                v.wait_ge(*dve.last())
                ve.reciprocal(V("z3")[:, 0:S], V("z3")[:, 0:S]).then_inc(*dve.step())
                for m in range(2):
                    stt(hT[:, 3 + m, :], V("z0", 2, S)[:, m, :], col("s5_norm", m), V("z3")[:, 0:S], ALU.mult,
                        ALU.mult, f"{L} mixed s5")
                steps.at[f"{L} s5 scratch free"] = ("dve", dve.count, dve.part)
                bias = V("bias", 6, 384)
                v.wait_ge(bias_loaded, 16 * (L + 1))
                for n in range(NT):
                    keys = (n + 1) * P
                    sprob = V("s", 6, keys)
                    v.wait_ge(*dve.at(f"{L} scores {n}"))
                    if n:
                        v.wait_ge(*dve.at(f"{L} PT psum 0 7"))
                    stt(sprob, ps[:, 0:6, 0:keys], 0.125, bias[:, :, (1 - n) * P:(1 - n) * P + keys],
                        ALU.mult, ALU.add, f"{L} scores {n} out")
                    v.wait_ge(*dve.last())
                    ve.memset(sprob[0:64, :, keys - 64:keys], -3.0e38).then_inc(*dve.step())
                    if n:
                        v.wait_ge(*dve.at(f"{L} probs 0"))
                    v.wait_ge(*dve.last())
                    ve.tensor_reduce(sm("rmax", 0, 6), sprob, AX.X, ALU.max).then_inc(*dve.step())
                    ts(sm("rmax", 0, 6), sm("rmax", 0, 6), -1.0, None, ALU.mult, None, f"{L} max {n}")
                    v.wait_ge(*dve.at(f"{L} probs {n}"))
                    v.wait_ge(*dve.last())
                    ve.reciprocal(sm("rinv", 0, 6), sm("rsum", 0, 6)).then_inc(*dve.step())
                    v.wait_ge(*dve.at(f"{L} o psum {n}"))
                    aO = V("aO", 2, 3, 2, 64)
                    for par in range(2):
                        tt(aO[:, n, :, par, :], ps[:, 1, 0:384].rearrange("p (a b c) -> p a b c", a=3, b=2)[:, :, par, :],
                           bc(sm("rinv", 3 * par, 3), 64), ALU.mult, f"{L} o {n}")
                    rstd(L, f"{L} o ss mean {n}", [f"{L} o ss {n}"], f"{L} o root {n}", 384, n)
                    ts(V("aO", 2, 384)[:, n, :], V("aO", 2, 384)[:, n, :], sm("rstd", n), None, ALU.mult, None,
                       f"{L} o normed {n}")
                for b in range(3):
                    for n in range(NT):
                        v.wait_ge(*dve.at(f"{L} natural psum {b} {n}"))
                for i in range(12):
                    v.wait_ge(*dve.at(f"{L} mat psum {i}"))
                    tt(MAT[:, i].rearrange("p a b -> p (a b)"), ps[:, i % 4, :], C("masks4"), ALU.mult, f"{L} mat {i}")
                for n in range(NT):
                    a_t = MAT[:, n * 6:n * 6 + 6, 0, :]
                    tt(Am[:, n], a_t, C("level")[:, 0:P].unsqueeze(1).to_broadcast([P, 6, P]), ALU.mult,
                       f"{L} Am 0 {n}")
                    tt(TT[:, n], Am[:, n], ident.unsqueeze(1).to_broadcast([P, 6, P]), ALU.add)
                for n in range(NT):
                    v.wait_ge(*dve.at(f"{L} Pm 0 {n}"))
                    tt(T[:, n], Pm[:, n], ident.unsqueeze(1).to_broadcast([P, 6, P]), ALU.add, f"{L} T 0 {n}")
                for lv in range(1, LEVELS):
                    for n in range(NT):
                        if lv < LEVELS - 1:
                            v.wait_ge(*dve.at(f"{L} T psum {lv} {n}"))
                            v.wait_ge(*dve.at(f"{L} Pm psum {lv} {n}"))
                            tt(V("T", 2, 768)[:, n], V("T", 2, 768)[:, n],
                               ps[:, 4 * n + 2:4 * n + 4, :].rearrange("p a b -> p (a b)")[:, 0:768], ALU.add,
                               f"{L} T {lv} {n}")
                        v.wait_ge(*dve.at(f"{L} TT psum {lv} {n}"))
                        tt(V("TT", 2, 768)[:, n], V("TT", 2, 768)[:, n],
                           ps[:, 4 * n:4 * n + 2, :].rearrange("p a b -> p (a b)")[:, 0:768], ALU.add,
                           f"{L} TT {lv} {n}")
                v.wait_ge(*dve.at(f"{L} state psum"))
                for q in range(3):
                    stt(V("st", 3, P)[:, q, :], ps[:, 7, q * P:(q + 1) * P], sm("dec", q), ones_head, ALU.mult,
                        ALU.mult, f"{L} state")
                OT, o1, o2 = V("OT"), V("o1"), V("o2")
                v.wait_ge(*dve.at(f"{L} mean psum"))
                v.wait_ge(*dve.at(f"{L} OT 1"))
                stt(o1, ps[:, 0:2, :].rearrange("p a b -> p (a b)")[:, 0:768], -1.0 / 64, OT, ALU.mult, ALU.add,
                    f"{L} centred")
                v.wait_ge(*dve.at(f"{L} var psum"))
                ts(o2, ps[:, 4:6, :].rearrange("p a b -> p (a b)")[:, 0:768], 1.0 / 64, GN_EPS, ALU.mult, ALU.add,
                   f"{L} gn var")
                v.wait_ge(*dve.at(f"{L} gn root"))
                v.wait_ge(*dve.last())
                ve.reciprocal(o2, o2).then_inc(*dve.step())
                tt(o1, o1, o2, ALU.mult)
                for q in range(3):
                    oq = V("o1", 3, S)[:, q, :]
                    ts(oq, oq, col("ln_w", q), col("ln_b", q), ALU.mult, ALU.add)
                tt(o1, o1, V("bonus"), ALU.add)
                v.wait_ge(*dve.at(f"{L} g"))
                tt(hT[:, 0:3, :].rearrange("p a b -> p (a b)"), o1, V("g"), ALU.mult, f"{L} mixed rwkv")
                steps.at[f"{L} mixing over"] = ("dve", dve.count, dve.part)
                steps.at[f"{L} mix used params"] = ("dve", dve.count, dve.part)
                rstd(L, f"{L} post ss mean", [f"{L} post square {n}" for n in range(NT)], f"{L} post root", D)
                v.wait_ge(gain_loaded, 16 + 32 * L)
                tmp = V("natural")[:, 0:D]
                for n in range(NT):
                    stt(tmp, ps[:, 2 * n:2 * n + 2, :].rearrange("p a b -> p (a b)"), sm("rstd", n), V("gain"),
                        ALU.mult, ALU.mult, f"{L} post read {n}")
                    if n == NT - 1:
                        steps.at[f"{L} mix post gained"] = ("dve", dve.count, dve.part)
                    tt(x[:, n, :], x[:, n, :], tmp, ALU.add, f"{L} x ready ffn {n}")
                steps.at["final"] = ("dve", dve.count, dve.part)
                normed(L, "ffn")
                if L == 0:
                    ffn("ffn", NT * CHUNKS)
                    for n in range(NT):
                        v.wait_ge(*dve.at(f"ffn down {20 + n}"))
                        v.wait_ge(*dve.last())
                        ve.tensor_copy(hn[:, n, :], ps[:, 4 + 2 * n:6 + 2 * n, :].rearrange("p a b -> p (a b)")
                                       ).then_inc(*dve.step(f"ffn y{n} taken"))
                    steps.at["0 f ready"] = ("dve", dve.count, dve.part)
                else:
                    route()
                    experts()
                    steps.at["1 f ready"] = ("dve", dve.count, "after")
                rstd(L, f"{L} fpost ss mean", [f"{L} fpost square {n}" for n in range(NT)], f"{L} fpost root", D)
                v.wait_ge(gain_loaded, 32 + 32 * L)
                tmp = V("natural")[:, 0:D]
                for n in range(NT):
                    stt(tmp, (hn, ffn_sum)[L][:, n, :], sm("rstd", n), V("gain"), ALU.mult, ALU.mult)
                    tt(x[:, n, :], x[:, n, :], tmp, ALU.add, f"{L + 1} x ready mix {n}")
                steps.at[f"{L + 1} gain 0 free"] = ("dve", dve.count, dve.part)
                steps.at["final"] = ("dve", dve.count, dve.part)

        @block.gpsimd
        def _(g):
            pool = Engine("pool", sems, steps)

            def tt(out, a0, a1, op, step=None):
                g.wait_ge(*pool.last())
                nc.gpsimd.tensor_tensor(out, a0, a1, op).then_inc(*pool.step(step))

            for L in range(LAYERS):
                g.wait_ge(*pool.at(f"{L} c scaled"))
                g.wait_ge(*pool.last())
                nc.gpsimd.memset(E[:, 0, :, 0:1], 1.0).then_inc(*pool.step())
                g.wait_ge(*pool.last())
                nc.gpsimd.memset(E[:, 1, :, 0:1], 0.0).then_inc(*pool.step())
                g.wait_ge(*pool.last())
                nc.gpsimd.tensor_copy(E[:, 0, :, 1], sm("cs", 0, 8)).then_inc(*pool.step())
                g.wait_ge(*pool.last())
                nc.gpsimd.tensor_copy(E[:, 1, :, 1], sm("sn", 0, 8)).then_inc(*pool.step(f"{L} E"))
                m = 2
                w0, w1 = V("natural")[:, 0:1016].rearrange("p (a b) -> p a b", a=8), \
                    V("natural")[:, 1024:2040].rearrange("p (a b) -> p a b", a=8)
                while m < S:
                    for first in (True, False):
                        a0, b0 = (slice(m - 1, m), 1) if first else (slice(1, m), m)
                        out = slice(m, m + 1) if first else slice(m + 1, 2 * m)
                        n = out.stop - out.start
                        br, bi = (E[:, q, :, b0:b0 + 1].to_broadcast([P, 8, n]) for q in range(2))
                        ar, ai = E[:, 0, :, a0], E[:, 1, :, a0]
                        o0, o1 = w0[:, :, 0:n], w1[:, :, 0:n]
                        tt(o0, ar, br, ALU.mult)
                        tt(o1, ai, bi, ALU.mult)
                        tt(E[:, 0, :, out], o0, o1, ALU.subtract)
                        tt(o0, ar, bi, ALU.mult)
                        tt(o1, ai, br, ALU.mult)
                        tt(E[:, 1, :, out], o0, o1, ALU.add, f"{L} E")
                    m *= 2
                for lv in range(1, LEVELS):
                    for n in range(NT):
                        g.wait_ge(*pool.at(f"{L} Pm psum {lv - 1} {n}"))
                        if lv == 1:
                            g.wait_ge(*pool.at(f"{L} T 0 {n}"))
                        level = C("level")[:, lv * P:(lv + 1) * P].unsqueeze(1).to_broadcast([P, 6, P])
                        tt(Am[:, n], MAT[:, n * 6:n * 6 + 6, 0, :], level, ALU.mult, f"{L} Am {lv} {n}")


def kernel(**inputs):
    import concourse.bacc as _bacc
    from concourse.bass_utils import run_bass_kernel_spmd as _run

    L = LAYERS
    i = {k: np.asarray(v) for k, v in inputs.items()}

    def tiles(a, n):
        return a.reshape(L, n, P).transpose(0, 2, 1)

    def groups(a):
        return a.reshape(L, 8, P).transpose(0, 2, 1)

    cols = np.concatenate([
        tiles(i["norm_mix_pre"], 8), tiles(i["norm_ffn_pre"], 8), tiles(i["rwkv_mu"], 11), tiles(i["rwkv_w0"], 3),
        tiles(i["rwkv_a0"], 3), tiles(i["rwkv_k_k"], 3), tiles(i["rwkv_k_a"], 3), tiles(i["rwkv_r_k"], 3),
        tiles(i["rwkv_ln_w"], 3), tiles(i["rwkv_ln_b"], 3), tiles(i["s5_d"], 2), tiles(i["s5_b_glu"], 2),
        tiles(i["s5_norm"], 2), tiles(i["attn_norm"], 3), groups(i["s5_a_re"]), groups(i["s5_a_im"]),
        groups(np.repeat(i["s5_log_step"][:, :, None], 64, axis=2))], axis=2)
    b_blk = np.zeros((L, 2, 4, 2, 16, 2, 2, 64), np.float32)
    c_blk = np.zeros((L, 2, 64, 2, 8, 2, 16), np.float32)
    for ri, (b, c) in enumerate([("s5_b_re", "s5_c_re"), ("s5_b_im", "s5_c_im")]):
        bb = i[b].reshape(L, 2, 4, 2, 64, 16)
        cc = i[c].reshape(L, 8, 2, 16, 64)
        for g in range(2):
            b_blk[:, :, :, g, :, ri, g, :] = bb[:, :, :, g].transpose(0, 1, 2, 4, 3)
            c_blk[:, g, :, ri, :, g, :] = cc[:, :, g].transpose(0, 3, 1, 2)
    b_blk = b_blk.transpose(0, 2, 3, 4, 1, 5, 6, 7).reshape(L, P, 512)
    c_blk = c_blk.reshape(L, P, 512)
    rel = np.clip(np.arange(P)[:, None] + P - np.arange(384)[None, :], -128, 128) + 128
    bias = i["attn_rel_bias"][:, :, rel][:, [0, 2, 4, 1, 3, 5]].transpose(0, 2, 1, 3).reshape(L, P, 2304)

    def ffn(gate, up, down):
        n = gate.shape[0]
        gu = np.stack([gate.reshape(n, KD, P, CHUNKS, FC), up.reshape(n, KD, P, CHUNKS, FC)], axis=4)
        gu = gu.transpose(0, 3, 2, 1, 4, 5).reshape(n, CHUNKS, P, KD * 512)
        dn = down.reshape(n, CHUNKS, 2, P, D).transpose(0, 1, 3, 2, 4).reshape(n, CHUNKS, P, 2 * D)
        return np.concatenate([gu, dn], axis=3).reshape(n * CHUNKS, P, SLOT)

    arrays = {
        "x": i["x"].reshape(S, D),
        "const": constants(),
        "cols": cols,
        "b_blk": b_blk,
        "c_blk": c_blk,
        "w_glu": i["s5_w_glu"].reshape(L, 2, P, S).transpose(0, 2, 1, 3).reshape(L, P, 512),
        "lora": np.concatenate([i["rwkv_w_up"], i["rwkv_a_up"]], axis=1),
        "g_up": i["rwkv_g_up"],
        "w_in": i["w_in"].reshape(L, KD, P, WT, P).transpose(0, 2, 3, 1, 4).reshape(L, P, WT * D),
        "w_out": i["w_out"].reshape(L, KD, P, D).transpose(0, 2, 1, 3).reshape(L, P, KD * D),
        "bias": bias,
        "mix_post": i["norm_mix_post"],
        "ffn_post": i["norm_ffn_post"],
        "router": i["moe_router"][0].reshape(KD, P, EXPERTS).transpose(1, 0, 2).reshape(P, KD * EXPERTS),
        "ffn": ffn(i["ffn_w_gate"], i["ffn_w_up"], i["ffn_w_down"]),
        "moe": ffn(i["moe_w_gate"][0], i["moe_w_up"][0], i["moe_w_down"][0]),
    }
    arrays = {k: np.ascontiguousarray(v) for k, v in arrays.items()}

    steps = Steps()
    for _ in range(2):
        nc = _bacc.Bacc("TRN2", target_bir_lowering=False, num_devices=1)
        io = {k: nc.dram_tensor(f"in_{k}", a.shape, mybir.dt.from_np(a.dtype), kind="ExternalInput").ap()
              for k, a in arrays.items()}
        io["out"] = nc.dram_tensor("out_0", (S, D), F32, kind="ExternalOutput").ap()
        build(nc, steps, io)
        steps.final = True
    r = _run(nc, [{f"in_{k}": a for k, a in arrays.items()}], core_ids=[0])
    return r.results[0]["out_0"].reshape(1, S, D)
```

```python
from contextlib import ExitStack

import numpy as np

import concourse.bass as bass
from concourse import mybir

F32 = mybir.dt.float32
F32R = mybir.dt.float32r
ALU = mybir.AluOpType
ACT = mybir.ActivationFunctionType
AX = mybir.AxisListType

P = 128
D = 1024
S = 256
NT = S // P
KD = D // P
LAYERS = 2
EXPERTS = 8
MORE = 3
COLUMNS = EXPERTS + MORE + 1
F = 2816
FC = 256
CHUNKS = F // FC
WIN = 2816
WT = WIN // P
UNIT = 2048
IN_ORDER = [11, 12, 13, 14, 15, 16, 17, 18, 19, 20, 21, 9, 10, 3, 4, 5, 0, 1, 2, 6, 7, 8]
UNITS = 7
USES = []
for _i in range(CHUNKS + 2):
    USES += [(_i, 0), (_i, 1)] if _i < CHUNKS else []
    USES += [(_i - 2, 2)] if _i >= 2 else []
NUSES = len(USES)
SPLIT_PLACE = [0, 1, 2, 3] * 3 + [0, 1, 2] * 3 + [0, 1, 2, 3] * 3
AHEAD = 4
assert NUSES == len(SPLIT_PLACE) == 33
EPS = 1e-6
GN_EPS = 64e-5
NEG_HALF_EXP = -0.6065306597126334
TWO_PI = 6.283185307179586
TWO_PI_HI = 6.28125
TWO_PI_LO = TWO_PI - TWO_PI_HI
ROUND = 12582912.0
GELU_C = 0.7978845608028654

COLS = {}
_at = 0
for _name, _n in [("mix_pre", 8), ("ffn_pre", 8), ("mu", 11), ("w0", 3), ("a0", 3), ("k_k", 3), ("k_a", 3),
                  ("r_k", 3), ("ln_w", 3), ("ln_b", 3), ("s5_d", 2), ("b_glu", 2), ("s5_norm", 2),
                  ("attn_norm", 3), ("a_re", 8), ("a_im", 8), ("log_step", 8)]:
    COLS[_name] = (_at, _n)
    _at += _n
NCOL = _at

LEVELS = 7
CONST = {}
_at = 0
for _name, _n in [("ident", 128), ("ones", 128), ("ones_head", 128), ("masks", 256), ("level", LEVELS * 128),
                  ("scan", 256), ("iota", 128)]:
    CONST[_name] = (_at, _n)
    _at += _n
NCONST = _at


def constants():
    i = np.arange(P)
    s, t = i[:, None], i[None, :]
    strict, incl = (s < t), (s <= t)
    level = [((s // (2 * m)) == (t // (2 * m))) & (s % (2 * m) < m) & (t % (2 * m) >= m)
             for m in (1 << np.arange(LEVELS))]
    scan = np.ones((P, S))
    scan[:, ::P] = 0
    parts = [np.eye(P), np.ones((P, P)), (s // 64) == (t // 64), strict, incl, *level, scan,
             np.broadcast_to(i, (P, P))]
    return np.concatenate([np.asarray(a, np.float32) for a in parts], axis=1)


ARENA = {}


def _place(start, items):
    at = start
    for name, n in items:
        ARENA[name] = (at, n)
        at += n
    return at


RING_END = UNITS * UNIT
_end = _place(RING_END, [
    ("x", NT * D), ("hT", KD * S), ("hn", NT * D), ("const", NCONST), ("cols", NCOL), ("b_blk", 512),
    ("c_blk", 512), ("w_glu", 512), ("lora", 384), ("g_up", 384), ("E", 4096), ("act", 1152),
    ("small", 320), ("router", 64)])
SCRATCH = _end
_end = _place(SCRATCH, [("kh", 768), ("bh", 768), ("pT", 11 * 257 + 1), ("pm", 2816), ("a", 768), ("lw", 768),
                        ("c", 768), ("qkT", 1536), ("vA", 768), ("bias", 2304), ("s", 1536),
                        ("PT", 1536), ("aO", 768)])
MIX_END = SCRATCH + 18432
assert _end <= MIX_END
ARENA_END = _place(MIX_END, [("natural", 2304), ("bonus", 768), ("g", 768)])
_place(ARENA["pT"][0], [("kkn", 768), ("e1", 768), ("e2", 768)])
_place(ARENA["natural"][0], [("z0", 1024), ("z1", 1024), ("z2", 1024)])
_place(ARENA["kh"][0], [("z3", 1024)])
_place(ARENA["lw"][0], [("z4", 1024)])
_place(ARENA["pT"][0], [("MAT", 12 * 512), ("T", 1536), ("TT", 1536), ("Pm", 1536), ("Am", 1536)])
assert ARENA["Am"][0] + 1536 <= MIX_END
_place(ARENA["hn"][0], [("AR", 1536), ("uT", 512)])
_place(ARENA["act"][0], [("rhs", 384), ("sa", 384), ("st", 384)])
_place(ARENA["hT"][0], [("hTe", 1024), ("ffn_gain", D)])
_place(ARENA["E"][0], [("mix_gain", D)])
_end = _place(ARENA["E"][0], [
    ("ffn_sum", 2048), ("y", 1024), ("sel", 16), ("rank", 24), ("eq", 16), ("cum", 16), ("over", 8), ("order", 8),
    ("onehot", 8), ("prod", 16), ("pick", 2), ("slot_of", NT * COLUMNS), ("gate_of", NT * COLUMNS), ("disp", 256),
    ("gated", 256), ("gatedT", 256)])
assert _end <= ARENA["E"][0] + 4096
_place(ARENA["Pm"][0], [("OT", 768), ("o1", 768)])
_place(ARENA["Am"][0], [("o2", 768)])

SMALL = {}
_at = 0
for _name, _n in [("ss", 2), ("v", 2), ("sq", 2), ("rstd", 2), ("theta", 16), ("t0", 16), ("t1", 16), ("t2", 16),
                  ("lr", 16), ("r", 16), ("sn", 16), ("cs", 16), ("fr", 8), ("fi", 8), ("u0", 8), ("u1", 8),
                  ("half", 8), ("rmax", 12), ("rsum", 12), ("rinv", 12), ("dec", 3), ("cmid", 6), ("lg", 16),
                  ("m8", 16), ("comb", 16), ("g1", 2), ("passes", 16), ("total", 1)]:
    SMALL[_name] = (_at, _n)
    _at += _n
assert _at <= 320, _at


class Steps:

    def __init__(self):
        self.at = {}
        self.per = {}
        self.final = False


class Engine:

    def __init__(self, name, sems, steps):
        self.name, self.sems, self.steps = name, sems, steps
        self.count, self.part, self.i, self.start = 0, "before", None, 0

    def step(self, name=None):
        self.count += 1
        if name is not None:
            self.steps.at[name] = (self.name, self.count, self.part)
        return self.sems[self.name], 1

    def enter(self, i):
        self.part, self.i, self.start = "loop", i, self.count

    def leave(self, total):
        self.steps.per[self.name] = self.count - self.start
        self.part, self.i, self.count = "after", total, self.start

    def value(self, engine, value, part, back=0):
        if part != "before":
            value = value + self.steps.per.get(engine, 1) * (self.i - back)
        return self.sems[engine], value

    def last(self):
        part = self.part
        if part != "before" and self.count == self.start:
            part = "loop"
        return self.value(self.name, self.count, part)

    def at(self, name, back=0):
        if name not in self.steps.at and self.steps.final:
            raise KeyError(name)
        engine, value, part = self.steps.at.get(name, ("pe", 1 << 12, "before"))
        return self.value(engine, value, part, back)


def build(nc, steps, io):
    ctx = ExitStack()
    with ctx:
        arena = ctx.enter_context(nc.sbuf_tensor("arena", [P, SCRATCH], F32))
        with nc.sbuf_tensor("scratch", [P, ARENA_END - SCRATCH], F32) as scratch:
            pass
        split = ctx.enter_context(nc.sbuf_tensor("split", [P, 4, 2, UNIT], F32R))
        hTr = ctx.enter_context(nc.sbuf_tensor("hTr", [P, 2, KD, S], F32R))
        actTr = ctx.enter_context(nc.sbuf_tensor("actTr", [P, 2, 2, 2, P], F32R))
        ps = ctx.enter_context(nc.psum_tensor("ps", [P, 8, 512], F32))
        sems = {n: ctx.enter_context(nc.semaphore(f"{n}_done")) for n in ("pe", "act", "dve", "pool")}
        unit_filled = [ctx.enter_context(nc.semaphore(f"unit_filled{i}")) for i in range(UNITS)]
        x_loaded = ctx.enter_context(nc.semaphore("x_loaded"))
        const_loaded = ctx.enter_context(nc.semaphore("const_loaded"))
        params_loaded = ctx.enter_context(nc.semaphore("params_loaded"))
        bias_loaded = ctx.enter_context(nc.semaphore("bias_loaded"))
        gain_loaded = ctx.enter_context(nc.semaphore("gain_loaded"))
        router_loaded = ctx.enter_context(nc.semaphore("router_loaded"))
        out_stored = ctx.enter_context(nc.semaphore("out_stored"))

        def V(name, *dims):
            at, n = ARENA[name]
            size = int(np.prod(dims)) if dims else n
            a = arena[:, at:at + size] if at < SCRATCH else scratch[:, at - SCRATCH:at - SCRATCH + size]
            if len(dims) > 1:
                names = "abcd"[:len(dims)]
                a = a.rearrange(f"p ({' '.join(names)}) -> p {' '.join(names)}", **dict(zip(names, dims)))
            return a

        def C(name):
            at, n = CONST[name]
            return V("const")[:, at:at + n]

        def col(name, i=None):
            at, n = COLS[name]
            c = V("cols")
            return c[:, at:at + n] if i is None else c[:, at + i:at + i + 1]

        def sm(name, i=None, n=1):
            at, k = SMALL[name]
            s = V("small")
            return s[:, at:at + k] if i is None else s[:, at + i:at + i + n]

        def unit(i):
            return arena[:, i * UNIT:(i + 1) * UNIT]

        x, hT, hn = V("x", NT, D), V("hT", KD, S), V("hn", NT, D)
        ident, ones, ones_head = C("ident"), C("ones"), C("ones_head")
        E = V("E", 2, 8, S)
        pT, pm = V("pT", 11, 257), V("pm", 11, S)
        AR = V("AR", 3, NT, 2, P)
        kh, bh = V("kh", 3, S), V("bh", 3, S)
        natural = V("natural", 3, NT, 384)
        MAT = V("MAT", 12, 4, P)
        T, TT, Pm, Am = (V(n, 2, 6, P) for n in ("T", "TT", "Pm", "Am"))
        act_buf = V("act")[:, 0:1024].rearrange("p (a b) -> p a b", a=4)
        uT, qkT, vA = V("uT", 2, S), V("qkT", 6, S), V("vA", NT, 384)

        def ffn_out(L, n):
            return ps[:, 4 + 2 * n:6 + 2 * n, :].rearrange("p a b -> p (a b)") if L == 0 else ffn_sum[:, n, :]

        def halves(a, lv, which):
            if len(a.shape) == 2:
                return a.rearrange("p (b k m) -> p b k m", k=2, m=1 << lv)[:, :, which, :]
            return a.rearrange("p h (b k m) -> p h b k m", k=2, m=1 << lv)[:, :, :, which, :]

        def six_of(bank):
            return ps[:, bank:bank + 2, :].rearrange("p a b -> p (a b)")[:, 0:768].rearrange("p (h m) -> p h m", h=6)

        def bc(a, n):
            return a.unsqueeze(2).to_broadcast([P, a.shape[1], n])

        ffn_sum, hTe, y_sb = V("ffn_sum", NT, D), V("hTe", KD, P), V("y")
        disp, gated, gatedT = V("disp", NT, P), V("gated", NT, P), V("gatedT", NT, P)
        slot_of, gate_of = V("slot_of", NT, COLUMNS), V("gate_of", NT, COLUMNS)
        passes_at = ARENA["small"][0] + SMALL["passes"][0]
        passes = arena[0:1, passes_at:passes_at + 17].bitcast(mybir.dt.int32)

        block = ctx.enter_context(nc.Block())

        statics = []
        for L in range(LAYERS):
            statics += [("win", L, g) for g in range(WT // 2)] + [("wout", L, g) for g in range(KD // 2)]
            if L == 0:
                statics += [("ffn", 0, k) for k in range(NUSES)]
        assert len(statics) % UNITS == 0
        number = {u: k for k, u in enumerate(statics)}

        def place(kind, L, g):
            return number[(kind, L, g)] % UNITS

        def filled(kind, L, g):
            k = number[(kind, L, g)]
            return unit_filled[k % UNITS], 16 * (k // UNITS + 1)

        def filled_of_pass(k, i):
            per_pass = len(range(k % UNITS, NUSES, UNITS))
            return unit_filled[k % UNITS], 16 * (len(statics) // UNITS + k // UNITS + 1) + i * (16 * per_pass)

        def before(k, places):
            same = [q for q in range(NUSES) if places[q] == places[k]]
            earlier = [q for q in same if q < k]
            return (earlier[-1], 0) if earlier else (same[-1], 1)

        turn_before = {USES.index((max(j - 1, 0), 2)) if j else USES.index((2, 0)): j for j in range(CHUNKS)}
        LAST_GATE_UP = USES.index((CHUNKS - 1, 1))
        TURN_GATED, GATHER = 4, 8
        GATED_TURNED = USES.index((TURN_GATED + 1, 0))

        splits_after = {k: [] for k in range(NUSES)}
        for u in range(AHEAD, NUSES + AHEAD):
            q = max(q for q in range(u) if (SPLIT_PLACE * 2)[q] == (SPLIT_PLACE * 2)[u])
            q = max(q, u - AHEAD)
            splits_after[q if q < LAST_GATE_UP else min(max(q + 1, LAST_GATE_UP + 2), NUSES - 1)].append(u)
        LEAD = UNITS + AHEAD
        ring_place = [k % UNITS for k in range(NUSES)]

        @block.sync
        def _(sp):
            en = Engine("sp", sems, steps)
            sp.dma_start(V("x", NT, D), io["x"].rearrange("(n p) d -> p n d", p=P)).then_inc(x_loaded, 16)
            sp.dma_start(V("const"), io["const"]).then_inc(const_loaded, 16)

            def params(L):
                for k, name in enumerate(["cols", "b_blk", "c_blk", "w_glu", "lora", "g_up"]):
                    sp.dma_start(V(name), io[name][L]).then_inc(params_loaded, 16)

            params(0)
            sp.dma_start(V("router"), io["router"]).then_inc(router_loaded, 16)
            for k, (kind, L, g) in enumerate(statics):
                if (kind, L, g) == ("win", 1, 0):
                    sp.wait_ge(*en.at("0 ffn hT low 7"))
                    sp.wait_ge(*en.at("0 mix used params"))
                    params(1)
                if (kind, L, g) == ("ffn", 0, UNITS):
                    sp.wait_ge(*en.at("0 mix post gained"))
                    sp.dma_start(V("ffn_gain"), io["ffn_post"][0:1].to_broadcast([P, D])).then_inc(gain_loaded, 16)
                if (kind, g) == ("win", UNITS):
                    if L:
                        sp.wait_ge(*en.at(f"ffn down {NT * CHUNKS - 1}"))
                    sp.dma_start(V("bias"), io["bias"][L]).then_inc(bias_loaded, 16)
                if k >= UNITS:
                    sp.wait_ge(*en.at("%s %d %d read" % statics[k - UNITS]))
                source = {"win": io["w_in"][L], "wout": io["w_out"][L], "ffn": io["ffn"]}[kind]
                sp.dma_start(unit(k % UNITS), source[g]).then_inc(unit_filled[k % UNITS], 16)
                if (kind, g) == ("wout", KD // 2 - 1):
                    sp.wait_ge(*en.at(f"{L} s5 x 1"))
                    sp.dma_start(V("mix_gain"), io["mix_post"][L:L + 1].to_broadcast([P, D])).then_inc(gain_loaded, 16)
            for k in range(LEAD):
                if k < UNITS:
                    sp.wait_ge(*en.at("%s %d %d read" % statics[len(statics) - UNITS + k]))
                else:
                    sp.wait_ge(*en.at(f"first split {k - UNITS}"))
                sp.dma_start(unit(k % UNITS), io["moe"][k]).then_inc(unit_filled[k % UNITS], 16)
            sp.wait_ge(*en.at("logits psum"))
            sp.dma_start(V("ffn_gain"), io["ffn_post"][1:2].to_broadcast([P, D])).then_inc(gain_loaded, 16)
            sp.wait_ge(*en.at("passes"))
            total = sp.value_load(passes[:, 16:17], min_val=EXPERTS, max_val=EXPERTS + MORE)

            def rest(expert):
                for k in range(LEAD, NUSES):
                    sp.wait_ge(*en.at(f"moe split {k - UNITS}", back=1))
                    sp.dma_start(unit(k % UNITS), io["moe"][expert * NUSES + k]).then_inc(unit_filled[k % UNITS], 16)

            with sp.Fori(1, total) as i:
                en.enter(i)
                rest(sp.value_load(passes[:, bass.ds(i - 1, 1)], min_val=0, max_val=EXPERTS - 1))
                expert = sp.value_load(passes[:, bass.ds(i, 1)], min_val=0, max_val=EXPERTS - 1)
                for k in range(LEAD):
                    sp.wait_ge(*en.at(f"moe split {before(k, ring_place)[0]}", back=1))
                    sp.dma_start(unit(k % UNITS), io["moe"][expert * NUSES + k]).then_inc(unit_filled[k % UNITS], 16)
            en.leave(total)
            rest(sp.value_load(passes[:, bass.ds(total - 1, 1)], min_val=0, max_val=EXPERTS - 1))
            for k in range(AHEAD):
                sp.wait_ge(*en.at(f"moe split {before(k, ring_place)[0]}", back=1))
                sp.dma_start(unit(k)[:, 0:16], io["moe"][k][:, 0:16]).then_inc(unit_filled[k], 16)
            for n in range(NT):
                sp.wait_ge(*en.at(f"{LAYERS} x ready mix {n}"))
                sp.dma_start(io["out"][n * P:(n + 1) * P, :], x[:, n, :]).then_inc(out_stored, 16)
            sp.wait_ge(out_stored, 16 * NT)

        @block.tensor
        def _(t):
            pe = Engine("pe", sems, steps)

            def mm(out, lhsT, rhs, start=True, stop=True, **kw):
                return nc.tensor.matmul(out, lhsT, rhs, start=start, stop=stop, **kw)

            reader = {}

            def take(banks, by):
                for b in banks:
                    for r in reader.get(b, ()):
                        t.wait_ge(*pe.at(r))
                    reader[b] = (by,) if isinstance(by, str) else tuple(by)

            def hidden(L, which):
                for c in range(KD):
                    take([c], f"{L} {which} hT low {c}" if (L, which) == (0, "ffn") else f"{L} {which} hT {c}")
                for n in range(NT):
                    t.wait_ge(*pe.at(f"{L} {which} hn {n}"))
                    for c in range(KD):
                        last = nc.tensor.transpose(ps[:, c, n * P:(n + 1) * P], hn[:, n, c * P:(c + 1) * P], ident)
                        if n == NT - 1:
                            last.then_inc(*pe.step(f"{L} {which} hT psum {c}"))

            def ffn(tag, tiles, after=lambda i: None):
                parts, loop = CHUNKS * tiles, pe.part == "loop"
                k = 0

                def same(p):
                    return (p - 2, 0) if p >= 2 else (parts - 1 - (parts - 1 - p) % 2, 1)

                for i in range(CHUNKS + 2):
                    for half in range(2 if i < CHUNKS else 0):
                        t.wait_ge(*pe.at(f"{tag} split {k}", back=1 if loop and k < AHEAD else 0))
                        w = split[:, SPLIT_PLACE[k], :, :].rearrange("p a (c m) -> p a c m", c=4)
                        for n in range(tiles):
                            p = i * tiles + n
                            if half == 0 and (p >= 2 or loop):
                                q, back = same(p)
                                t.wait_ge(*pe.at(f"{tag} act {q}", back=back))
                            for c in range(4):
                                for a, b in ((0, 0), (0, 1), (1, 0)):
                                    last = mm(ps[:, p % 2, :], hTr[:, a, 4 * half + c, n * P:(n + 1) * P], w[:, b, c, :],
                                              start=(half == 0 and c == 0 and (a, b) == (0, 0)),
                                              stop=(half == 1 and c == 3 and (a, b) == (1, 0)), skip_group_check=True)
                            last.then_inc(*pe.step(f"{tag} gate_up {p}" if half else None))
                        steps.at[f"{tag} used {k}"] = ("pe", pe.count, pe.part)
                        k += 1
                    after(i)
                    for n in range(tiles if 1 <= i <= CHUNKS else 0):
                        p = (i - 1) * tiles + n
                        t.wait_ge(*pe.at(f"{tag} act {p}"))
                        if p >= 2 or loop:
                            q, back = same(p)
                            t.wait_ge(*pe.at(f"{tag} actT {q}", back=back))
                        for m in range(2):
                            last = nc.tensor.transpose(ps[:, 2 + p % 2, m * P:(m + 1) * P],
                                                       act_buf[:, p % 2, m * P:(m + 1) * P], ident)
                        last.then_inc(*pe.step(f"{tag} turned {p}"))
                    if i < 2:
                        continue
                    t.wait_ge(*pe.at(f"{tag} split {k}"))
                    w = split[:, SPLIT_PLACE[k], :, :].rearrange("p a (m d) -> p a m d", m=2)
                    if loop and i == 2:
                        t.wait_ge(*pe.at("moe summed 1"))
                    for n in range(tiles):
                        p = (i - 2) * tiles + n
                        t.wait_ge(*pe.at(f"{tag} actT {p}"))
                        for m in range(2):
                            for a, b in ((0, 0), (0, 1), (1, 0)):
                                for h in range(2):
                                    last = mm(ps[:, 4 + 2 * n + h, :], actTr[:, p % 2, a, m, :],
                                              w[:, b, m, h * 512:(h + 1) * 512],
                                              start=(i == 2 and m == 0 and (a, b) == (0, 0)),
                                              stop=(i == CHUNKS + 1 and m == 1 and (a, b) == (1, 0)),
                                              skip_group_check=True)
                        last.then_inc(*pe.step(f"{tag} down {p}"))
                    steps.at[f"{tag} used {k}"] = ("pe", pe.count, pe.part)
                    k += 1

            def gather(tag):
                for b in range(2):
                    for c in range(4 * b, 4 * b + 4):
                        for n in range(NT):
                            last = mm(ps[:, 6 + b, (c % 4) * P:(c % 4 + 1) * P], hn[:, n, c * P:(c + 1) * P],
                                      disp[:, n, :], start=(n == 0), stop=(n == NT - 1))
                    last.then_inc(*pe.step(f"{tag} gathered {b}"))

            def scatter(tag):
                t.wait_ge(*pe.at("moe y taken", back=1))
                t.wait_ge(*pe.at("moe hTe 1", back=1))
                for q in range(4):
                    n, h = q // 2, q % 2
                    mm(ps[:, 4 + q, :], gatedT[:, n, :], y_sb[:, h * 512:(h + 1) * 512]
                       ).then_inc(*pe.step(f"{tag} scattered {q}"))

            def experts():
                t.wait_ge(*pe.at("disp built"))
                gather("first")
                t.wait_ge(*pe.at("first hT low"))
                t.wait_ge(*pe.at(f"first split {AHEAD - 1}"))
                t.wait_ge(*pe.at("no outputs"))
                total = t.value_load(passes[:, 16:17], min_val=EXPERTS, max_val=EXPERTS + MORE)
                with t.Fori(0, total) as i:
                    pe.enter(i)
                    t.wait_ge(*pe.at("moe hT low", back=1))

                    def after(i):
                        if i == 0:
                            scatter("moe")
                        if i == TURN_GATED:
                            t.wait_ge(*pe.at("moe summed 3"))
                            for n in range(NT):
                                last = nc.tensor.transpose(ps[:, 6, n * P:(n + 1) * P], gated[:, n, :], ident)
                            last.then_inc(*pe.step("moe gated turned"))
                        if i == GATHER:
                            t.wait_ge(*pe.at("moe disp built"))
                            t.wait_ge(*pe.at("moe gatedT"))
                            gather("moe")

                    ffn("moe", 1, after)
                pe.leave(total)
                scatter("last")

            def win_tile(L, f):
                k = IN_ORDER.index(f)
                t.wait_ge(*filled("win", L, k // 2))
                return unit(place("win", L, k // 2))[:, (k % 2) * D:(k % 2 + 1) * D].rearrange("p (c m) -> p c m", c=KD)

            def project(L, f, bank):
                if f == 11:
                    for c in range(KD):
                        t.wait_ge(*pe.at(f"{L} mix hT {c}"))
                w = win_tile(L, f)
                take([bank], f"{L} proj {f}")
                for c in range(KD):
                    last = mm(ps[:, bank, 0:S], w[:, c, :], hT[:, c, :], start=(c == 0), stop=(c == KD - 1))
                last.then_inc(*pe.step(f"{L} proj psum {f}"))
                steps.at[f"win {L} {IN_ORDER.index(f) // 2} read"] = ("pe", pe.count, pe.part)

            def scores(L, n):
                keys = (n + 1) * P
                if n == 0:
                    for f in range(13, 19):
                        t.wait_ge(*pe.at(f"{L} proj {f}"))
                take(range(6), f"{L} scores {n} out")
                for h in range(6):
                    r, q = slice(64 * (h // 3), 64 * (h // 3) + 64), h % 3
                    last = mm(ps[:, h, 0:keys], qkT[r, q, n * P:(n + 1) * P], qkT[r, 3 + q, 0:keys])
                last.then_inc(*pe.step(f"{L} scores {n}"))

            def probs_turned(L, n, banks):
                t.wait_ge(*pe.at(f"{L} probs {n}"))
                sprob = V("s", 6, (n + 1) * P)
                for k, m in enumerate(banks):
                    take([m], f"{L} PT {n} {m}")
                    blocks = [(h, jb) for h in range(6) for jb in range(n + 1)][4 * k:4 * k + 4]
                    for i, (h, jb) in enumerate(blocks):
                        last = nc.tensor.transpose(ps[:, m, i * P:(i + 1) * P], sprob[:, h, jb * P:(jb + 1) * P],
                                                   ident)
                    last.then_inc(*pe.step(f"{L} PT psum {n} {m}"))

            def attended(L, n, banks):
                PT = V("PT", 3, 4, P)
                bank = (1, 3)[n]
                take([bank], f"{L} o {n}")
                for n2 in range(n + 1):
                    t.wait_ge(*pe.at(f"{L} vA {n2}"))
                for m in banks:
                    t.wait_ge(*pe.at(f"{L} PT {n} {m}"))
                for h in range(6):
                    head = 2 * (h % 3) + h // 3
                    for jb in range(n + 1):
                        i = h * (n + 1) + jb
                        last = mm(ps[:, bank, head * 64:head * 64 + 64], PT[:, i // 4, i % 4, :],
                                  vA[:, jb, head * 64:head * 64 + 64], start=(jb == 0), stop=(jb == n))
                last.then_inc(*pe.step(f"{L} o psum {n}"))

            def out_turned(L, n, bank):
                t.wait_ge(*pe.at(f"{L} o normed {n}"))
                take([bank], f"{L} oT {n}")
                aO = V("aO", 2, 384)
                for q in range(3):
                    last = nc.tensor.transpose(ps[:, bank, q * P:(q + 1) * P], aO[:, n, q * P:(q + 1) * P], ident)
                last.then_inc(*pe.step(f"{L} oT psum {n}"))

            def s5_in(L, H):
                b_blk = V("b_blk", 2, 2, P)
                t.wait_ge(*pe.at(f"{L} proj {11 + H}"))
                take([4, 5, 6, 7], f"{L} bu {H} read")
                for i in range(4):
                    r = slice(32 * i, 32 * i + 32)
                    for ri in range(2):
                        last = mm(ps[:, 4 + i, ri * S:(ri + 1) * S], b_blk[r, H, ri, :], uT[r, H, :],
                                  start=True, stop=True, tile_position=(32 * i, 0))
                last.then_inc(*pe.step(f"{L} bu {H}"))

            def s5_out(L, H):
                c_blk = V("c_blk", 2, 8, 32)
                t.wait_ge(*pe.at(f"{L} s5 x {H}"))
                t.wait_ge(*pe.at(f"{L} c scaled"))
                take([H], f"{L} y0 {H}")
                for i in range(4):
                    for ri, xx in enumerate((V("z0", 4, S), V("z2", 4, S))):
                        last = mm(ps[32 * i:32 * i + 32, H, 0:S], c_blk[:, ri, 4 * H + i, :], xx[:, i, :],
                                  start=(ri == 0), stop=(ri == 1))
                last.then_inc(*pe.step(f"{L} y psum {H}"))

            t.wait_ge(const_loaded, 16)
            for L in range(LAYERS):
                hidden(L, "mix")
                t.wait_ge(params_loaded, 96 * (L + 1))
                for f in range(11, 19):
                    project(L, f, f - 11)
                for n in range(NT):
                    b = 3 + n
                    take([b], f"{L} vA {n}")
                    for q in range(3):
                        w = win_tile(L, 19 + q)
                        for c in range(KD):
                            last = mm(ps[:, b, q * P:(q + 1) * P], hT[:, c, n * P:(n + 1) * P],
                                      w[:, c, :], start=(c == 0), stop=(c == KD - 1))
                    last.then_inc(*pe.step(f"{L} vA psum {n}"))
                steps.at[f"win {L} 4 read"] = ("pe", pe.count, pe.part)
                scores(L, 0)
                project(L, 9, 6)
                project(L, 10, 7)
                probs_turned(L, 0, [6, 7])
                scores(L, 1)
                project(L, 3, 6)
                attended(L, 0, [6, 7])
                s5_in(L, 0)
                project(L, 4, 0)
                probs_turned(L, 1, [2, 3, 0])
                project(L, 5, 2)
                attended(L, 1, [2, 3, 0])
                project(L, 0, 0)
                s5_in(L, 1)
                project(L, 1, 2)
                s5_out(L, 0)
                project(L, 2, 2)
                project(L, 6, 2)
                project(L, 7, 4)
                project(L, 8, 5)
                out_turned(L, 0, 6)
                out_turned(L, 1, 2)
                s5_out(L, 1)
                lora, g_up = V("lora"), V("g_up")
                t.wait_ge(*pe.at(f"{L} w_lo tanh"))
                t.wait_ge(*pe.at(f"{L} shifted 9"))
                for q in range(3):
                    take([q], f"{L} decay {q}")
                    mm(ps[:, q, 0:S], lora[0:64, q * P:(q + 1) * P], pm[0:64, 9, :]).then_inc(*pe.step(f"{L} decay psum {q}"))
                for q in range(3):
                    take([3 + q], f"{L} rate {q}")
                    mm(ps[:, 3 + q, 0:S], lora[64:128, q * P:(q + 1) * P], pm[64:128, 9, :]).then_inc(*pe.step(f"{L} rate psum {q}"))
                t.wait_ge(*pe.at(f"{L} g_lo sigmoid"))
                take([6, 7], f"{L} g")
                for q in range(3):
                    last = mm(ps[:, 6 + q // 2, (q % 2) * S:(q % 2 + 1) * S], g_up[:, q * P:(q + 1) * P], pm[:, 10, :],
                              start=True, stop=True)
                last.then_inc(*pe.step(f"{L} g psum"))
                y = V("z0", 2, S)
                t.wait_ge(*pe.at(f"{L} gelu"))
                take([2], f"{L} glu")
                w_glu = V("w_glu", 2, S)
                for m in range(2):
                    for c in range(2):
                        last = mm(ps[:, 2, m * S:(m + 1) * S], w_glu[:, c, m * P:(m + 1) * P], y[:, c, :],
                                  start=(c == 0), stop=(c == 1))
                last.then_inc(*pe.step(f"{L} glu psum"))
                t.wait_ge(*pe.at(f"{L} kk squared"))
                take([0, 1], f"{L} kk sum out")
                sq = V("e2")
                mm(ps[:, 0, :], ones_head, sq[:, 0:512])
                mm(ps[:, 1, 0:256], ones_head, sq[:, 512:768]).then_inc(*pe.step(f"{L} kk sum"))
                t.wait_ge(*pe.at(f"{L} s5 squared"))
                take([3], f"{L} s5 var")
                sq = V("z1", 2, S)
                for c in range(2):
                    last = mm(ps[:, 3, 0:S], ones, sq[:, c, :], start=(c == 0), stop=(c == 1))
                last.then_inc(*pe.step(f"{L} s5 sum"))
                t.wait_ge(*pe.at(f"{L} rk"))
                take([2, 3], f"{L} bonus")
                sq = V("e1")
                mm(ps[:, 2, :], ones_head, sq[:, 0:512])
                mm(ps[:, 3, 0:256], ones_head, sq[:, 512:768]).then_inc(*pe.step(f"{L} rk sum"))
                for k, (src, step) in enumerate([(bh, "bh"), (kh, "kh"), (pm[:, 6:9, :], "shifted 8")]):
                    t.wait_ge(*pe.at(f"{L} {step}"))
                    for n in range(NT):
                        b = (4 + 2 * k + n) % 8
                        take([b], f"{L} natural {k} {n}")
                        for q in range(3):
                            last = nc.tensor.transpose(ps[:, b, q * P:(q + 1) * P], src[:, q, n * P:(n + 1) * P], ident)
                        last.then_inc(*pe.step(f"{L} natural psum {k} {n}"))
                t.wait_ge(*pe.at(f"{L} AR"))
                for n in range(NT):
                    for h in range(6):
                        q, r = h // 2, slice(64 * (h % 2), 64 * (h % 2) + 64)
                        i = n * 6 + h
                        b = i % 4
                        take([b], f"{L} mat {i}")
                        ar = AR[r, q, n, :, :]
                        mm(ps[:, b, 0:256].rearrange("p (a b) -> p a b", a=2), bh[r, q, n * P:(n + 1) * P], ar)
                        mm(ps[:, b, 256:512].rearrange("p (a b) -> p a b", a=2),
                                   kh[r, q, n * P:(n + 1) * P], ar).then_inc(*pe.step(f"{L} mat psum {i}"))
                def six(out_bank, lhs, rhs, step, part=lambda a: a):
                    for h in range(6):
                        last = mm(part(ps[:, out_bank + h // 4, (h % 4) * P:(h % 4 + 1) * P]), lhs(h), part(rhs(h)),
                                  start=True, stop=True)
                    last.then_inc(*pe.step(step))

                for lv in range(LEVELS):
                    for n in range(NT):
                        t.wait_ge(*pe.at(f"{L} Am {lv} {n}"))
                        if lv:
                            t.wait_ge(*pe.at(f"{L} T {lv - 1} {n}"))
                            if lv > 1:
                                t.wait_ge(*pe.at(f"{L} TT {lv - 1} {n}"))
                        take([4 * n, 4 * n + 1], f"{L} Pm {lv} {n}")
                        six(4 * n, lambda h: Am[:, n, h, :], lambda h: T[:, n, h, :] if lv else ident,
                            f"{L} Pm psum {lv} {n}")
                    if lv == 0:
                        continue
                    for n in range(NT):
                        t.wait_ge(*pe.at(f"{L} Pm {lv} {n}"))
                        if lv < LEVELS - 1:
                            take([4 * n + 2, 4 * n + 3], f"{L} T {lv} {n}")
                            six(4 * n + 2, lambda h: TT[:, n, h, :], lambda h: Pm[:, n, h, :], f"{L} T psum {lv} {n}",
                                lambda a: halves(a, lv, 0))
                        take([4 * n, 4 * n + 1], f"{L} TT {lv} {n}")
                        six(4 * n, lambda h: Pm[:, n, h, :], lambda h: TT[:, n, h, :], f"{L} TT psum {lv} {n}",
                            lambda a: halves(a, lv, 1))
                early = [(n, c, h) for n in range(NT) for c in range(3, KD) for h in range(2)]

                def out_product(n, c, h):
                    if (c, h) == (3, 0):
                        t.wait_ge(*pe.at(f"{L} mixed s5"))
                        t.wait_ge(*pe.at(f"{L} oT {n}"))
                        take([4 * n, 4 * n + 1], (f"{L} post square {n}", f"{L} post read {n}"))
                    t.wait_ge(*filled("wout", L, c // 2))
                    w = unit(place("wout", L, c // 2)).rearrange("p (c m) -> p c m", c=2)
                    return mm(ps[:, 4 * n + h, :], hT[:, c, n * P:(n + 1) * P], w[:, c % 2, h * 512:(h + 1) * 512],
                              start=(c == 3), stop=(c == 2), skip_group_check=True)

                def fill(count):
                    for _ in range(min(count, len(early))):
                        out_product(*early.pop(0))

                rhs, sa, st = V("rhs"), V("sa"), V("st", 3, P)
                for n in range(NT):
                    take([2], f"{L} rhs {n}")
                    for q in range(3):
                        if n:
                            t.wait_ge(*pe.at(f"{L} state"))
                            mm(ps[:, 2, q * P:(q + 1) * P], AR[:, q, n, 0, :], st[:, q, :], start=True, stop=False,
                               skip_group_check=True)
                        for h in (2 * q, 2 * q + 1):
                            last = mm(ps[:, 2, h * 64:h * 64 + 64], MAT[:, n * 6 + h, 2, :],
                                      natural[:, 2, n, h * 64:h * 64 + 64], start=(n == 0), stop=True,
                                      skip_group_check=True)
                    last.then_inc(*pe.step(f"{L} rhs psum {n}"))
                    fill(1)
                    t.wait_ge(*pe.at(f"{L} rhs {n}"))
                    t.wait_ge(*pe.at(f"{L} TT {LEVELS - 1} {n}"))
                    take([3], f"{L} sa {n}")
                    for h in range(6):
                        last = mm(ps[:, 3, h * 64:h * 64 + 64], TT[:, n, h, :], rhs[:, h * 64:h * 64 + 64])
                    last.then_inc(*pe.step(f"{L} sa psum {n}"))
                    fill(1)
                    t.wait_ge(*pe.at(f"{L} sa {n}"))
                    take([6], f"{L} OT {n}")
                    for q in range(3):
                        if n:
                            mm(ps[:, 6, q * P:(q + 1) * P], st[:, q, :], AR[:, q, n, 1, :], start=True, stop=False,
                               skip_group_check=True)
                        for h in (2 * q, 2 * q + 1):
                            o = ps[64 * (h % 2):64 * (h % 2) + 64, 6, q * P:(q + 1) * P]
                            mm(o, sa[:, h * 64:h * 64 + 64], MAT[:, n * 6 + h, 1, :], start=(n == 0), stop=False,
                               skip_group_check=True)
                            last = mm(o, natural[:, 2, n, h * 64:h * 64 + 64], MAT[:, n * 6 + h, 3, :],
                                      start=False, stop=True, skip_group_check=True)
                    last.then_inc(*pe.step(f"{L} OT psum {n}"))
                    if n == 0:
                        take([7], f"{L} state")
                        for q in range(3):
                            w = slice(q * P, (q + 1) * P)
                            mm(ps[:, 7, w], natural[:, 0, n, w], sa[:, w], start=True, stop=False)
                            last = mm(ps[:, 7, w], natural[:, 1, n, w], natural[:, 2, n, w], start=False, stop=True)
                        last.then_inc(*pe.step(f"{L} state psum"))
                        fill(1)
                OT, o1, o2 = V("OT"), V("o1"), V("o2")
                t.wait_ge(*pe.at(f"{L} OT 1"))
                take([2, 3], f"{L} centred")
                mm(ps[:, 2, :], ones_head, OT[:, 0:512])
                mm(ps[:, 3, 0:256], ones_head, OT[:, 512:768]).then_inc(*pe.step(f"{L} mean psum"))
                fill(2)
                t.wait_ge(*pe.at(f"{L} o squared"))
                take([6, 7], f"{L} gn var")
                mm(ps[:, 6, :], ones_head, o2[:, 0:512])
                mm(ps[:, 7, 0:256], ones_head, o2[:, 512:768]).then_inc(*pe.step(f"{L} var psum"))
                fill(len(early))
                t.wait_ge(*pe.at(f"{L} mixed rwkv"))
                for n in range(NT):
                    for c in range(3):
                        for h in range(2):
                            last = out_product(n, c, h)
                    last.then_inc(*pe.step(f"{L} out psum {n}"))
                for g in range(KD // 2):
                    steps.at[f"wout {L} {g} read"] = ("pe", pe.count, pe.part)
                hidden(L, "ffn")
                for c in range(KD):
                    t.wait_ge(*pe.at(f"{L} ffn hT {c}"))
                if L == 0:
                    t.wait_ge(*pe.at("0 ffn hT low 7"))
                    ffn("ffn", NT)
                    post = [(f"0 fpost square {n}", f"0 fpost read {n}") for n in range(NT)]
                    last = NT * CHUNKS - 1
                    reader = {0: (f"ffn act {last - 1}",), 1: (f"ffn act {last}",), 2: (f"ffn actT {last - 1}",),
                              3: (f"ffn actT {last}",), 4: post[0], 5: post[0], 6: post[1], 7: post[1]}
                else:
                    t.wait_ge(router_loaded, 16)
                    router = V("router", KD, 8)
                    take([0], "logits")
                    for n in range(NT):
                        for c in range(KD):
                            last = mm(ps[:, 0, n * 8:n * 8 + 8], hT[:, c, n * P:(n + 1) * P], router[:, c, :],
                                      start=(c == 0), stop=(c == KD - 1))
                    last.then_inc(*pe.step("logits psum"))
                    sel = V("sel", NT, EXPERTS)
                    earlier = C("masks")[:, 0:P]
                    take([1], "ranks")
                    t.wait_ge(*pe.at("sel"))
                    mm(ps[:, 1, 0:8], earlier, sel[:, 0, :])
                    mm(ps[:, 1, 8:16], earlier, sel[:, 1, :], stop=False)
                    mm(ps[:, 1, 8:16], ones, sel[:, 0, :], start=False)
                    mm(ps[:, 1, 16:24], ones, sel[:, 0, :], stop=False)
                    mm(ps[:, 1, 16:24], ones, sel[:, 1, :], start=False).then_inc(*pe.step("ranks psum"))
                    experts()

        @block.scalar
        def _(a):
            act = Engine("act", sems, steps)
            fn = nc.scalar.activation

            def rms(L, which, n):
                if L == 0 and which == "mix":
                    a.wait_ge(x_loaded, 16)
                else:
                    a.wait_ge(*act.at(f"{L} x ready {which} {n}"))
                a.wait_ge(*act.last())
                fn(V("act")[:, 0:D], x[:, n, :], ACT.Square, accum_out=sm("ss", n)).then_inc(*act.step(f"{L} {which} ss {n}"))
                a.wait_ge(*act.at(f"{L} {which} ss mean {n}"))
                a.wait_ge(*act.last())
                fn(sm("sq", n), sm("v", n), ACT.Sqrt).then_inc(*act.step(f"{L} {which} root {n}"))

            def hidden(L, which):
                for c in range(0, KD, 1 if (L, which) == (0, "ffn") else 2):
                    a.wait_ge(*act.at(f"{L} {which} hT psum {c}"))
                    fn(hTr[:, 0, c, :] if (L, which) == (0, "ffn") else hT[:, c, :], ps[:, c, 0:S], ACT.Copy,
                       scale=col("mix_pre" if which == "mix" else "ffn_pre", c)).then_inc(*act.step(f"{L} {which} hT {c}"))

            def high(tag, name, k, i=None):
                if tag == "moe":
                    if i is None:
                        a.wait_ge(*filled_of_pass(k, 0))
                    else:
                        a.wait_ge(*filled_of_pass(k, i))
                    source = unit(k % UNITS)
                else:
                    a.wait_ge(*filled("ffn", 0, k))
                    source = unit(place("ffn", 0, k))
                q, back = before(k, SPLIT_PLACE)
                if act.part == "loop" or back == 0:
                    a.wait_ge(*act.at(f"{tag} used {q}", back=back if k >= AHEAD else 0))
                fn(split[:, SPLIT_PLACE[k], 0, :], source, ACT.Copy).then_inc(
                    *act.step(f"{name} high {k}"))

            def ffn(tag, tiles, i=None):
                parts, loop = CHUNKS * tiles, act.part == "loop"

                if loop:
                    fn(sm("fr", 0, 1), sm("fr", 0, 1), ACT.Silu).then_inc(*act.step())
                for k in range(NUSES):
                    chunk, third = USES[k]
                    for n in range(tiles if third == 1 else 0):
                        p = chunk * tiles + n
                        a.wait_ge(*act.at(f"{tag} gate_up {p}"))
                        if p >= 2:
                            a.wait_ge(*act.at(f"{tag} act {p - 2}"))
                        elif loop:
                            a.wait_ge(*act.at(f"{tag} act {parts - 1}", back=1))
                        fn(act_buf[:, 2 + p % 2, :], ps[:, p % 2, 0:FC], ACT.Silu).then_inc(*act.step(f"{tag} silu {p}"))
                    for n in range(tiles if k in turn_before else 0):
                        p = turn_before[k] * tiles + n
                        a.wait_ge(*act.at(f"{tag} turned {p}"))
                        if p >= 2:
                            a.wait_ge(*act.at(f"{tag} down {p - 2}"))
                        elif loop:
                            a.wait_ge(*act.at(f"{tag} down {parts - 1}", back=1))
                        fn(actTr[:, p % 2, 0, :, :], ps[:, 2 + p % 2, 0:2 * P].rearrange("p (a b) -> p a b", a=2),
                           ACT.Copy).then_inc(*act.step(f"{tag} actT high {p}"))
                    if loop and k == GATED_TURNED:
                        a.wait_ge(*act.at("moe gated turned"))
                        a.wait_ge(*act.at("moe scattered 3"))
                        fn(gatedT, ps[:, 6, 0:2 * P].rearrange("p (a b) -> p a b", a=2), ACT.Copy
                           ).then_inc(*act.step("moe gatedT"))
                    if loop and k == LAST_GATE_UP + 1:
                        a.wait_ge(*act.at("moe hTe 1"))
                        a.wait_ge(*act.at(f"moe used {LAST_GATE_UP}"))
                        fn(hTr[:, 0, :, 0:P], hTe, ACT.Copy).then_inc(*act.step("moe hT high"))
                    for u in splits_after[k]:
                        if u < NUSES:
                            high(tag, tag, u, i)
                        elif loop:
                            high(tag, tag, u - NUSES, i + 1)

            def projected(L, f, bank):
                a.wait_ge(*act.at(f"{L} proj psum {f}"))
                dst = pT[:, f, 1:257] if f < 11 else uT[:, f - 11, :] if f < 13 else qkT[:, f - 13, :]
                fn(dst, ps[:, bank, 0:S], ACT.Copy).then_inc(*act.step(f"{L} proj {f}"))

            def softmax(L, n):
                sprob = V("s", 6, (n + 1) * P)
                a.wait_ge(*act.at(f"{L} max {n}"))
                for h in range(6):
                    fn(sprob[:, h, :], sprob[:, h, :], ACT.Exp, bias=sm("rmax", 6 * n + h),
                       accum_out=sm("rsum", 6 * n + h)).then_inc(*act.step(f"{L} probs {n}" if h == 5 else None))

            def probs_turned(L, n, banks):
                PT = V("PT", 3, 4, P)
                if n:
                    a.wait_ge(*act.at(f"{L} o psum 0"))
                for k, m in enumerate(banks):
                    a.wait_ge(*act.at(f"{L} PT psum {n} {m}"))
                    w = 4 if n or k == 0 else 2
                    fn(PT[:, k, 0:w, :], ps[:, m, 0:w * P].rearrange("p (a b) -> p a b", a=w), ACT.Copy
                       ).then_inc(*act.step(f"{L} PT {n} {m}"))

            def out_turned(L, n, bank):
                a.wait_ge(*act.at(f"{L} oT psum {n}"))
                for q in range(3):
                    fn(hT[:, 5 + q, n * P:(n + 1) * P], ps[:, bank, q * P:(q + 1) * P], ACT.Copy,
                       scale=col("attn_norm", q)).then_inc(*act.step(f"{L} oT {n}" if q == 2 else None))

            for L in range(LAYERS):
                for n in range(NT if L == 0 else 0):
                    rms(L, "mix", n)
                a.wait_ge(params_loaded, 96 * (L + 1))
                hidden(L, "mix")
                a.wait_ge(*act.last())
                fn(sm("lr", 0, 8), col("log_step"), ACT.Exp).then_inc(*act.step(f"{L} step"))
                a.wait_ge(*act.at(f"{L} half angle"))
                a.wait_ge(*act.last())
                fn(sm("sn", 0, 8), sm("t1", 0, 8), ACT.Sin).then_inc(*act.step())
                a.wait_ge(*act.at(f"{L} half co-angle"))
                a.wait_ge(*act.last())
                fn(sm("cs", 0, 8), sm("t2", 0, 8), ACT.Sin).then_inc(*act.step(f"{L} sines"))
                a.wait_ge(*act.at(f"{L} log r"))
                a.wait_ge(*act.last())
                fn(sm("r", 0, 8), sm("r", 0, 8), ACT.Exp).then_inc(*act.step(f"{L} r"))
                for f in (11, 13, 15, 17):
                    projected(L, f, f - 11)
                a.wait_ge(*act.at(f"{L} vA psum 0"))
                a.wait_ge(*act.last())
                fn(vA[:, 0, :], ps[:, 3, 0:384], ACT.Copy).then_inc(*act.step(f"{L} vA 0"))
                softmax(L, 0)
                projected(L, 9, 6)
                projected(L, 10, 7)
                probs_turned(L, 0, [6, 7])
                projected(L, 3, 6)
                softmax(L, 1)
                projected(L, 4, 0)
                probs_turned(L, 1, [2, 3, 0])
                projected(L, 5, 2)
                projected(L, 0, 0)
                projected(L, 1, 2)
                projected(L, 2, 2)
                projected(L, 6, 2)
                projected(L, 7, 4)
                projected(L, 8, 5)
                for n in range(NT):
                    a.wait_ge(*act.at(f"{L} o {n}"))
                    a.wait_ge(*act.last())
                    fn(V("act")[:, 0:384], V("aO", 2, 384)[:, n, :], ACT.Square, accum_out=sm("ss", n)
                       ).then_inc(*act.step(f"{L} o ss {n}"))
                a.wait_ge(*act.at(f"{L} o ss mean"))
                a.wait_ge(*act.last())
                fn(sm("sq"), sm("v"), ACT.Sqrt).then_inc(*act.step(f"{L} o root"))
                out_turned(L, 0, 6)
                out_turned(L, 1, 2)
                a.wait_ge(*act.at(f"{L} gelu in"))
                a.wait_ge(*act.last())
                fn(V("z1")[:, 0:512], V("z1")[:, 0:512], ACT.Tanh, scale=GELU_C).then_inc(*act.step(f"{L} gelu tanh"))
                a.wait_ge(*act.at(f"{L} shifted 9"))
                a.wait_ge(*act.last())
                fn(pm[0:64, 9, :], pm[0:64, 9, :], ACT.Tanh).then_inc(*act.step(f"{L} w_lo tanh"))
                a.wait_ge(*act.at(f"{L} shifted 10"))
                a.wait_ge(*act.last())
                fn(pm[:, 10, :], pm[:, 10, :], ACT.Tanh, scale=0.5).then_inc(*act.step(f"{L} g_lo tanh"))
                a.wait_ge(*act.at(f"{L} halved"))
                for q in range(3):
                    a.wait_ge(*act.at(f"{L} decay psum {q}"))
                    a.wait_ge(*act.last())
                    fn(V("lw", 3, S)[:, q, :], ps[:, q, 0:S], ACT.Tanh, scale=0.5, bias=sm("half", q)).then_inc(*act.step(f"{L} decay {q}"))
                for q in range(3):
                    a.wait_ge(*act.at(f"{L} rate psum {q}"))
                    a.wait_ge(*act.last())
                    fn(V("a", 3, S)[:, q, :], ps[:, 3 + q, 0:S], ACT.Tanh, scale=0.5, bias=sm("half", 3 + q)).then_inc(*act.step(f"{L} rate {q}"))
                a.wait_ge(*act.at(f"{L} g psum"))
                a.wait_ge(*act.last())
                fn(V("g"), ps[:, 6:8, :].rearrange("p a b -> p (a b)")[:, 0:768], ACT.Copy).then_inc(*act.step(f"{L} g"))
                a.wait_ge(*act.at(f"{L} kk"))
                a.wait_ge(*act.last())
                fn(V("e2"), V("kkn"), ACT.Square).then_inc(*act.step(f"{L} kk squared"))
                a.wait_ge(*act.at(f"{L} c centred"))
                a.wait_ge(*act.last())
                fn(V("e1"), V("c"), ACT.Exp).then_inc(*act.step(f"{L} grown"))
                a.wait_ge(*act.at(f"{L} glu psum"))
                for m in range(2):
                    a.wait_ge(*act.last())
                    fn(V("z2", 2, S)[:, m, :], ps[:, 2, m * S:(m + 1) * S], ACT.Tanh, scale=0.5,
                                bias=sm("half", 6 + m)).then_inc(*act.step(f"{L} glu" if m else None))
                a.wait_ge(*act.at(f"{L} s5 y"))
                a.wait_ge(*act.last())
                fn(V("z1")[:, 0:512], V("z0")[:, 0:512], ACT.Square).then_inc(*act.step(f"{L} s5 squared"))
                a.wait_ge(*act.at(f"{L} kk sum out"))
                a.wait_ge(*act.last())
                fn(V("e2"), V("e2"), ACT.Sqrt).then_inc(*act.step(f"{L} kk root"))
                a.wait_ge(*act.at(f"{L} s5 var"))
                a.wait_ge(*act.last())
                fn(V("z1")[:, 512:768], V("z1")[:, 512:768], ACT.Sqrt).then_inc(*act.step(f"{L} s5 root"))
                a.wait_ge(*act.at(f"{L} r~"))
                a.wait_ge(*act.last())
                fn(V("e1"), V("lw"), ACT.Exp).then_inc(*act.step(f"{L} grown before"))
                a.wait_ge(*act.at(f"{L} b k"))
                a.wait_ge(*act.last())
                fn(V("e2"), V("c"), ACT.Exp, scale=-1.0).then_inc(*act.step(f"{L} shrunk"))
                a.wait_ge(*act.at(f"{L} dec sum"))
                a.wait_ge(*act.last())
                fn(sm("dec"), sm("dec"), ACT.Exp).then_inc(*act.step(f"{L} dec"))
                a.wait_ge(*act.at(f"{L} E"))
                for k in range(3):
                    for n in range(NT):
                        a.wait_ge(*act.at(f"{L} natural psum {k} {n}"))
                        a.wait_ge(*act.last())
                        fn(natural[:, k, n, :], ps[:, (4 + 2 * k + n) % 8, 0:384], ACT.Copy).then_inc(*act.step(f"{L} natural {k} {n}"))
                for lv in range(LEVELS):
                    for n in range(NT):
                        a.wait_ge(*act.at(f"{L} Pm psum {lv} {n}"))
                        if lv >= 1:
                            a.wait_ge(*act.at(f"{L} TT psum {lv - 1} {n}")) if lv > 1 else None
                        a.wait_ge(*act.last())
                        fn(V("Pm", 2, 768)[:, n, :],
                                    ps[:, 4 * n:4 * n + 2, :].rearrange("p a b -> p (a b)")[:, 0:768], ACT.Copy).then_inc(*act.step(f"{L} Pm {lv} {n}"))
                for n in range(NT):
                    a.wait_ge(*act.at(f"{L} rhs psum {n}"))
                    a.wait_ge(*act.last())
                    fn(V("rhs"), ps[:, 2, 0:384], ACT.Copy).then_inc(*act.step(f"{L} rhs {n}"))
                    a.wait_ge(*act.at(f"{L} sa psum {n}"))
                    a.wait_ge(*act.last())
                    fn(V("sa"), ps[:, 3, 0:384], ACT.Copy).then_inc(*act.step(f"{L} sa {n}"))
                    a.wait_ge(*act.at(f"{L} OT psum {n}"))
                    a.wait_ge(*act.last())
                    fn(V("OT", 3, NT, P)[:, :, n, :], ps[:, 6, 0:384].rearrange("p (a b) -> p a b", a=3),
                                ACT.Copy).then_inc(*act.step(f"{L} OT {n}"))
                a.wait_ge(*act.at(f"{L} centred"))
                a.wait_ge(*act.last())
                fn(V("o2"), V("o1"), ACT.Square).then_inc(*act.step(f"{L} o squared"))
                a.wait_ge(*act.at(f"{L} gn var"))
                a.wait_ge(*act.last())
                fn(V("o2"), V("o2"), ACT.Sqrt).then_inc(*act.step(f"{L} gn root"))
                a.wait_ge(*act.at(f"{L} mixing over"))
                for k in range(AHEAD - 1):
                    high(("ffn", "moe")[L], ("ffn", "first")[L], k)
                for n in range(NT):
                    a.wait_ge(*act.at(f"{L} out psum {n}"))
                    a.wait_ge(*act.last())
                    fn(V("act")[:, 0:D], ps[:, 4 * n:4 * n + 2, :].rearrange("p a b -> p (a b)"),
                                ACT.Square, accum_out=sm("ss", n)).then_inc(*act.step(f"{L} post square {n}"))
                    a.wait_ge(*act.at(f"{L} post ss mean {n}"))
                    a.wait_ge(*act.last())
                    fn(sm("sq", n), sm("v", n), ACT.Sqrt).then_inc(*act.step(f"{L} post root {n}"))
                    rms(L, "ffn", n)
                high(("ffn", "moe")[L], ("ffn", "first")[L], AHEAD - 1)
                hidden(L, "ffn")
                if L == 0:
                    ffn("ffn", NT)
                else:
                    a.wait_ge(*act.at("gate in"))
                    a.wait_ge(*act.last())
                    fn(sm("g1"), sm("g1"), ACT.Exp).then_inc(*act.step("gate exp"))
                    a.wait_ge(*act.at("lg shifted"))
                    a.wait_ge(*act.last())
                    fn(sm("lg"), sm("lg"), ACT.Exp).then_inc(*act.step("lg exp"))
                    a.wait_ge(*act.at("first hTe 1"))
                    a.wait_ge(*act.last())
                    fn(hTr[:, 0, :, 0:P], hTe, ACT.Copy).then_inc(*act.step("first hT high"))
                    a.wait_ge(*act.at("passes"))
                    total = a.value_load(passes[:, 16:17], min_val=EXPERTS, max_val=EXPERTS + MORE)
                    with a.Fori(0, total) as i:
                        act.enter(i)
                        ffn("moe", 1, i)
                        a.wait_ge(*act.at(f"moe down {CHUNKS - 1}"))
                        a.wait_ge(*act.at("moe scattered 3"))
                        a.wait_ge(*act.last())
                        fn(y_sb, ps[:, 4:6, :].rearrange("p a b -> p (a b)"), ACT.Copy
                           ).then_inc(*act.step("moe y taken"))
                    act.leave(total)
                for n in range(NT):
                    if L == 0:
                        a.wait_ge(*act.at(f"ffn down {NT * (CHUNKS - 1) + n}"))
                    else:
                        a.wait_ge(*act.at(f"1 f ready {n}"))
                    a.wait_ge(*act.last())
                    fn(V("act")[:, 0:D], ffn_out(L, n), ACT.Square, accum_out=sm("ss", n)
                       ).then_inc(*act.step(f"{L} fpost square {n}"))
                    a.wait_ge(*act.at(f"{L} fpost ss mean {n}"))
                    a.wait_ge(*act.last())
                    fn(sm("sq", n), sm("v", n), ACT.Sqrt).then_inc(*act.step(f"{L} fpost root {n}"))
                    if L < LAYERS - 1:
                        rms(L + 1, "mix", n)

        @block.vector
        def _(v):
            dve = Engine("dve", sems, steps)
            ve = nc.vector

            def tt(out, a0, a1, op, step=None):
                v.wait_ge(*dve.last())
                ve.tensor_tensor(out, a0, a1, op).then_inc(*dve.step(step))

            def ts(out, a0, s1, s2, op0, op1=None, step=None):
                v.wait_ge(*dve.last())
                (ve.tensor_scalar(out, a0, s1, s2, op0, op1) if op1 is not None
                         else ve.tensor_scalar(out, a0, s1, None, op0)).then_inc(*dve.step(step))

            def stt(out, a0, s, a1, op0, op1, step=None):
                v.wait_ge(*dve.last())
                ve.scalar_tensor_tensor(out=out, in0=a0, scalar=s, in1=a1, op0=op0, op1=op1).then_inc(*dve.step(step))

            def rstd(L, what, ssname, rootname, width, n=None):
                for s in ssname:
                    v.wait_ge(*dve.at(s))
                s = (lambda k: sm(k)) if n is None else (lambda k: sm(k, n))
                ts(s("v"), s("ss"), 1.0 / width, EPS, ALU.mult, ALU.add, what)
                v.wait_ge(*dve.at(rootname))
                v.wait_ge(*dve.last())
                ve.reciprocal(s("rstd"), s("sq")).then_inc(*dve.step())

            def normed(L, which, n):
                rstd(L, f"{L} {which} ss mean {n}", [f"{L} {which} ss {n}"], f"{L} {which} root {n}", D, n)
                ts(hn[:, n, :], x[:, n, :], sm("rstd", n), None, ALU.mult, None, f"{L} {which} hn {n}")

            def hidden(L, which):
                for c in range(1, KD, 2):
                    v.wait_ge(*dve.at(f"{L} {which} hT psum {c}"))
                    ts(hT[:, c, :], ps[:, c, 0:S], col("mix_pre" if which == "mix" else "ffn_pre", c), None, ALU.mult,
                       None, f"{L} {which} hT {c}")

            def table(L):
                th, st, r = sm("theta", 0, 8), sm("lr", 0, 8), sm("r", 0, 8)
                sn, cs, t0, t1, t2 = (sm(k, 0, 8) for k in ("sn", "cs", "t0", "t1", "t2"))
                v.wait_ge(*dve.at(f"{L} step"))
                tt(th, col("a_im"), st, ALU.mult)
                ts(t0, th, 1.0 / TWO_PI, ROUND, ALU.mult, ALU.add)
                ts(t0, t0, ROUND, None, ALU.subtract)
                stt(th, t0, -TWO_PI_HI, th, ALU.mult, ALU.add)
                stt(th, t0, -TWO_PI_LO, th, ALU.mult, ALU.add)
                ts(t1, th, 0.5, None, ALU.mult, None, f"{L} half angle")
                ts(t2, t1, -1.0, None, ALU.mult)
                tt(t2, t1, t2, ALU.max)
                ts(t2, t2, -1.0, TWO_PI / 4, ALU.mult, ALU.add, f"{L} half co-angle")
                ts(t0, col("a_re"), -1e-4, None, ALU.min)
                tt(r, t0, st, ALU.mult, f"{L} log r")
                v.wait_ge(*dve.at(f"{L} sines"))
                tt(t1, sn, sn, ALU.mult)
                stt(sn, sn, 2.0, cs, ALU.mult, ALU.mult)
                ts(cs, t1, -2.0, 1.0, ALU.mult, ALU.add)
                v.wait_ge(*dve.at(f"{L} r"))
                are, aim, fr, fi, u0, u1 = t0, col("a_im"), sm("fr"), sm("fi"), sm("u0"), sm("u1")
                tt(u0, r, cs, ALU.mult)
                ts(u0, u0, 1.0, None, ALU.subtract)
                tt(u1, r, sn, ALU.mult)
                tt(fr, u0, are, ALU.mult)
                tt(t1, u1, aim, ALU.mult)
                tt(fr, fr, t1, ALU.add)
                tt(fi, u1, are, ALU.mult)
                tt(t1, u0, aim, ALU.mult)
                tt(fi, fi, t1, ALU.subtract)
                tt(t1, are, are, ALU.mult)
                tt(t2, aim, aim, ALU.mult)
                tt(t1, t1, t2, ALU.add)
                v.wait_ge(*dve.last())
                ve.reciprocal(t1, t1).then_inc(*dve.step())
                tt(fr, fr, t1, ALU.mult)
                tt(fi, fi, t1, ALU.mult)
                cb = V("c_blk", 2, 8, 32)
                s0, s1, s2 = (V("natural")[:, k * 256:(k + 1) * 256].rearrange("p (a b) -> p a b", a=8)
                              for k in range(3))
                tt(s0, cb[:, 0], bc(fi, 32), ALU.mult)
                tt(s1, cb[:, 1], bc(fi, 32), ALU.mult)
                tt(s2, cb[:, 0], bc(fr, 32), ALU.mult)
                tt(cb[:, 0], s2, s1, ALU.subtract)
                tt(s1, cb[:, 1], bc(fr, 32), ALU.mult)
                stt(cb[:, 1], s1, -1.0, s0, ALU.mult, ALU.subtract, f"{L} c scaled")

            def low(tag, name, k):
                source = unit(place("ffn", 0, k) if tag == "ffn" else k % UNITS)
                v.wait_ge(*dve.at(f"{name} high {k}"))
                tt(split[:, SPLIT_PLACE[k], 1, :], source, split[:, SPLIT_PLACE[k], 0, :], ALU.subtract,
                   f"{name} split {k}")
                steps.at[f"{tag} 0 {k} read"] = ("dve", dve.count, dve.part)

            def ffn(tag, tiles, at_use):
                parts, loop = CHUNKS * tiles, dve.part == "loop"

                for k in range(NUSES):
                    chunk, third = USES[k]
                    for n in range(tiles if third == 1 else 0):
                        p = chunk * tiles + n
                        v.wait_ge(*dve.at(f"{tag} silu {p}"))
                        if p >= 2:
                            v.wait_ge(*dve.at(f"{tag} turned {p - 2}"))
                        elif loop:
                            v.wait_ge(*dve.at(f"{tag} turned {parts - 1}", back=1))
                        tt(act_buf[:, p % 2, :], act_buf[:, 2 + p % 2, :], ps[:, p % 2, FC:2 * FC], ALU.mult,
                           f"{tag} act {p}")
                    for n in range(tiles if k in turn_before else 0):
                        p = turn_before[k] * tiles + n
                        v.wait_ge(*dve.at(f"{tag} actT high {p}"))
                        tt(actTr[:, p % 2, 1, :, :], ps[:, 2 + p % 2, 0:2 * P].rearrange("p (a b) -> p a b", a=2),
                           actTr[:, p % 2, 0, :, :], ALU.subtract, f"{tag} actT {p}")
                    at_use(k)
                    for u in splits_after[k]:
                        if u < NUSES or loop:
                            low(tag, tag, u % NUSES)

            def dispatch(i, name):
                for n in range(NT):
                    at = slot_of[:, n, bass.ds(i, 1)] if dve.part == "loop" else slot_of[:, n, i:i + 1]
                    gate = gate_of[:, n, bass.ds(i, 1)] if dve.part == "loop" else gate_of[:, n, i:i + 1]
                    ts(disp[:, n, :], C("iota"), at, None, ALU.is_equal, None)
                    ts(gated[:, n, :], C("iota"), at, gate, ALU.is_equal, ALU.mult, name)

            def gathered(tag):
                for b in range(2):
                    v.wait_ge(*dve.at(f"{tag} gathered {b}"))
                    tt(hTe[:, 4 * b:4 * b + 4, :], ps[:, 6 + b, :].rearrange("p (c t) -> p c t", c=4),
                       bc(col("ffn_pre")[:, 4 * b:4 * b + 4], P), ALU.mult, f"{tag} hTe {b}")

            def route():
                for name, value in (("ffn_sum", 0.0), ("y", 0.0), ("gatedT", 0.0), ("slot_of", -1.0), ("gate_of", 0.0)):
                    v.wait_ge(*dve.last())
                    ve.memset(V(name), value).then_inc(*dve.step("no outputs"))
                v.wait_ge(*dve.at("logits psum"))
                lg, lg3 = sm("lg"), sm("lg").rearrange("p (n e) -> p n e", n=NT)
                v.wait_ge(*dve.last())
                ve.tensor_copy(lg, ps[:, 0, 0:16]).then_inc(*dve.step("logits"))
                for n in range(NT):
                    v.wait_ge(*dve.last())
                    ve.max(sm("m8", 8 * n, 8), sm("lg", 8 * n, 8)).then_inc(*dve.step())
                m8 = sm("m8").rearrange("p (n e) -> p n e", n=NT)
                second = m8[:, :, 1:2].to_broadcast([P, NT, EXPERTS])
                sel, eq, cum, prod = (V(k, NT, EXPERTS) for k in ("sel", "eq", "cum", "prod"))
                pick = V("pick")
                tt(sel, lg3, second, ALU.is_gt)
                tt(eq, lg3, second, ALU.is_equal)
                v.wait_ge(*dve.last())
                ve.tensor_reduce(pick, sel, AX.X, ALU.add).then_inc(*dve.step())
                for n in range(NT):
                    v.wait_ge(*dve.last())
                    ve.tensor_tensor_scan(cum[:, n, :], ones[:, 0:8], eq[:, n, :], 0.0, ALU.mult, ALU.add
                                          ).then_inc(*dve.step())
                tt(cum, cum, bc(pick, EXPERTS), ALU.add)
                stt(eq, cum, 2.0, eq, ALU.is_le, ALU.mult)
                tt(sel, sel, eq, ALU.add, "sel")
                tt(sm("g1"), m8[:, :, 1], m8[:, :, 0], ALU.subtract, "gate in")
                tt(lg3, lg3, m8[:, :, 0:1].to_broadcast([P, NT, EXPERTS]), ALU.subtract, "lg shifted")
                v.wait_ge(*dve.at("gate exp"))
                ts(sm("g1"), sm("g1"), 1.0, None, ALU.add)
                v.wait_ge(*dve.last())
                ve.reciprocal(sm("g1"), sm("g1")).then_inc(*dve.step())
                v.wait_ge(*dve.at("lg exp"))
                tt(lg3, lg3, bc(sm("g1"), EXPERTS), ALU.mult)
                tt(lg3, lg3, sel, ALU.mult)
                v.wait_ge(*dve.at("ranks psum"))
                v.wait_ge(*dve.last())
                ve.tensor_copy(V("rank"), ps[:, 1, 0:24]).then_inc(*dve.step("ranks"))
                rank, count = V("rank")[:, 0:16].rearrange("p (n e) -> p n e", n=NT), V("rank")[:, 16:24]
                stt(rank, rank, 1.0, sel, ALU.add, ALU.mult)
                ts(slot_of[:, :, 0:EXPERTS], rank, 1.0, None, ALU.subtract)
                v.wait_ge(*dve.last())
                ve.tensor_copy(gate_of[:, :, 0:EXPERTS], lg3).then_inc(*dve.step())
                dispatch(0, "disp built")
                over, order, onehot = V("over"), V("order"), V("onehot")
                iota8 = C("iota")[:, 0:EXPERTS]
                ids, total = sm("m8"), sm("total")
                ts(over, count, float(P), None, ALU.is_gt)
                v.wait_ge(*dve.last())
                ve.tensor_tensor_scan(order, ones[:, 0:8], over, 0.0, ALU.mult, ALU.add).then_inc(*dve.step())
                ts(total, order[:, 7:8], float(EXPERTS), None, ALU.add)
                v.wait_ge(*dve.last())
                ve.memset(ids, 0.0).then_inc(*dve.step())
                v.wait_ge(*dve.last())
                ve.tensor_copy(ids[:, 0:EXPERTS], iota8).then_inc(*dve.step())
                for m in range(MORE):
                    stt(onehot, order, float(m + 1), over, ALU.is_equal, ALU.mult)
                    tt(V("prod")[:, 0:8], onehot, iota8, ALU.mult)
                    v.wait_ge(*dve.last())
                    ve.tensor_reduce(ids[:, EXPERTS + m:EXPERTS + m + 1], V("prod")[:, 0:8], AX.X, ALU.add
                                     ).then_inc(*dve.step())
                    hot = onehot.unsqueeze(1).to_broadcast([P, NT, EXPERTS])
                    stt(prod, rank, float(P), hot, ALU.subtract, ALU.mult)
                    v.wait_ge(*dve.last())
                    ve.tensor_reduce(pick, prod, AX.X, ALU.add).then_inc(*dve.step())
                    ts(slot_of[:, :, EXPERTS + m], pick, 1.0, None, ALU.subtract)
                    tt(prod, gate_of[:, :, 0:EXPERTS], hot, ALU.mult)
                    v.wait_ge(*dve.last())
                    ve.tensor_reduce(gate_of[:, :, EXPERTS + m], prod, AX.X, ALU.add).then_inc(*dve.step())
                v.wait_ge(*dve.last())
                ve.tensor_copy(passes[:, 0:16], ids[0:1, :]).then_inc(*dve.step())
                v.wait_ge(*dve.last())
                ve.tensor_copy(passes[:, 16:17], total[0:1, :]).then_inc(*dve.step("passes"))

            def hT_low(name):
                v.wait_ge(*dve.at(f"{name} hT high"))
                tt(hTr[:, 1, :, 0:P], hTe, hTr[:, 0, :, 0:P], ALU.subtract, f"{name} hT low")

            def summed(tag, which):
                for q in which:
                    n, h = q // 2, q % 2
                    v.wait_ge(*dve.at(f"{tag} scattered {q}"))
                    part = ffn_sum[:, n, h * 512:(h + 1) * 512]
                    tt(part, part, ps[:, 4 + q, :], ALU.add, f"{tag} summed {q}")

            def experts():
                gathered("first")
                hT_low("first")
                total = v.value_load(passes[:, 16:17], min_val=EXPERTS, max_val=EXPERTS + MORE)
                with v.Fori(0, total) as i:
                    dve.enter(i)

                    def at_use(k):
                        if 2 <= k < 6:
                            summed("moe", [k - 2])
                        if k == GATED_TURNED:
                            v.wait_ge(*dve.at("moe gated turned"))
                            dispatch(i + 1, "moe disp built")
                        if USES[k] == (GATHER - 2, 2):
                            gathered("moe")
                        if k == LAST_GATE_UP + 1:
                            hT_low("moe")

                    ffn("moe", 1, at_use)
                dve.leave(total)

            def rotated(L, H):
                Er, Ei = E[:, 0, 4 * H:4 * H + 4, :], E[:, 1, 4 * H:4 * H + 4, :]
                z = [V(f"z{i}", 4, S) for i in range(5)]
                v.wait_ge(*dve.at(f"{L} bu {H}"))
                if H:
                    v.wait_ge(*dve.at(f"{L} y psum 0"))
                br, bi = ps[:, 4:8, 0:S], ps[:, 4:8, S:2 * S]
                tt(z[0], br, Er, ALU.mult)
                tt(z[1], bi, Ei, ALU.mult)
                tt(z[2], bi, Er, ALU.mult)
                tt(z[3], br, Ei, ALU.mult, f"{L} bu {H} read")
                tt(z[0], z[0], z[1], ALU.add)
                tt(z[2], z[2], z[3], ALU.subtract)
                for i in range(4):
                    rr = sm("r", 4 * H + i).to_broadcast([P, S])
                    v.wait_ge(*dve.last())
                    ve.tensor_tensor_scan(z[1][:, i, :], rr, z[0][:, i, :], 0.0, ALU.mult, ALU.add).then_inc(*dve.step())
                    v.wait_ge(*dve.last())
                    ve.tensor_tensor_scan(z[3][:, i, :], rr, z[2][:, i, :], 0.0, ALU.mult, ALU.add).then_inc(*dve.step())
                tt(z[0], z[1], Er, ALU.mult)
                tt(z[2], z[3], Ei, ALU.mult)
                tt(z[0], z[0], z[2], ALU.subtract)
                tt(z[2], z[3], Er, ALU.mult)
                tt(z[4], z[1], Ei, ALU.mult)
                tt(z[2], z[2], z[4], ALU.add, f"{L} s5 x {H}")

            def scored(L, n):
                keys, bias = (n + 1) * P, V("bias", 6, 384)
                sprob = V("s", 6, keys)
                v.wait_ge(*dve.at(f"{L} scores {n}"))
                if n:
                    v.wait_ge(*dve.at(f"{L} PT psum 0 7"))
                stt(sprob, ps[:, 0:6, 0:keys], 0.125, bias[:, :, (1 - n) * P:(1 - n) * P + keys],
                    ALU.mult, ALU.add, f"{L} scores {n} out")
                v.wait_ge(*dve.last())
                ve.memset(sprob[0:64, :, keys - 64:keys], -3.0e38).then_inc(*dve.step())
                v.wait_ge(*dve.last())
                ve.tensor_reduce(sm("rmax", 6 * n, 6), sprob, AX.X, ALU.max).then_inc(*dve.step())
                ts(sm("rmax", 6 * n, 6), sm("rmax", 6 * n, 6), -1.0, None, ALU.mult, None, f"{L} max {n}")

            def attended(L, n):
                v.wait_ge(*dve.at(f"{L} probs {n}"))
                v.wait_ge(*dve.last())
                ve.reciprocal(sm("rinv", 6 * n, 6), sm("rsum", 6 * n, 6)).then_inc(*dve.step())
                v.wait_ge(*dve.at(f"{L} o psum {n}"))
                aO = V("aO", 2, 3, 2, 64)
                for par in range(2):
                    tt(aO[:, n, :, par, :], ps[:, (1, 3)[n], 0:384].rearrange("p (a b c) -> p a b c", a=3, b=2)[:, :, par, :],
                       bc(sm("rinv", 6 * n + 3 * par, 3), 64), ALU.mult, f"{L} o {n}")

            for L in range(LAYERS):
                for n in range(NT if L == 0 else 0):
                    normed(L, "mix", n)
                v.wait_ge(params_loaded, 96 * (L + 1))
                hidden(L, "mix")
                table(L)
                v.wait_ge(*dve.last())
                ve.memset(pT[:, :, 0:1], 0.0).then_inc(*dve.step())
                for f in (12, 14, 16, 18):
                    v.wait_ge(*dve.at(f"{L} proj psum {f}"))
                    dst = uT[:, f - 11, :] if f < 13 else qkT[:, f - 13, :]
                    v.wait_ge(*dve.last())
                    ve.tensor_copy(dst, ps[:, f - 11, 0:S]).then_inc(*dve.step(f"{L} proj {f}"))
                v.wait_ge(*dve.at(f"{L} vA psum 1"))
                v.wait_ge(*dve.last())
                ve.tensor_copy(vA[:, 1, :], ps[:, 4, 0:384]).then_inc(*dve.step(f"{L} vA 1"))
                v.wait_ge(bias_loaded, 16 * (L + 1))
                scored(L, 0)
                scored(L, 1)
                v.wait_ge(*dve.at(f"{L} E"))
                rotated(L, 0)
                attended(L, 0)
                attended(L, 1)
                rotated(L, 1)
                rstd(L, f"{L} o ss mean", [f"{L} o ss {n}" for n in range(NT)], f"{L} o root", 384)
                for n in range(NT):
                    ts(V("aO", 2, 384)[:, n, :], V("aO", 2, 384)[:, n, :], sm("rstd", n), None, ALU.mult, None,
                       f"{L} o normed {n}")
                for H in range(2):
                    v.wait_ge(*dve.at(f"{L} y psum {H}"))
                    stt(uT[:, H, :], uT[:, H, :], col("s5_d", H), ps[:, H, 0:S], ALU.mult, ALU.add, f"{L} y0 {H}")
                y, w1, w2 = V("z0")[:, 0:512], V("z1")[:, 0:512], V("z2")[:, 0:512]
                u, var = V("uT"), V("z1")[:, 512:768]
                tt(w1, u, u, ALU.mult)
                ts(w1, w1, 0.044715, 1.0, ALU.mult, ALU.add)
                tt(w1, w1, u, ALU.mult, f"{L} gelu in")
                for f in (9, 10, 3, 4, 5):
                    v.wait_ge(*dve.at(f"{L} proj {f}"))
                    tt(pm[:, f, :], pT[:, f, 0:256], pT[:, f, 1:257], ALU.subtract)
                    stt(pm[:, f, :], pm[:, f, :], col("mu", f), pT[:, f, 1:257], ALU.mult, ALU.add,
                        f"{L} shifted {f}")
                ts(sm("half", 0, 3), col("w0"), 0.5, None, ALU.mult)
                ts(sm("half", 3, 3), col("a0"), 0.5, None, ALU.mult)
                ts(sm("half", 6, 2), col("b_glu"), 0.5, None, ALU.mult, None, f"{L} halved")
                v.wait_ge(*dve.at(f"{L} gelu tanh"))
                stt(y, w1, 1.0, u, ALU.add, ALU.mult)
                ts(y, y, 0.5, None, ALU.mult, None, f"{L} gelu")
                v.wait_ge(*dve.at(f"{L} g_lo tanh"))
                ts(pm[:, 10, :], pm[:, 10, :], 0.5, 0.5, ALU.mult, ALU.add, f"{L} g_lo sigmoid")
                kkn, e1, e2, a_, lw, c = (V(k, 3, S) for k in ("kkn", "e1", "e2", "a", "lw", "c"))
                flat = {k: V(k) for k in ("kkn", "e1", "e2", "a", "lw", "c", "kh", "bh")}
                r_, k_ = pm[:, 0:3, :], pm[:, 3:6, :]
                v.wait_ge(*dve.at(f"{L} shifted 8"))
                for q in range(3):
                    ts(kkn[:, q, :], k_[:, q, :], col("k_k", q), None, ALU.mult, None, f"{L} kk")
                v.wait_ge(*dve.at(f"{L} rate 2"))
                ts(flat["a"], flat["a"], 0.5, 0.5, ALU.mult, ALU.add)
                v.wait_ge(*dve.at(f"{L} decay 2"))
                ts(flat["lw"], flat["lw"], 0.5 * NEG_HALF_EXP, 0.5 * NEG_HALF_EXP, ALU.mult, ALU.add)
                for q in range(3):
                    v.wait_ge(*dve.last())
                    ve.tensor_tensor_scan(c[:, q, :], C("scan"), lw[:, q, :], 0.0, ALU.mult, ALU.add).then_inc(*dve.step())
                c4 = V("c", 3, NT, P)
                mid = c4[:, :, :, 63:64]
                v.wait_ge(*dve.last())
                ve.tensor_copy(sm("cmid").rearrange("p (a b c) -> p a b c", a=3, b=2), mid).then_inc(*dve.step())
                cm = sm("cmid").rearrange("p (a b) -> p a b", a=3)
                tt(sm("dec"), c4[:, :, 0, 127], cm[:, :, 0], ALU.subtract)
                tt(sm("dec"), sm("dec"), cm[:, :, 1], ALU.add, f"{L} dec sum")
                tt(V("c", 6, P), V("c", 6, P), bc(sm("cmid"), P), ALU.subtract, f"{L} c centred")
                tt(flat["lw"], flat["c"], flat["lw"], ALU.subtract)
                for q in range(3):
                    ts(bh[:, q, :], a_[:, q, :], 1.0, col("k_a", q), ALU.subtract, ALU.mult)
                stt(k_, bh, 1.0, k_, ALU.add, ALU.mult)
                v.wait_ge(*dve.at(f"{L} glu"))
                ts(w2, w2, 0.5, 0.5, ALU.mult, ALU.add)
                tt(y, y, w2, ALU.mult, f"{L} s5 y")
                v.wait_ge(*dve.at(f"{L} kk sum"))
                ts(flat["e2"], ps[:, 0:2, :].rearrange("p a b -> p (a b)")[:, 0:768], 1e-24, None, ALU.max, None,
                   f"{L} kk sum out")
                v.wait_ge(*dve.at(f"{L} s5 sum"))
                ts(var, ps[:, 3, 0:S], 1.0 / S, EPS, ALU.mult, ALU.add, f"{L} s5 var")
                v.wait_ge(*dve.at(f"{L} kk root"))
                v.wait_ge(*dve.last())
                ve.reciprocal(flat["e2"], flat["e2"]).then_inc(*dve.step())
                tt(flat["kkn"], flat["kkn"], flat["e2"], ALU.mult)
                v.wait_ge(*dve.at(f"{L} s5 root"))
                v.wait_ge(*dve.last())
                ve.reciprocal(var, var).then_inc(*dve.step())
                for m in range(2):
                    stt(hT[:, 3 + m, :], V("z0", 2, S)[:, m, :], col("s5_norm", m), var, ALU.mult, ALU.mult,
                        f"{L} mixed s5")
                v.wait_ge(*dve.at(f"{L} grown"))
                for q in range(3):
                    v.wait_ge(*dve.at(f"{L} shifted 2"))
                    tt(AR[:, q, :, 1, :], r_[:, q, :].rearrange("p (n s) -> p n s", n=NT),
                       e1[:, q, :].rearrange("p (n s) -> p n s", n=NT), ALU.mult, f"{L} r~")
                v.wait_ge(*dve.at(f"{L} grown before"))
                for q in range(3):
                    stt(AR[:, q, :, 0, :], kkn[:, q, :].rearrange("p (n s) -> p n s", n=NT), -1.0,
                        e1[:, q, :].rearrange("p (n s) -> p n s", n=NT), ALU.mult, ALU.mult, f"{L} AR")
                for q in range(3):
                    stt(e1[:, q, :], r_[:, q, :], col("r_k", q), k_[:, q, :], ALU.mult, ALU.mult, f"{L} rk")
                tt(flat["bh"], flat["kkn"], flat["a"], ALU.mult, f"{L} b k")
                v.wait_ge(*dve.at(f"{L} shrunk"))
                tt(flat["bh"], flat["bh"], flat["e2"], ALU.mult, f"{L} bh")
                tt(kh, k_, e2, ALU.mult, f"{L} kh")
                v.wait_ge(*dve.at(f"{L} rk sum"))
                v.wait_ge(*dve.at(f"{L} shifted 8"))
                tt(V("bonus"), ps[:, 2:4, :].rearrange("p a b -> p (a b)")[:, 0:768],
                   pm[:, 6:9, :].rearrange("p a b -> p (a b)"), ALU.mult, f"{L} bonus")
                for b in range(3):
                    for n in range(NT):
                        v.wait_ge(*dve.at(f"{L} natural psum {b} {n}"))
                for i in range(12):
                    v.wait_ge(*dve.at(f"{L} mat psum {i}"))
                    tt(MAT[:, i].rearrange("p (a b) c -> p a (b c)", a=2),
                       ps[:, i % 4, :].rearrange("p (a b) -> p a b", a=2),
                       C("masks").unsqueeze(1).to_broadcast([P, 2, 2 * P]), ALU.mult, f"{L} mat {i}")
                for n in range(NT):
                    a_t = MAT[:, n * 6:n * 6 + 6, 0, :]
                    tt(Am[:, n], a_t, C("level")[:, 0:P].unsqueeze(1).to_broadcast([P, 6, P]), ALU.mult,
                       f"{L} Am 0 {n}")
                    tt(TT[:, n], Am[:, n], ident.unsqueeze(1).to_broadcast([P, 6, P]), ALU.add)
                for n in range(NT):
                    v.wait_ge(*dve.at(f"{L} Pm 0 {n}"))
                    tt(T[:, n], Pm[:, n], ident.unsqueeze(1).to_broadcast([P, 6, P]), ALU.add, f"{L} T 0 {n}")
                for lv in range(1, LEVELS):
                    for n in range(NT):
                        if lv < LEVELS - 1:
                            v.wait_ge(*dve.at(f"{L} T psum {lv} {n}"))
                            v.wait_ge(*dve.at(f"{L} Pm psum {lv} {n}"))
                            part = halves(T[:, n], lv, 0)
                            tt(part, part, halves(six_of(4 * n + 2), lv, 0), ALU.add, f"{L} T {lv} {n}")
                        v.wait_ge(*dve.at(f"{L} TT psum {lv} {n}"))
                        part = halves(TT[:, n], lv, 1)
                        tt(part, part, halves(six_of(4 * n), lv, 1), ALU.add, f"{L} TT {lv} {n}")
                v.wait_ge(*dve.at(f"{L} state psum"))
                for q in range(3):
                    stt(V("st", 3, P)[:, q, :], ps[:, 7, q * P:(q + 1) * P], sm("dec", q), ones_head, ALU.mult,
                        ALU.mult, f"{L} state")
                OT, o1, o2 = V("OT"), V("o1"), V("o2")
                v.wait_ge(*dve.at(f"{L} mean psum"))
                v.wait_ge(*dve.at(f"{L} OT 1"))
                stt(o1, ps[:, 2:4, :].rearrange("p a b -> p (a b)")[:, 0:768], -1.0 / 64, OT, ALU.mult, ALU.add,
                    f"{L} centred")
                v.wait_ge(*dve.at(f"{L} var psum"))
                ts(o2, ps[:, 6:8, :].rearrange("p a b -> p (a b)")[:, 0:768], 1.0 / 64, GN_EPS, ALU.mult, ALU.add,
                   f"{L} gn var")
                v.wait_ge(*dve.at(f"{L} gn root"))
                v.wait_ge(*dve.last())
                ve.reciprocal(o2, o2).then_inc(*dve.step())
                tt(o1, o1, o2, ALU.mult)
                for q in range(3):
                    oq = V("o1", 3, S)[:, q, :]
                    ts(oq, oq, col("ln_w", q), col("ln_b", q), ALU.mult, ALU.add)
                tt(o1, o1, V("bonus"), ALU.add)
                v.wait_ge(*dve.at(f"{L} g"))
                tt(hT[:, 0:3, :].rearrange("p a b -> p (a b)"), o1, V("g"), ALU.mult, f"{L} mixed rwkv")
                steps.at[f"{L} mixing over"] = ("dve", dve.count, dve.part)
                steps.at[f"{L} mix used params"] = ("dve", dve.count, dve.part)
                for k in range(AHEAD - 1):
                    low(("ffn", "moe")[L], ("ffn", "first")[L], k)
                v.wait_ge(gain_loaded, 16 + 32 * L)
                tmp = V("natural")[:, 0:D]
                for n in range(NT):
                    rstd(L, f"{L} post ss mean {n}", [f"{L} post square {n}"], f"{L} post root {n}", D, n)
                    stt(tmp, ps[:, 4 * n:4 * n + 2, :].rearrange("p a b -> p (a b)"), sm("rstd", n), V("mix_gain"),
                        ALU.mult, ALU.mult, f"{L} post read {n}")
                    if n == NT - 1:
                        steps.at[f"{L} mix post gained"] = ("dve", dve.count, dve.part)
                    tt(x[:, n, :], x[:, n, :], tmp, ALU.add, f"{L} x ready ffn {n}")
                    normed(L, "ffn", n)
                low(("ffn", "moe")[L], ("ffn", "first")[L], AHEAD - 1)
                if L == 0:
                    for c in range(KD):
                        v.wait_ge(*dve.at(f"0 ffn hT {c}"))
                        stt(hTr[:, 1, c, :], ps[:, c, 0:S], col("ffn_pre", c), hTr[:, 0, c, :], ALU.mult, ALU.subtract,
                            f"0 ffn hT low {c}")
                    ffn("ffn", NT, lambda k: None)
                else:
                    hidden(1, "ffn")
                    route()
                    experts()
                v.wait_ge(gain_loaded, 32 + 32 * L)
                tmp = V("natural")[:, 0:D]
                for n in range(NT):
                    if L:
                        summed("last", [2 * n, 2 * n + 1])
                        steps.at[f"1 f ready {n}"] = ("dve", dve.count, "after")
                    rstd(L, f"{L} fpost ss mean {n}", [f"{L} fpost square {n}"], f"{L} fpost root {n}", D, n)
                    stt(tmp, ffn_out(L, n), sm("rstd", n), V("ffn_gain"), ALU.mult, ALU.mult, f"{L} fpost read {n}")
                    tt(x[:, n, :], x[:, n, :], tmp, ALU.add, f"{L + 1} x ready mix {n}")
                    if L < LAYERS - 1:
                        normed(L + 1, "mix", n)

        @block.gpsimd
        def _(g):
            pool = Engine("pool", sems, steps)

            def tt(out, a0, a1, op, step=None):
                g.wait_ge(*pool.last())
                nc.gpsimd.tensor_tensor(out, a0, a1, op).then_inc(*pool.step(step))

            for L in range(LAYERS):
                g.wait_ge(*pool.at(f"{L} c scaled"))
                g.wait_ge(*pool.last())
                nc.gpsimd.memset(E[:, 0, :, 0:1], 1.0).then_inc(*pool.step())
                g.wait_ge(*pool.last())
                nc.gpsimd.memset(E[:, 1, :, 0:1], 0.0).then_inc(*pool.step())
                g.wait_ge(*pool.last())
                nc.gpsimd.tensor_copy(E[:, 0, :, 1], sm("cs", 0, 8)).then_inc(*pool.step())
                g.wait_ge(*pool.last())
                nc.gpsimd.tensor_copy(E[:, 1, :, 1], sm("sn", 0, 8)).then_inc(*pool.step(f"{L} E"))
                m = 2
                w0, w1 = V("natural")[:, 0:1016].rearrange("p (a b) -> p a b", a=8), \
                    V("natural")[:, 1024:2040].rearrange("p (a b) -> p a b", a=8)
                while m < S:
                    for first in (True, False):
                        a0, b0 = (slice(m - 1, m), 1) if first else (slice(1, m), m)
                        out = slice(m, m + 1) if first else slice(m + 1, 2 * m)
                        n = out.stop - out.start
                        br, bi = (E[:, q, :, b0:b0 + 1].to_broadcast([P, 8, n]) for q in range(2))
                        ar, ai = E[:, 0, :, a0], E[:, 1, :, a0]
                        o0, o1 = w0[:, :, 0:n], w1[:, :, 0:n]
                        tt(o0, ar, br, ALU.mult)
                        tt(o1, ai, bi, ALU.mult)
                        tt(E[:, 0, :, out], o0, o1, ALU.subtract)
                        tt(o0, ar, bi, ALU.mult)
                        tt(o1, ai, br, ALU.mult)
                        tt(E[:, 1, :, out], o0, o1, ALU.add, f"{L} E")
                    m *= 2
                for first in (0, 6):
                    for f in range(first, first + 3):
                        g.wait_ge(*pool.at(f"{L} proj {f}"))
                    three = slice(first, first + 3)
                    now, was, out = pT[:, three, 1:257], pT[:, three, 0:256], pm[:, three, :]
                    mu = bc(col("mu")[:, three], S)
                    tt(out, was, now, ALU.subtract)
                    tt(out, out, mu, ALU.mult)
                    tt(out, out, now, ALU.add, f"{L} shifted {first + 2}")
                for lv in range(1, LEVELS):
                    for n in range(NT):
                        g.wait_ge(*pool.at(f"{L} Pm psum {lv - 1} {n}"))
                        if lv == 1:
                            g.wait_ge(*pool.at(f"{L} T 0 {n}"))
                        level = C("level")[:, lv * P:(lv + 1) * P].unsqueeze(1).to_broadcast([P, 6, P])
                        tt(Am[:, n], MAT[:, n * 6:n * 6 + 6, 0, :], level, ALU.mult, f"{L} Am {lv} {n}")


def kernel(**inputs):
    import concourse.bacc as _bacc
    from concourse.bass_utils import run_bass_kernel_spmd as _run

    L = LAYERS
    i = {k: np.asarray(v) for k, v in inputs.items()}

    def tiles(a, n):
        return a.reshape(L, n, P).transpose(0, 2, 1)

    def groups(a):
        return a.reshape(L, 8, P).transpose(0, 2, 1)

    cols = np.concatenate([
        tiles(i["norm_mix_pre"], 8), tiles(i["norm_ffn_pre"], 8), tiles(i["rwkv_mu"], 11), tiles(i["rwkv_w0"], 3),
        tiles(i["rwkv_a0"], 3), tiles(i["rwkv_k_k"], 3), tiles(i["rwkv_k_a"], 3), tiles(i["rwkv_r_k"], 3),
        tiles(i["rwkv_ln_w"], 3), tiles(i["rwkv_ln_b"], 3), tiles(i["s5_d"], 2), tiles(i["s5_b_glu"], 2),
        tiles(i["s5_norm"], 2), tiles(i["attn_norm"], 3), groups(i["s5_a_re"]), groups(i["s5_a_im"]),
        groups(np.repeat(i["s5_log_step"][:, :, None], 64, axis=2))], axis=2)
    b_blk = np.zeros((L, 2, 4, 2, 16, 2, 2, 64), np.float32)
    c_blk = np.zeros((L, 2, 64, 2, 8, 2, 16), np.float32)
    for ri, (b, c) in enumerate([("s5_b_re", "s5_c_re"), ("s5_b_im", "s5_c_im")]):
        bb = i[b].reshape(L, 2, 4, 2, 64, 16)
        cc = i[c].reshape(L, 8, 2, 16, 64)
        for g in range(2):
            b_blk[:, :, :, g, :, ri, g, :] = bb[:, :, :, g].transpose(0, 1, 2, 4, 3)
            c_blk[:, g, :, ri, :, g, :] = cc[:, :, g].transpose(0, 3, 1, 2)
    b_blk = b_blk.transpose(0, 2, 3, 4, 1, 5, 6, 7).reshape(L, P, 512)
    c_blk = c_blk.reshape(L, P, 512)
    rel = np.clip(np.arange(P)[:, None] + P - np.arange(384)[None, :], -128, 128) + 128
    bias = i["attn_rel_bias"][:, :, rel][:, [0, 2, 4, 1, 3, 5]].transpose(0, 2, 1, 3).reshape(L, P, 2304)

    def ffn(gate, up, down):
        n = gate.shape[0]
        gu = np.stack([gate.reshape(n, KD, P, CHUNKS, FC), up.reshape(n, KD, P, CHUNKS, FC)], axis=4)
        gu = gu.transpose(0, 3, 2, 1, 4, 5).reshape(n, CHUNKS, P, KD * 512)
        dn = down.reshape(n, CHUNKS, 2, P, D).transpose(0, 1, 3, 2, 4).reshape(n, CHUNKS, P, 2 * D)
        chunks = np.concatenate([gu, dn], axis=3).reshape(n, CHUNKS, P, 3, UNIT).transpose(0, 1, 3, 2, 4)
        chunks = chunks.reshape(n, NUSES, P, UNIT)[:, [3 * c + third for c, third in USES]]
        return chunks.reshape(n * NUSES, P, UNIT)

    arrays = {
        "x": i["x"].reshape(S, D),
        "const": constants(),
        "cols": cols,
        "b_blk": b_blk,
        "c_blk": c_blk,
        "w_glu": i["s5_w_glu"].reshape(L, 2, P, S).transpose(0, 2, 1, 3).reshape(L, P, 512),
        "lora": np.concatenate([i["rwkv_w_up"], i["rwkv_a_up"]], axis=1),
        "g_up": i["rwkv_g_up"],
        "w_in": i["w_in"].reshape(L, KD, P, WT, P)[:, :, :, IN_ORDER].reshape(L, KD, P, WT // 2, 2, P).transpose(0, 3, 2, 4, 1, 5)
            .reshape(L, WT // 2, P, UNIT),
        "w_out": i["w_out"].reshape(L, KD // 2, 2, P, D).transpose(0, 1, 3, 2, 4).reshape(L, KD // 2, P, UNIT),
        "bias": bias,
        "mix_post": i["norm_mix_post"],
        "ffn_post": i["norm_ffn_post"],
        "router": i["moe_router"][0].reshape(KD, P, EXPERTS).transpose(1, 0, 2).reshape(P, KD * EXPERTS),
        "ffn": ffn(i["ffn_w_gate"], i["ffn_w_up"], i["ffn_w_down"]),
        "moe": ffn(i["moe_w_gate"][0], i["moe_w_up"][0], i["moe_w_down"][0]),
    }
    arrays = {k: np.ascontiguousarray(v) for k, v in arrays.items()}

    steps = Steps()
    for _ in range(2):
        nc = _bacc.Bacc("TRN2", target_bir_lowering=False, num_devices=1)
        io = {k: nc.dram_tensor(f"in_{k}", a.shape, mybir.dt.from_np(a.dtype), kind="ExternalInput").ap()
              for k, a in arrays.items()}
        io["out"] = nc.dram_tensor("out_0", (S, D), F32, kind="ExternalOutput").ap()
        build(nc, steps, io)
        steps.final = True
    r = _run(nc, [{f"in_{k}": a for k, a in arrays.items()}], core_ids=[0])
    return r.results[0]["out_0"].reshape(1, S, D)
```
